# Optimizing a Trainium2 kernel written in Bass

```python
import math
import jax
import jax.numpy as jnp
from jax import lax
import numpy as np
import jax, jax.numpy as jnp

D_MODEL = 1024
BATCH = 1
SEQ = 256
DEPTH = 2

HEAD_DIM = 64
MIX_WIDTH = D_MODEL
N_HEADS_A = (MIX_WIDTH // 2) // (2 * HEAD_DIM)
DV_A = 2 * HEAD_DIM
N_HEADS_B = (MIX_WIDTH // 2) // HEAD_DIM
DILATED_PATTERNS = ((128, 1), (512, 4), (2048, 16))
N_HEADS_C = (MIX_WIDTH // 2) // HEAD_DIM
MOBA_BLOCK = 256
MOBA_TOPK = 3
MOBA_Q_CHUNK = 16
N_HEADS_D = (MIX_WIDTH // 2) // HEAD_DIM
FORGET_BIAS_INIT = 4.0
Q_BLOCK = 128
NUM_BUCKETS = 32
MAX_DISTANCE = 128
N_BIAS_HEADS = max(N_HEADS_A + N_HEADS_B, N_HEADS_C)
D_FF = -(-8 * D_MODEL // (3 * 256)) * 256
LN_EPS = 1e-5
DEEPNORM_ALPHA = (2 * DEPTH) ** 0.25
DEEPNORM_BETA = (8 * DEPTH) ** -0.25
ATTN_SCALE = HEAD_DIM ** -0.5

AB_SIZES = [N_HEADS_A * 2 * HEAD_DIM, N_HEADS_A * 2 * HEAD_DIM, N_HEADS_A * DV_A,
            N_HEADS_B * HEAD_DIM, N_HEADS_B * HEAD_DIM, N_HEADS_B * HEAD_DIM]
CD_SIZES = [N_HEADS_C * HEAD_DIM] * 3 + [N_HEADS_D * HEAD_DIM] * 3 + [N_HEADS_D]
AB_SPLITS = [int(s) for s in np.cumsum(AB_SIZES)[:-1]]
CD_SPLITS = [int(s) for s in np.cumsum(CD_SIZES)[:-1]]
IN_AB = sum(AB_SIZES)
IN_CD = sum(CD_SIZES)


f32 = jnp.float32

def t5_bucket(dist):
    n = jnp.maximum(dist, 0)
    max_exact = NUM_BUCKETS // 2
    nf = jnp.maximum(n, 1).astype(f32)
    large = max_exact + (jnp.log(nf / max_exact) / math.log(MAX_DISTANCE / max_exact)
                         * (NUM_BUCKETS - max_exact)).astype(jnp.int32)
    large = jnp.minimum(large, NUM_BUCKETS - 1)
    return jnp.where(n < max_exact, n, large)

def t5_bias(table_cols, dist):
    return jnp.moveaxis(table_cols[t5_bucket(dist)], -1, 0).astype(f32)

def layer_norm(x, g, b):
    xf = x.astype(f32)
    mu = xf.mean(-1, keepdims=True)
    var = jnp.square(xf - mu).mean(-1, keepdims=True)
    return ((xf - mu) * lax.rsqrt(var + LN_EPS) * g + b).astype(x.dtype)

def causal_block_attention(q, k, v, map_w, bias_fn):
    B, H, M, T, _ = q.shape
    k_pos = jnp.arange(T)

    def block(q0):
        qb = lax.dynamic_slice_in_dim(q, q0, Q_BLOCK, axis=3)
        q_pos = q0 + jnp.arange(Q_BLOCK)
        s = jnp.einsum('bhmqd,bhmkd->bhmqk', qb, k).astype(f32) + bias_fn(q_pos)
        s = jnp.where(k_pos[None, :] <= q_pos[:, None], s, -jnp.inf)
        p = jnp.einsum('bhmqk,m->bhqk', jax.nn.softmax(s, axis=-1), map_w)
        return jnp.einsum('bhqk,bhkd->bhqd', p.astype(v.dtype), v)

    out = lax.map(block, jnp.arange(T // Q_BLOCK) * Q_BLOCK)
    return jnp.moveaxis(out, 0, 2).reshape(B, H, T, v.shape[-1])

def dilated_attention(q, k, v, table_cols):
    B, H, T, dh = q.shape
    outs, lses = [], []
    for window, dil in DILATED_PATTERNS:
        W = window // dil
        L = T // dil
        nb = -(-L // W)
        pad = nb * W - L

        def strided(a):
            a = a.reshape(B, H, L, dil, a.shape[-1]).swapaxes(2, 3)
            return jnp.pad(a, ((0, 0), (0, 0), (0, 0), (0, pad), (0, 0)))

        def with_prev(a):
            ab = a.reshape(B, H, dil, nb, W, a.shape[-1])
            prev = jnp.pad(ab, ((0, 0), (0, 0), (0, 0), (1, 0), (0, 0), (0, 0)))[:, :, :, :-1]
            return jnp.concatenate([prev, ab], axis=4)

        qb = strided(q).reshape(B, H, dil, nb, W, dh)
        kb = with_prev(strided(k))
        vb = with_prev(strided(v))
        u_q = jnp.arange(nb)[:, None] * W + jnp.arange(W)[None, :]
        u_k = jnp.arange(nb)[:, None] * W + jnp.arange(-W, W)[None, :]
        du = u_q[:, :, None] - u_k[:, None, :]
        valid = (du >= 0) & (du <= W) & (u_k[:, None, :] >= 0)
        bias = t5_bias(table_cols, du * dil)
        s = jnp.einsum('bhrnqd,bhrnkd->bhrnqk', qb, kb).astype(f32) + bias[None, :, None]
        s = jnp.where(valid, s, -jnp.inf)
        m = s.max(-1, keepdims=True)
        p = jnp.exp(s - m)
        den = p.sum(-1)
        o = jnp.einsum('bhrnqk,bhrnkd->bhrnqd', p.astype(vb.dtype), vb) / den[..., None]
        o = o.reshape(B, H, dil, nb * W, dh)[:, :, :, :L].swapaxes(2, 3).reshape(B, H, T, dh)
        lse = (m[..., 0] + jnp.log(den)).reshape(B, H, dil, nb * W)[..., :L]
        outs.append(o)
        lses.append(lse.swapaxes(2, 3).reshape(B, H, T))
    w = jax.nn.softmax(jnp.stack(lses), axis=0)
    return jnp.sum(w[..., None] * jnp.stack(outs), axis=0).astype(q.dtype)

def moba_attention(q, k, v, table_cols):
    B, H, T, dh = q.shape
    n_blk = -(-T // MOBA_BLOCK)
    pad = n_blk * MOBA_BLOCK - T
    kp = jnp.pad(k, ((0, 0), (0, 0), (0, pad), (0, 0)))
    vp = jnp.pad(v, ((0, 0), (0, 0), (0, pad), (0, 0)))
    k_blk = kp.reshape(B, H, n_blk, MOBA_BLOCK, dh)
    v_blk = vp.reshape(B, H, n_blk, MOBA_BLOCK, dh)
    k_mean = k_blk.mean(axis=3)
    top = min(MOBA_TOPK, n_blk)
    b_idx = jnp.arange(B)[:, None, None, None]
    h_idx = jnp.arange(H)[None, :, None, None]
    bias_flat = table_cols.T.reshape(-1).astype(f32)
    in_blk = jnp.arange(MOBA_BLOCK)

    def chunk(q0):
        qc = lax.dynamic_slice_in_dim(q, q0, MOBA_Q_CHUNK, axis=2)
        q_pos = q0 + jnp.arange(MOBA_Q_CHUNK)
        own = q0 // MOBA_BLOCK
        gate = jnp.einsum('bhcd,bhnd->bhcn', qc, k_mean).astype(f32)
        gate = jnp.where(jnp.arange(n_blk) < own, gate, -jnp.inf)
        top_s, top_i = lax.top_k(gate, top)
        sel_ok = jnp.isfinite(top_s)
        k_sel = k_blk[b_idx, h_idx, top_i]
        v_sel = v_blk[b_idx, h_idx, top_i]
        sel_pos = top_i[..., None] * MOBA_BLOCK + in_blk
        sel_bucket = t5_bucket(q_pos[:, None, None] - sel_pos)
        s_sel = (jnp.einsum('bhcd,bhcnkd->bhcnk', qc, k_sel).astype(f32)
                 + bias_flat[h_idx[..., None] * NUM_BUCKETS + sel_bucket])
        s_sel = jnp.where(sel_ok[..., None], s_sel, -jnp.inf)
        own_start = own * MOBA_BLOCK
        k_own = lax.dynamic_slice_in_dim(kp, own_start, MOBA_BLOCK, axis=2)
        v_own = lax.dynamic_slice_in_dim(vp, own_start, MOBA_BLOCK, axis=2)
        own_dist = q_pos[:, None] - (own_start + in_blk)[None, :]
        s_own = (jnp.einsum('bhcd,bhkd->bhck', qc, k_own).astype(f32)
                 + t5_bias(table_cols, own_dist)[None])
        s_own = jnp.where(own_dist >= 0, s_own, -jnp.inf)
        s = jnp.concatenate([s_sel.reshape(B, H, MOBA_Q_CHUNK, top * MOBA_BLOCK), s_own], axis=-1)
        p = jax.nn.softmax(s, axis=-1).astype(v.dtype)
        p_sel = p[..., :top * MOBA_BLOCK].reshape(B, H, MOBA_Q_CHUNK, top, MOBA_BLOCK)
        p_own = p[..., top * MOBA_BLOCK:]
        return (jnp.einsum('bhcnk,bhcnkd->bhcd', p_sel, v_sel)
                + jnp.einsum('bhck,bhkd->bhcd', p_own, v_own))

    out = lax.map(chunk, jnp.arange(T // MOBA_Q_CHUNK) * MOBA_Q_CHUNK)
    return jnp.moveaxis(out, 0, 2).reshape(B, H, T, dh)

def split_heads(a, dh):
    B, T, _ = a.shape
    return a.reshape(B, T, -1, dh).transpose(0, 2, 1, 3)

def merge_heads(a):
    B, H, T, dh = a.shape
    return a.transpose(0, 2, 1, 3).reshape(B, T, H * dh)

def mixer_ab(h, w_in, w_o, lam, subln_g, table, lambda_init):
    B, T, _ = h.shape
    qa, ka, va, qb, kb, vb = jnp.split(h @ w_in, AB_SPLITS, axis=-1)
    qa = qa.reshape(B, T, N_HEADS_A, 2, HEAD_DIM).transpose(0, 2, 3, 1, 4) * ATTN_SCALE
    ka = ka.reshape(B, T, N_HEADS_A, 2, HEAD_DIM).transpose(0, 2, 3, 1, 4)
    va = split_heads(va, DV_A)
    lamf = lam.astype(f32)
    lam_full = (jnp.exp(jnp.sum(lamf[0] * lamf[1])) - jnp.exp(jnp.sum(lamf[2] * lamf[3]))
                + lambda_init)
    map_w = jnp.stack([jnp.ones((), f32), -lam_full])
    table_a = table[:, :N_HEADS_A]
    k_pos = jnp.arange(T)
    bias_a = lambda q_pos: t5_bias(table_a, q_pos[:, None] - k_pos[None, :])[None, :, None]
    oa = causal_block_attention(qa, ka, va, map_w, bias_a).astype(f32)
    oa = oa * lax.rsqrt(jnp.mean(jnp.square(oa), -1, keepdims=True) + LN_EPS)
    oa = (oa * subln_g * (1.0 - lambda_init)).astype(h.dtype)
    ob = dilated_attention(split_heads(qb, HEAD_DIM) * ATTN_SCALE, split_heads(kb, HEAD_DIM),
                           split_heads(vb, HEAD_DIM), table[:, N_HEADS_A:N_HEADS_A + N_HEADS_B])
    return jnp.concatenate([merge_heads(oa), merge_heads(ob)], axis=-1) @ w_o

def mixer_cd(h, w_in, w_o, forget_b, table):
    qc, kc, vc, qd, kd, vd, fd = jnp.split(h @ w_in, CD_SPLITS, axis=-1)
    oc = moba_attention(split_heads(qc, HEAD_DIM) * ATTN_SCALE, split_heads(kc, HEAD_DIM),
                        split_heads(vc, HEAD_DIM), table[:, :N_HEADS_C])
    log_f = jax.nn.log_sigmoid((fd + forget_b).astype(f32)).transpose(0, 2, 1)
    cum = jnp.cumsum(log_f, axis=-1)
    fox_bias = lambda q_pos: (cum[:, :, q_pos, None] - cum[:, :, None, :])[:, :, None]
    od = causal_block_attention((split_heads(qd, HEAD_DIM) * ATTN_SCALE)[:, :, None],
                                split_heads(kd, HEAD_DIM)[:, :, None],
                                split_heads(vd, HEAD_DIM), jnp.ones((1,), f32), fox_bias)
    return jnp.concatenate([merge_heads(oc), merge_heads(od)], axis=-1) @ w_o

def swiglu(h, w_in, w_out):
    g, u = jnp.split(h @ w_in, 2, axis=-1)
    return (jax.nn.silu(g) * u) @ w_out

def first_inputs(seed: int = 0) -> dict:
    key = jax.random.key(seed)
    ks = jax.random.split(key, 15)
    n_even = (DEPTH + 1) // 2
    n_odd = DEPTH // 2
    nrm = lambda k, shape, std: jax.random.normal(k, shape, f32) * std
    return {
        "x": nrm(ks[0], (BATCH, SEQ, D_MODEL), 1.0),
        "c": nrm(ks[1], (BATCH, D_MODEL), 1.0),
        "rel_bias": nrm(ks[2], (NUM_BUCKETS, N_BIAS_HEADS), 0.5),
        "w_ada": nrm(ks[3], (DEPTH, D_MODEL, 6 * D_MODEL), 0.1 * D_MODEL ** -0.5),
        "b_ada": nrm(ks[4], (DEPTH, 6 * D_MODEL), 0.01),
        "ln_g": 1.0 + nrm(ks[5], (DEPTH, 2, D_MODEL), 0.01),
        "ln_b": nrm(ks[6], (DEPTH, 2, D_MODEL), 0.01),
        "w_in_ab": nrm(ks[7], (n_even, D_MODEL, IN_AB), D_MODEL ** -0.5),
        "diff_lambda": nrm(ks[8], (n_even, 4, HEAD_DIM), 0.1),
        "diff_subln_g": 1.0 + nrm(ks[9], (n_even, DV_A), 0.01),
        "w_in_cd": nrm(ks[10], (n_odd, D_MODEL, IN_CD), D_MODEL ** -0.5),
        "forget_b": FORGET_BIAS_INIT + nrm(ks[11], (n_odd, N_HEADS_D), 0.5),
        "w_o": nrm(ks[12], (DEPTH, MIX_WIDTH, D_MODEL), DEEPNORM_BETA * MIX_WIDTH ** -0.5),
        "w_ffn_in": nrm(ks[13], (DEPTH, D_MODEL, 2 * D_FF), D_MODEL ** -0.5),
        "w_ffn_out": nrm(ks[14], (DEPTH, D_FF, D_MODEL), DEEPNORM_BETA * D_FF ** -0.5),
    }

def first_block(x, c, rel_bias, w_ada, b_ada, ln_g, ln_b, w_in_ab, diff_lambda, diff_subln_g,
              w_in_cd, forget_b, w_o, w_ffn_in, w_ffn_out):
    for l in range(DEPTH):
        ada = jax.nn.silu(c) @ w_ada[l] + b_ada[l]
        sh1, sc1, g1, sh2, sc2, g2 = [a[:, None, :] for a in jnp.split(ada, 6, axis=-1)]
        h = x * (1.0 + sc1) + sh1
        if l % 2 == 0:
            i = l // 2
            lambda_init = 0.8 - 0.6 * math.exp(-0.3 * l)
            y = mixer_ab(h, w_in_ab[i], w_o[l], diff_lambda[i], diff_subln_g[i], rel_bias,
                         lambda_init)
        else:
            i = l // 2
            y = mixer_cd(h, w_in_cd[i], w_o[l], forget_b[i], rel_bias)
        x = layer_norm(DEEPNORM_ALPHA * x + (1.0 + g1) * y, ln_g[l, 0], ln_b[l, 0])
        h = x * (1.0 + sc2) + sh2
        y = swiglu(h, w_ffn_in[l], w_ffn_out[l])
        x = layer_norm(DEEPNORM_ALPHA * x + (1.0 + g2) * y, ln_g[l, 1], ln_b[l, 1])
    return x


DEPTH_2 = 1

CHUNK = 64
PLE_DIM = 256
D_MIX = D_MODEL
D_CONV = D_MIX // 2
D_LRU = D_MIX - D_CONV
CONV_HEADS = 8
LRU_HEADS = 8
LRU_HEAD_DIM = D_LRU // LRU_HEADS
CONV_WIDTH = 31
LRU_CONV_WIDTH = 4
LRU_C = 8.0
N_GROUPS = 4
EXPERTS_PER_GROUP = 8
N_EXPERTS = N_GROUPS * EXPERTS_PER_GROUP
TOP_K = 2
D_EXPERT = D_MODEL // 2
ROUTE_BLOCK = 128
EPS = 1e-6


def _rmsnorm(x, g):
    xf = x.astype(jnp.float32)
    y = xf * lax.rsqrt(jnp.mean(xf * xf, axis=-1, keepdims=True) + EPS)
    return (y * g.astype(jnp.float32)).astype(x.dtype)

def _layernorm(x, g, b):
    xf = x.astype(jnp.float32)
    mu = jnp.mean(xf, axis=-1, keepdims=True)
    var = jnp.mean(jnp.square(xf - mu), axis=-1, keepdims=True)
    y = (xf - mu) * lax.rsqrt(var + EPS)
    return (y * g.astype(jnp.float32) + b.astype(jnp.float32)).astype(x.dtype)

def _causal_depthwise_conv(x, w, b):
    width = w.shape[0]
    y = lax.conv_general_dilated(
        x, w[:, None, :], window_strides=(1,), padding=((width - 1, 0),),
        dimension_numbers=('NWC', 'WIO', 'NWC'), feature_group_count=x.shape[-1])
    return y + b

def _conformer_conv(v, g, w_dw, b_dw, ln_g, ln_b):
    u = v * jax.nn.sigmoid(g)
    u = _causal_depthwise_conv(u, w_dw, b_dw)
    return jax.nn.silu(_layernorm(u, ln_g, ln_b))

def _rglru(x, w_r, b_r, w_i, b_i, lam):
    B, S, C = x.shape
    xh = x.reshape(B, S, LRU_HEADS, LRU_HEAD_DIM)
    r = jax.nn.sigmoid(jnp.einsum('bshi,hij->bshj', xh, w_r).reshape(B, S, C) + b_r)
    i_g = jax.nn.sigmoid(jnp.einsum('bshi,hij->bshj', xh, w_i).reshape(B, S, C) + b_i)
    log_a = -LRU_C * r.astype(jnp.float32) * jax.nn.softplus(-lam.astype(jnp.float32))
    a = jnp.exp(log_a)
    u = jnp.sqrt(-jnp.expm1(2.0 * log_a)) * (i_g * x).astype(jnp.float32)
    nc = S // CHUNK
    a_c = a.reshape(B, nc, CHUNK, C)
    u_c = u.reshape(B, nc, CHUNK, C)

    def combine(left, right):
        a_l, h_l = left
        a_r, h_r = right
        return a_l * a_r, a_r * h_l + h_r

    a_cum, h_loc = lax.associative_scan(combine, (a_c, u_c), axis=2)

    def step(h_prev, xs):
        ac, hl = xs
        h = hl + ac * h_prev[:, None, :]
        return h[:, -1, :], h

    _, h = lax.scan(step, jnp.zeros((B, C), jnp.float32),
                    (jnp.moveaxis(a_cum, 1, 0), jnp.moveaxis(h_loc, 1, 0)))
    return jnp.moveaxis(h, 0, 1).reshape(B, S, C).astype(x.dtype)

def _hier_route(h, w_group, b_group, w_expert, b_expert):
    T = h.shape[0]
    g_logits = (h @ w_group).astype(jnp.float32) + b_group.astype(jnp.float32)
    g_prob, g_idx = lax.top_k(jax.nn.softmax(g_logits, axis=-1), 1)
    e_logits = ((h @ w_expert).astype(jnp.float32) + b_expert.astype(jnp.float32))
    e_logits = e_logits.reshape(T, N_GROUPS, EXPERTS_PER_GROUP)
    e_sel = jnp.take_along_axis(e_logits, g_idx[:, :, None], axis=1)[:, 0]
    e_prob, e_loc = lax.top_k(jax.nn.softmax(e_sel, axis=-1), TOP_K)
    e_prob = e_prob / jnp.sum(e_prob, axis=-1, keepdims=True)
    gate = g_prob * e_prob
    expert_id = g_idx * EXPERTS_PER_GROUP + e_loc
    return expert_id, gate

def _routed_experts(h, expert_id, gate, w1, w3, w2):
    T, D = h.shape
    A = T * TOP_K
    flat_e = expert_id.reshape(A)
    flat_tok = jnp.repeat(jnp.arange(T, dtype=jnp.int32), TOP_K, total_repeat_length=A)
    flat_gate = gate.reshape(A)
    order = jnp.argsort(flat_e)
    se, st, sg = flat_e[order], flat_tok[order], flat_gate[order]
    counts = jnp.zeros((N_EXPERTS,), jnp.int32).at[flat_e].add(1)
    padded = (counts + ROUTE_BLOCK - 1) // ROUTE_BLOCK * ROUTE_BLOCK
    start = jnp.cumsum(counts) - counts
    pad_end = jnp.cumsum(padded)
    pad_start = pad_end - padded
    dest = pad_start[se] + (jnp.arange(A, dtype=jnp.int32) - start[se])
    n_blocks = -(-A // ROUTE_BLOCK) + N_EXPERTS
    P = n_blocks * ROUTE_BLOCK
    buf_tok = jnp.zeros((P,), jnp.int32).at[dest].set(st)
    buf_gate = jnp.zeros((P,), jnp.float32).at[dest].set(sg)
    block_start = jnp.arange(n_blocks, dtype=jnp.int32) * ROUTE_BLOCK
    block_e = jnp.minimum(jnp.searchsorted(pad_end, block_start, side='right'), N_EXPERTS - 1)

    def expert_block(args):
        tok, e, g = args
        xb = h[tok]
        y = (jax.nn.silu(xb @ w1[e]) * (xb @ w3[e])) @ w2[e]
        return (y * g[:, None]).astype(h.dtype)

    y = lax.map(expert_block, (buf_tok.reshape(n_blocks, ROUTE_BLOCK), block_e,
                               buf_gate.reshape(n_blocks, ROUTE_BLOCK)))
    return jnp.zeros_like(h).at[buf_tok].add(y.reshape(P, D))

def second_inputs(seed: int = 0) -> dict:
    key = jax.random.key(seed)
    ks = jax.random.split(key, 32)
    f32 = jnp.float32
    L = DEPTH_2

    def nrm(k, shape, scale):
        return jax.random.normal(k, shape, f32) * scale

    def gain(k, shape):
        return 1.0 + 0.05 * jax.random.normal(k, shape, f32)

    u = jax.random.uniform(ks[14], (L, D_LRU), f32, 0.9, 0.999)
    s = u ** (1.0 / LRU_C)
    lru_lambda = jnp.log(s) - jnp.log1p(-s)
    return {
        'x': nrm(ks[0], (BATCH, SEQ, D_MODEL), 1.0),
        'p': nrm(ks[1], (L, BATCH, SEQ, PLE_DIM), 1.0),
        'g_mix': gain(ks[2], (L, D_MODEL)),
        'w_in': nrm(ks[3], (L, D_MODEL, 2 * D_CONV + 2 * D_LRU), D_MODEL ** -0.5),
        'conv_dw_w': nrm(ks[4], (L, CONV_WIDTH, D_CONV), CONV_WIDTH ** -0.5),
        'conv_dw_b': nrm(ks[5], (L, D_CONV), 0.02),
        'conv_ln_g': gain(ks[6], (L, D_CONV)),
        'conv_ln_b': nrm(ks[7], (L, D_CONV), 0.02),
        'lru_conv_w': nrm(ks[8], (L, LRU_CONV_WIDTH, D_LRU), LRU_CONV_WIDTH ** -0.5),
        'lru_conv_b': nrm(ks[9], (L, D_LRU), 0.02),
        'lru_w_r': nrm(ks[10], (L, LRU_HEADS, LRU_HEAD_DIM, LRU_HEAD_DIM), LRU_HEAD_DIM ** -0.5),
        'lru_b_r': nrm(ks[11], (L, D_LRU), 0.02),
        'lru_w_i': nrm(ks[12], (L, LRU_HEADS, LRU_HEAD_DIM, LRU_HEAD_DIM), LRU_HEAD_DIM ** -0.5),
        'lru_b_i': nrm(ks[13], (L, D_LRU), 0.02),
        'lru_lambda': lru_lambda,
        'w_out': nrm(ks[15], (L, D_MIX, D_MODEL), D_MIX ** -0.5),
        'g_ffn': gain(ks[16], (L, D_MODEL)),
        'w_group': nrm(ks[17], (L, D_MODEL, N_GROUPS), D_MODEL ** -0.5),
        'b_group': nrm(ks[18], (L, N_GROUPS), 0.01),
        'w_expert': nrm(ks[19], (L, D_MODEL, N_EXPERTS), D_MODEL ** -0.5),
        'b_expert': nrm(ks[20], (L, N_EXPERTS), 0.01),
        'w1': nrm(ks[21], (L, N_EXPERTS, D_MODEL, D_EXPERT), D_MODEL ** -0.5),
        'w3': nrm(ks[22], (L, N_EXPERTS, D_MODEL, D_EXPERT), D_MODEL ** -0.5),
        'w2': nrm(ks[23], (L, N_EXPERTS, D_EXPERT, D_MODEL), D_EXPERT ** -0.5),
        'g_ple': gain(ks[24], (L, D_MODEL)),
        'w_ple': nrm(ks[25], (L, PLE_DIM, D_MODEL), PLE_DIM ** -0.5),
        'g_ple_proj': gain(ks[26], (L, D_MODEL)),
        'w_ple_gate': nrm(ks[27], (L, D_MODEL, D_MODEL), D_MODEL ** -0.5),
        'g_final': gain(ks[28], (D_MODEL,)),
    }

def second_block(x, p, g_mix, w_in, conv_dw_w, conv_dw_b, conv_ln_g, conv_ln_b,
              lru_conv_w, lru_conv_b, lru_w_r, lru_b_r, lru_w_i, lru_b_i, lru_lambda,
              w_out, g_ffn, w_group, b_group, w_expert, b_expert, w1, w3, w2,
              g_ple, w_ple, g_ple_proj, w_ple_gate, g_final):
    B, S, D = x.shape
    for i in range(DEPTH_2):
        h = _rmsnorm(x, g_mix[i])
        z = h @ w_in[i]
        conv_v, conv_g, lru_x, lru_g = jnp.split(
            z, [D_CONV, 2 * D_CONV, 2 * D_CONV + D_LRU], axis=-1)
        y_conv = _conformer_conv(conv_v, conv_g, conv_dw_w[i], conv_dw_b[i],
                                 conv_ln_g[i], conv_ln_b[i])
        xr = _causal_depthwise_conv(lru_x, lru_conv_w[i], lru_conv_b[i])
        y_lru = _rglru(xr, lru_w_r[i], lru_b_r[i], lru_w_i[i], lru_b_i[i],
                       lru_lambda[i]) * jax.nn.gelu(lru_g)
        x = x + jnp.concatenate([y_conv, y_lru], axis=-1) @ w_out[i]
        hf = _rmsnorm(x, g_ffn[i]).reshape(B * S, D)
        eid, gate = _hier_route(hf, w_group[i], b_group[i], w_expert[i], b_expert[i])
        x = x + _routed_experts(hf, eid, gate, w1[i], w3[i], w2[i]).reshape(B, S, D)
        e = _rmsnorm(p[i] @ w_ple[i], g_ple_proj[i])
        pg = jax.nn.sigmoid(_rmsnorm(x, g_ple[i]) @ w_ple_gate[i])
        x = x + pg * e
    return _rmsnorm(x, g_final)


def setup_inputs(seed=0):
    out = dict(first_inputs(seed))
    for name, value in second_inputs(seed + 1).items():
        if name != "x":
            out[name + "_2"] = value
    return out


def reference(
    x, c, rel_bias, w_ada, b_ada, ln_g, ln_b, w_in_ab, diff_lambda, diff_subln_g, w_in_cd,
    forget_b, w_o, w_ffn_in, w_ffn_out, p_2, g_mix_2, w_in_2, conv_dw_w_2, conv_dw_b_2,
    conv_ln_g_2, conv_ln_b_2, lru_conv_w_2, lru_conv_b_2, lru_w_r_2, lru_b_r_2, lru_w_i_2,
    lru_b_i_2, lru_lambda_2, w_out_2, g_ffn_2, w_group_2, b_group_2, w_expert_2, b_expert_2,
    w1_2, w3_2, w2_2, g_ple_2, w_ple_2, g_ple_proj_2, w_ple_gate_2, g_final_2,
):
    x = first_block(
        x, c, rel_bias, w_ada, b_ada, ln_g, ln_b, w_in_ab, diff_lambda, diff_subln_g, w_in_cd,
        forget_b, w_o, w_ffn_in, w_ffn_out,
    )
    return second_block(
        x, p_2, g_mix_2, w_in_2, conv_dw_w_2, conv_dw_b_2, conv_ln_g_2, conv_ln_b_2,
        lru_conv_w_2, lru_conv_b_2, lru_w_r_2, lru_b_r_2, lru_w_i_2, lru_b_i_2, lru_lambda_2,
        w_out_2, g_ffn_2, w_group_2, b_group_2, w_expert_2, b_expert_2, w1_2, w3_2, w2_2,
        g_ple_2, w_ple_2, g_ple_proj_2, w_ple_gate_2, g_final_2,
    )


_drawn_inputs = setup_inputs


def setup_inputs(seed=0):
    import zlib

    import numpy as np

    out = dict(_drawn_inputs(seed))
    spreads = {}
    factors = {'diff_subln_g': 27.407,
     'conv_ln_b_2': 5.718,
     'lru_b_r_2': 8.0,
     'lru_b_i_2': 8.0,
     'b_group_2': 10.112,
     'b_expert_2': 13.875,
     'g_ple_2': 6.911,
     'conv_dw_b_2': 3.276}
    for name, (base, spread) in spreads.items():
        noise = np.random.default_rng([zlib.crc32(name.encode()), seed]).standard_normal(out[name].shape)
        drawn = base * np.exp(spread * noise) if base else spread * noise
        out[name] = jnp.asarray(drawn.astype(out[name].dtype))
    for name, factor in factors.items():
        out[name] = (out[name] * factor).astype(out[name].dtype)
    return out
```

```python
import math
from contextlib import ExitStack

import numpy as np

import concourse.bass as bass
from concourse import mybir
from concourse.alu_op_type import AluOpType as ALU

ACT = mybir.ActivationFunctionType
F32 = mybir.dt.float32
I32 = mybir.dt.int32
AX_X = mybir.AxisListType.X

P = 128
T = 256
TT = T // P
D = 1024
KT = D // P
DEPTH = 2
DH = 64
D_FF = 2816
FT = D_FF // P
ALPHA = (2 * DEPTH) ** 0.25
LN_EPS = 1e-5
RMS_EPS = 1e-6
LAMBDA_INIT = 0.8 - 0.6 * math.exp(0.0)
MASKED = 1e30
MAPS = 16
BUCKETS = 32
CONV_W, LRU_W = 31, 4
CT = 4
NE, NG, EPG = 32, 4, 8
FE = 512
CAP = 64
PAIRS = NE // 2

RING = 4
UNIT = 2048
ARING = 2

VECS = [("b_ada", 96), ("ln_g", 32), ("ln_b", 32), ("subln_g", 1), ("conv_w", CT * CONV_W),
        ("conv_b", 4), ("conv_ln_g", 4), ("conv_ln_b", 4), ("lru_w", CT * LRU_W), ("lru_b", 4),
        ("b_r", 4), ("b_i", 4), ("lam", 4), ("g_mix", 8), ("g_ffn", 8), ("g_ple", 8),
        ("g_ple_proj", 8), ("g_final", 8)]
VEC_AT = {}
_at = 0
for _name, _n in VECS:
    VEC_AT[_name] = _at
    _at += _n
N_VEC = _at

RC_TRI, RC_SLOT, RC_W4, RC_W32, N_RC = 0, 128, 192, 196, 228

STAGES = [("v0", 4), ("qk0", 8), ("wo0", 4), ("fi0", 22), ("fo0", 11),
          ("v1", 4), ("qk1", 8), ("wo1", 4), ("fi1", 22), ("fo1", 11),
          ("z", 8), ("ple", 1), ("wout", 4), ("pg", 4)]
UNIT_AT = {}
_at = 0
for _name, _n in STAGES:
    UNIT_AT[_name] = _at
    _at += _n
N_UNITS = _at
BANK_AT = {"v0": 0, "qk0": 4, "fi0": 12, "v1": 34, "qk1": 38, "fi1": 46, "z": 68}

NORMS = [("heads", 4), ("ln0", 8), ("ln1", 8), ("ln2", 8), ("ln3", 8), ("mix", 8), ("ple_proj", 8),
         ("conv", 4), ("ffn", 8), ("gate", 8), ("final", 8)]
SQ_AT = {}
_at = 0
for _name, _n in NORMS:
    SQ_AT[_name] = _at
    _at += _n
NORM_NO = {name: i for i, (name, _) in enumerate(NORMS)}

CONSTS = 13 * 16
ADA_PIECES = 48


def shape_constants():
    ident = np.eye(P, dtype=np.float32)
    consts = np.concatenate([ident, np.ones((P, P), np.float32)], axis=1)
    n = 255 - np.arange(384)
    past = np.maximum(n, 0)
    large = 16 + (np.log(np.maximum(past, 1).astype(np.float32) / 16) / np.float32(math.log(128 / 16)) * 16).astype(np.int32)
    bucket = np.where(past < 16, past, np.minimum(large, BUCKETS - 1))
    hot = ((bucket[None, :] == np.arange(BUCKETS)[:, None]) & (n >= 0)[None, :]).astype(np.float32)
    times = (n <= 128).astype(np.float32) + (n % 4 == 0) + (n % 16 == 0)
    plain = np.where(n >= 0, 0.0, MASKED).astype(np.float32)
    dilated = np.where((n >= 0) & (times > 0), -np.log(np.maximum(times, 1)), MASKED).astype(np.float32)
    added = np.concatenate([np.tile(plain, (8, 1)), np.tile(dilated, (8, 1))]).astype(np.float32)
    q, k = np.arange(P)[:, None], np.arange(P)[None, :]
    causal = np.concatenate([np.zeros((P, P)), np.where(k <= q, 0.0, MASKED)], axis=1).astype(np.float32)
    router = np.zeros((P, N_RC), np.float32)
    router[:, RC_TRI:RC_TRI + P] = (q < k)
    router[:, RC_SLOT:RC_SLOT + CAP] = np.arange(CAP)
    router[:, RC_W4:RC_W4 + NG] = 8 - np.arange(NG)
    router[:, RC_W32:RC_W32 + NE] = 64 - np.arange(NE)
    rows = np.zeros((4, 32, 8), np.float32)
    rows[:, np.arange(8), np.arange(8)] = 1
    rows = rows.reshape(P, 8)
    return {"consts": consts, "hot": hot, "added": added, "causal": causal, "router_consts": router,
            "head_rows": rows, "flip": np.ascontiguousarray(ident[::-1])}


def build(nc, a, out):
    ctx = ExitStack()
    with ctx:
        def sb(name, shape, dt=F32):
            return ctx.enter_context(nc.sbuf_tensor(name, shape, dt))

        def sem(name):
            return ctx.enter_context(nc.semaphore(name))

        wring = sb("wring", [P, RING, UNIT])
        aring = sb("aring", [P, ARING, UNIT])
        w13 = sb("w13", [P, 4, 4096])
        arena = sb("arena", [P, 8192])
        arena2 = sb("arena2", [P, 6656])
        x = sb("x", [P, KT, T])
        h = sb("h", [P, KT, T])
        d = sb("d", [P, KT, T])
        sq = sb("sq", [P, 2, T])
        rstd = sb("rstd", [P, T])
        vec = sb("vec", [P, N_VEC])
        cb = sb("cb", [P, D])
        lam_in = sb("lam_in", [P, 256])
        cst = sb("cst", [P, 2 * P])
        w_route = sb("w_route", [P, KT, 36])
        w_forget = sb("w_forget", [P, KT, 8])
        ada = sb("ada", [P, DEPTH, 48])
        ada_raw = sb("ada_raw", [P, 4])
        drv = sb("drv", [P, 4, 5, 8])
        mins = sb("mins", [P, MAPS, 2])
        den = sb("den", [P, MAPS, 2])
        small = sb("small", [P, 64])
        fsmall = sb("fsmall", [P, 16])

        ident = cst[:, 0:P]
        ones = cst[:, P:2 * P]
        h_tile = lambda kt: h[:, kt, :]
        qk = arena[:, 0:4096].rearrange("p (n t) -> p n t", t=T)
        val = arena[:, 4096:6144].rearrange("p (a n) -> p a n", a=TT)
        o = arena[:, 6144:8192].rearrange("p (n t) -> p n t", t=T)
        bias = arena2[:, 0:17 * 256].rearrange("p (n t) -> p n t", t=256)
        score = arena2[:, 4352:4352 + 4 * 384].rearrange("p (n t) -> p n t", t=384)
        prob_t = arena2[:, 5888:5888 + 2 * 384].rearrange("p (n t) -> p n t", t=384)
        act = arena[:, 0:FT * T].rearrange("p (n t) -> p n t", t=T)
        gate_s = arena[:, FT * T:(FT + 2) * T].rearrange("p (n t) -> p n t", t=T)
        f_u, f_v = d[:, 0, :], d[:, 1, :]
        f_vh = [d[:, 2, :], d[:, 3, :]]
        f_x, f_e, f_z, f_w = (d[:, i, :] for i in (4, 5, 6, 7))
        PU, PL = CONV_W - 1, LRU_W - 1
        u_pad = arena2[:, 0:CT * (PU + T)].rearrange("p (n t) -> p n t", t=PU + T)
        l_pad = arena2[:, 1144:1144 + CT * (PL + T)].rearrange("p (n t) -> p n t", t=PL + T)
        lru_g = arena2[:, 2180:2180 + 1024].rearrange("p (n t) -> p n t", t=T)
        conv = arena2[:, 3204:3204 + 1024].rearrange("p (n t) -> p n t", t=T)
        lru_x = arena2[:, 4228:4228 + 1024].rearrange("p (n t) -> p n t", t=T)
        pt_in = arena2[:, 5252:5252 + 512].rearrange("p (n t) -> p n t", t=T)
        DIAGS = 8
        diag = arena[:, 7168:7168 + DIAGS * P].rearrange("p (n j) -> p n j", j=P)
        cat = arena[:, 0:2048].rearrange("p (n t) -> p n t", t=T)
        g_r, g_i, t_a, t_b, t_c = (arena[:, 2048 + 1024 * i:3072 + 1024 * i].rearrange(
            "p (n t) -> p n t", t=T) for i in range(5))
        blk_w = cb[:, :].rearrange("p (g n j) -> p g n j", g=2, n=CT)
        ple_e = aring[:, 0, :].rearrange("p (n t) -> p n t", t=T)
        E0 = 0
        xe_t = arena2[:, E0:E0 + 1024].rearrange("p (k c) -> p k c", k=KT)
        hot_s = arena2[:, 1024:1280].rearrange("p (a e c) -> p a e c", a=TT, e=2)
        hot_g = arena2[:, 1280:1536].rearrange("p (a e c) -> p a e c", a=TT, e=2)
        hot_gt = arena2[:, 1536:1792]
        silu1 = arena2[:, 1792:2304]
        act_e = arena2[:, 2304:2816]
        act_t = arena2[:, 2816:3328].rearrange("p (f c) -> p f c", f=4)
        y_e = arena2[:, 3328:4352]
        rc = arena2[:, 5764:5764 + N_RC]
        rt = arena2[:, 5992:6656]
        b_route = rt[:, 0:36]
        by_tile = lambda lo, n: rt[:, lo:lo + TT * n].rearrange("p (a e) -> p a e", a=TT)
        r_logit, r_hot_m, r_gate = by_tile(36, 36), by_tile(108, NE), by_tile(172, NE)
        r_rank = by_tile(236, NE + 2)
        r_first, r_work, r_el = by_tile(304, NE), by_tile(368, NE), by_tile(432, NE)
        r_ghot, r_gwork, r_pen = by_tile(496, NG), by_tile(504, NG), by_tile(512, NG)
        r_s = rt[:, 528:576].rearrange("p (n a) -> p n a", a=TT)
        d_flat = d[:].rearrange("p k t -> p (k t)")

        def hf_t(t, kt):
            return d_flat[:, t * D + kt * P:t * D + (kt + 1) * P]

        table_in, hot_in = d_flat[0:BUCKETS, 1024:1040], d_flat[0:BUCKETS, 0:384]
        flip_in = d_flat[:, 384:512]
        added_in, bias_rows = d_flat[0:16, 512:896], d_flat[0:16, 1536:1920]

        psum = ctx.enter_context(nc.psum_tensor("psum", [P, 8, 512], F32))

        def half(bank, i):
            return psum[:, bank, i * T:(i + 1) * T]

        def y_ps(n):
            return half(4 + n // 2, n % 2)

        consts_in = sem("consts_in")
        w_loaded = [sem(f"w_loaded{i}") for i in range(RING)]
        unit_done = sem("unit_done")
        bank_free = sem("bank_free")
        a_loaded = [sem(f"a_loaded{i}") for i in range(ARING)]
        ada_done = sem("ada_done")
        silu_c = sem("silu_c")
        dve_seq, act_seq, pool_seq = sem("dve_seq"), sem("act_seq"), sem("pool_seq")
        bias_mm, bias_row, bias_out, bias_in = sem("bias_mm"), sem("bias_row"), sem("bias_out"), sem("bias_in")
        flip_mm, flipped = sem("flip_mm"), sem("flipped")
        drv_ready = sem("drv_ready")
        h_ready = sem("h_ready")
        x_ready = sem("x_ready")
        score_mm, score_rd, exp_done = sem("score_mm"), sem("score_rd"), sem("exp_done")
        prob_ready, pt_mm, pt_copied, o_mm, o_copied = (sem(n) for n in (
            "prob_ready", "pt_mm", "pt_copied", "o_mm", "o_copied"))
        fd_mm, fd_in, fd_abs, fd_exp, fd_ready, fd_head = (sem(n) for n in (
            "fd_mm", "fd_in", "fd_abs", "fd_exp", "fd_ready", "fd_head"))
        head_std, o_ready = sem("head_std"), sem("o_ready")
        resid, centred, normed = sem("resid"), sem("centred"), sem("normed")
        sq_ready, sq_used = sem("sq_ready"), sem("sq_used")
        mean_mm = sem("mean_mm")
        std_ready = sem("std_ready")
        gate_done = sem("gate_done")
        z_in = sem("z_in")
        pad_zero = sem("pad_zero")
        blk_in, blk_zero = sem("blk_in"), sem("blk_zero")
        ple_in = sem("ple_in")
        conv_done, dve_taps = sem("conv_done"), sem("dve_taps")
        diag_ready, diag_used = sem("diag_ready"), sem("diag_used")
        ada_sum = sem("ada_sum")
        lam_sum, lam_exp, lru_abs = sem("lam_sum"), sem("lam_exp"), sem("lru_abs")
        conv_norm, cat_ready = sem("conv_norm"), sem("cat_ready")
        xr_ready, gates_mm, gates_act, lru_l, lru_t, lru_u, gelu_a, gelu_b = (sem(n) for n in (
            "xr_ready", "gates_mm", "gates_act", "lru_l", "lru_t", "lru_u", "gelu_a", "gelu_b"))
        e_copied = sem("e_copied")
        route_mm, route_d, route_exp, route_m, rank_mm, routed = (sem(n) for n in (
            "route_mm", "route_d", "route_exp", "route_m", "rank_mm", "routed"))
        rc_in = sem("rc_in")
        tok_mm, tok_copied = sem("tok_mm"), sem("tok_copied")
        w13_loaded = [sem("w1_loaded"), sem("w3_loaded")]
        w2_loaded = sem("w2_loaded")
        s_ready, sg_ready, gat0, gat1, gat0_c, gat1_c = (sem(n) for n in (
            "s_ready", "sg_ready", "gat0", "gat1", "gat0_c", "gat1_c"))
        up1, up3, silu_e, act_ready, actt_mm, actt_c = (sem(n) for n in (
            "up1", "up3", "silu_e", "act_ready", "actt_mm", "actt_c"))
        sgt_mm, sgt_c, y0_mm, y1_mm, y0_c, y1_c, scattered = (sem(n) for n in (
            "sgt_mm", "sgt_c", "y0_mm", "y1_mm", "y0_c", "y1_c", "scattered"))
        ple_scaled, next_round = sem("ple_scaled"), sem("next_round")
        out_ready, stored = sem("out_ready"), sem("stored")

        scratch = nc.dram_tensor("bias_rows", (16, 384), F32, kind="Internal").ap()
        rounds_i = sb("rounds_i", [P, 1], I32)

        def V(name, i=0, n=1):
            return vec[:, VEC_AT[name] + i:VEC_AT[name] + i + n]

        def each_unit(eng, n, first, body, peel=0):
            for j in range(peel):
                body(j, None, j)
            whole = (n - peel) // RING
            if whole >= 2:
                with eng.Fori(0, whole) as i:
                    for k in range(RING):
                        body(peel + k, i, peel + k + i * RING)
                at = peel + whole * RING
            else:
                at = peel
            for j in range(at, n):
                body(j, None, j)

        def turn(j, i, base, period):
            t = (base + j) // period
            return t if i is None else t + i * (RING // period)

        H_VERSION = {"v0": 1, "fi0": 2, "v1": 3, "fi1": 4, "z": 5, "route": 6, "pg": 7}
        ADA_H = 8

        def convolve(eng, nce, tiles, taps):
            for t in range(CONV_W):
                for k, j in enumerate(tiles):
                    if t:
                        eng.wait_ge(taps, 2 * (t - 1) + k + 1)
                        ins = nce.scalar_tensor_tensor(conv[:, j, :], u_pad[:, j, t:t + T],
                                                       V("conv_w", j * CONV_W + t), conv[:, j, :], ALU.mult, ALU.add)
                    else:
                        ins = nce.tensor_scalar(conv[:, j, :], u_pad[:, j, 0:T], V("conv_w", j * CONV_W),
                                                V("conv_b", j), ALU.mult, ALU.add)
                    ins.then_inc(conv_done if t == CONV_W - 1 else taps, 1)

        block = ctx.enter_context(nc.Block())

        @block.sync
        def _(sp):
            for dst, src in ((table_in, a["table"]), (hot_in, a["hot"]), (added_in, a["added"]),
                             (cst[:], a["consts"]), (flip_in, a["flip"]), (vec[:], a["vecs"]), (x[:], a["x_t"]),
                             (bias[:, 16, :], a["causal"]), (lam_in[:], a["lam_in"]), (w_forget[:], a["w_forget"]),
                             (w_route[:], a["w_route"]), (fsmall[0:8, 0:1], a["forget_b"]),
                             (fsmall[:, 1:9], a["head_rows"])):
                sp.dma_start(dst, src).then_inc(consts_in, 16)

            def load_unit(k):
                if k >= RING:
                    sp.wait_ge(unit_done, k - RING + 1)
                sp.dma_start(wring[:, k % RING, :], a["units"][k]).then_inc(w_loaded[k % RING], 16)

            def load_w13(e2, which):
                for s in range(2):
                    sp.dma_start(w13[:, 2 * which + s, :], a["w3" if which else "w1"][e2, s]).then_inc(
                        w13_loaded[which], 16)

            def load_w2(e2):
                for s in range(2):
                    sp.dma_start(arena[:, 4096 * s:4096 * (s + 1)], a["w2"][e2, s]).then_inc(w2_loaded, 16)

            for k in range(RING):
                load_unit(k)
            groups = (N_UNITS - RING) // RING
            with sp.Fori(0, groups) as i:
                for k in range(RING):
                    sp.wait_ge(unit_done, i * RING + (k + 1))
                    sp.dma_start(wring[:, k, :], a["units"][i * RING + (RING + k)]).then_inc(w_loaded[k], 16)
            for k in range(RING * (groups + 1), N_UNITS):
                load_unit(k)
            load_w13(0, 0)
            load_w13(0, 1)
            sp.wait_ge(unit_done, UNIT_AT["wout"] + 4)
            load_w2(0)

            def load_pair(e2, n):
                sp.wait_ge(up1, n)
                load_w13(e2, 0)
                sp.wait_ge(up3, n)
                load_w13(e2, 1)
                sp.wait_ge(y1_mm, n)
                load_w2(e2)

            with sp.Fori(1, PAIRS) as p:
                load_pair(p, p)
            sp.wait_ge(routed, 2)
            rounds = sp.value_load(rounds_i[0:1, 0:1], min_val=1, max_val=4)
            with sp.If(rounds > 1):
                with sp.Fori(1, rounds) as r:
                    with sp.Fori(0, PAIRS) as p:
                        load_pair(p, r * PAIRS + p)
            sp.wait_ge(out_ready, 8)
            sp.dma_start(out, d[:]).then_inc(stored, 16)
            sp.wait_ge(stored, 16)

        @block.gpsimd
        def _(pool):
            seq = [0]

            def link(ins):
                seq[0] += 1
                ins.then_inc(pool_seq, 1)
                pool.wait_ge(pool_seq, seq[0])

            def ada_piece(k):
                if k >= ARING:
                    pool.wait_ge(ada_done, k - ARING + 1)
                pool.dma_start(aring[:, k % ARING, :], a["ada"][k]).then_inc(a_loaded[k % ARING], 16)

            def pieces(lo, hi):
                for k in range(lo, hi):
                    ada_piece(k)

            pieces(0, 8)
            pool.wait_ge(h_ready, 8)
            nc.gpsimd.tensor_scalar(x[:], x[:], ALPHA, None, ALU.mult).then_inc(x_ready, 1)
            pieces(8, 24)

            def layer_norm_x(q):
                pool.wait_ge(drv_ready, q + 2)
                for kt in range(KT):
                    pool.wait_ge(normed, 8 * q + kt + 1)
                    nc.gpsimd.tensor_scalar(x[:, kt, :], d[:, kt, :], drv[:, q, 3, kt:kt + 1],
                                            drv[:, q, 4, kt:kt + 1], ALU.mult, ALU.add).then_inc(x_ready, 1)

            layer_norm_x(0)
            with pool.Fori(0, 10) as i:
                for s in range(ARING):
                    pool.wait_ge(ada_done, i * 2 + (24 + s - ARING + 1))
                    pool.dma_start(aring[:, s, :], a["ada"][i * 2 + (24 + s)]).then_inc(a_loaded[s], 16)
            pieces(44, 48)
            layer_norm_x(1)
            layer_norm_x(2)
            layer_norm_x(3)

            pool.wait_ge(ada_done, ADA_PIECES)
            link(nc.gpsimd.memset(cb[:], 0.0))
            for g, name in enumerate(("w_r", "w_i")):
                for s in range(2):
                    pool.dma_start(blk_w[64 * s:64 * s + 64, g, :, 64 * s:64 * s + 64],
                                   a[name][64 * s:64 * s + 64]).then_inc(blk_in, 16)
            pool.wait_ge(o_copied, 28)
            pool.dma_start(pt_in, a["p_t"]).then_inc(ple_in, 16)
            nc.gpsimd.memset(u_pad[:, :, 0:PU], 0.0).then_inc(pad_zero, 1)
            nc.gpsimd.memset(l_pad[:, :, 0:PL], 0.0).then_inc(pad_zero, 1)

            pool.wait_ge(z_in, 1)
            for n in range(2 * CONV_W):
                if n >= DIAGS:
                    pool.wait_ge(diag_used, n - DIAGS + 1)
                nc.gpsimd.tensor_scalar(diag[:, n % DIAGS, :], ident, V("conv_w", 2 * CONV_W + n), None,
                                        ALU.mult).then_inc(diag_ready, 1)
            pool.dma_start(rc, a["router_consts"]).then_inc(rc_in, 16)
            pool.dma_start(b_route, a["b_route"]).then_inc(rc_in, 16)

        @block.tensor
        def _(pe):
            def unit(base, j, i):
                slot = (base + j) % RING
                pe.wait_ge(w_loaded[slot], (turn(j, i, base, RING) + 1) * 16)
                return slot

            def bank(stage, j, i):
                n = BANK_AT[stage] + j
                if n >= 2:
                    pe.wait_ge(bank_free, n - 1 if i is None else i * RING + (n - 1))
                return n % 2

            def to_features(stage, n_units, h_needed, src=h, src_ready=None):
                base = UNIT_AT[stage]

                def body(j, i, idx):
                    slot, b = unit(base, j, i), bank(stage, j, i)
                    for s in range(2):
                        for kt in range(KT):
                            if j == 0 and s == 0 and h_needed:
                                pe.wait_ge(h_ready, h_needed + kt + 1)
                            last = nc.tensor.matmul(half(b, s), wring[:, slot, kt * 256 + s * P:kt * 256 + (s + 1) * P],
                                                    src[:, kt, :], start=kt == 0, stop=kt == KT - 1)
                    last.then_inc(unit_done, 1)

                each_unit(pe, n_units, base, body)

            def to_tokens(stage, n_units, h_needed):
                base = UNIT_AT[stage]

                def body(j, i, idx):
                    slot, b = unit(base, j, i), bank(stage, j, i)
                    for t in range(TT):
                        for kt in range(KT):
                            if j == 0 and t == 0:
                                pe.wait_ge(h_ready, h_needed + kt + 1)
                            last = nc.tensor.matmul(half(b, t), h[:, kt, t * P:(t + 1) * P],
                                                    wring[:, slot, kt * 256:(kt + 1) * 256],
                                                    start=kt == 0, stop=kt == KT - 1)
                    last.then_inc(unit_done, 1)

                each_unit(pe, n_units, base, body)

            def to_y(stage, src, wait):
                base = UNIT_AT[stage]

                for j in range(4):
                    slot = unit(base, j, None)
                    for s in range(2):
                        for kt in range(KT):
                            if j == 0 and s == 0:
                                wait(kt)
                            last = nc.tensor.matmul(y_ps(2 * j + s), wring[:, slot, kt * 256 + s * P:kt * 256 + (s + 1) * P],
                                                    src[:, kt, :], start=kt == 0, stop=kt == KT - 1)
                    last.then_inc(unit_done, 1)

            def ffn_out(stage, n_fi):
                base = UNIT_AT[stage]

                def body(j, i, idx):
                    slot = unit(base, j, i)
                    pe.wait_ge(bank_free, n_fi + 2 * idx + 2)
                    for s in range(2):
                        for n in range(KT):
                            rhs = act[:, bass.ds(idx * 2 + s, 1), :] if i is not None else act[:, 2 * j + s, :]
                            last = nc.tensor.matmul(y_ps(n), wring[:, slot, s * D + n * P:s * D + (n + 1) * P],
                                                    rhs,
                                                    start=j == 0 and s == 0 and n % 2 == 0,
                                                    stop=i is None and j == FT // 2 - 1 and s == 1,
                                                    skip_group_check=True)
                    last.then_inc(unit_done, 1)

                each_unit(pe, FT // 2, base, body, peel=1)

            def sum_squares(norm, out_ap, n):
                base = SQ_AT[norm]
                for kt in range(n):
                    pe.wait_ge(sq_ready, base + kt + 1)
                    nc.tensor.matmul(out_ap, ones, sq[:, kt % 2, :], start=kt == 0, stop=kt == n - 1).then_inc(sq_used, 1)

            def layer_norm(q):
                for kt in range(KT):
                    pe.wait_ge(resid, 8 * q + kt + 1)
                    last = nc.tensor.matmul(half(2, 0), ones, d[:, kt, :], start=kt == 0, stop=kt == KT - 1)
                last.then_inc(mean_mm, 1)
                sum_squares(f"ln{q}", half(3, 0), KT)

            def attention(layer):
                items = [(0, [2 * i, 2 * i + 1]) for i in range(4)] if layer == 0 else [(1, [i]) for i in range(8)]
                items += [(1, [8 + i]) for i in range(8)]
                item0 = 12 * layer
                map0 = MAPS * layer

                def scores(maps):
                    for m in maps:
                        n = map0 + m
                        if m >= 4:
                            pe.wait_ge(score_rd, n - 3)
                        qt, at = (m // 8) * 8 + (m % 8) // 2, (m % 2) * DH
                        q, k = qk[at:at + DH, qt, :], qk[at:at + DH, qt + 4, :]
                        b = m % 4
                        forget = layer == 1 and m >= 8
                        if forget:
                            pe.wait_ge(fd_head, m - 8 + 1)
                        for dst, tok, keys in ((psum[:, b, 0:256], slice(P, T), T), (psum[:, b, 256:384], slice(0, P), P)):
                            last = nc.tensor.matmul(dst, q[:, tok], k[:, 0:keys], start=True, stop=not forget)
                            if forget:
                                last = nc.tensor.matmul(dst, f_u[at:at + DH, tok], f_vh[m % 2][at:at + DH, 0:keys],
                                                        start=False, stop=True)
                        last.then_inc(score_mm, 1)

                scores(items[0][1])
                head = 0
                for i, (single, maps) in enumerate(items):
                    if i + 1 < len(items):
                        scores(items[i + 1][1])
                    n = item0 + i
                    s = score[:, maps[0] % 4, :]
                    pe.wait_ge(prob_ready, n + 1)
                    if i >= 2:
                        pe.wait_ge(pt_copied, n - 1)
                    b = 4 + i % 2
                    nc.tensor.transpose(psum[:, b, 0:P], s[:, 256:384], ident)
                    nc.tensor.transpose(psum[:, b, P:2 * P], s[:, 0:P], ident)
                    nc.tensor.transpose(psum[:, b, 2 * P:3 * P], s[:, P:2 * P], ident).then_inc(pt_mm, 1)
                    pe.wait_ge(pt_copied, n + 1)
                    if i >= 2:
                        pe.wait_ge(o_copied, n - 1)
                    b = 6 + i % 2
                    if single:
                        hd = (maps[0] % 8) + 8 * (maps[0] // 8)
                        lo, width, at = hd * DH, DH, (hd % 2) * DH
                    else:
                        lo, width, at = i * P, P, 0
                    nc.tensor.matmul(psum[at:at + width, b, 0:T], val[:, 0, lo:lo + width], prob_t[:, i % 2, 0:T],
                                     start=True, stop=False)
                    nc.tensor.matmul(psum[at:at + width, b, P:T], val[:, 1, lo:lo + width], prob_t[:, i % 2, T:T + P],
                                     start=False, stop=True).then_inc(o_mm, 1)

            pe.wait_ge(consts_in, CONSTS)
            nc.tensor.matmul(psum[0:16, 2, 0:384], table_in, hot_in, start=True, stop=True).then_inc(bias_mm, 1)

            pe.wait_ge(bias_in, 16)
            for n in range(2):
                if n:
                    pe.wait_ge(flipped, 1)
                for b in range(4):
                    last = nc.tensor.matmul(psum[:, 4 + b, :], flip_in, arena[:, (4 * n + b) * 512:(4 * n + b + 1) * 512],
                                            start=True, stop=True)
                last.then_inc(flip_mm, 1)

            for layer in range(DEPTH):
                hv = 16 * layer
                to_tokens(f"v{layer}", 4, hv)
                to_features(f"qk{layer}", 8, 0)
                if layer == 1:
                    for kt in range(KT):
                        last = nc.tensor.matmul(psum[0:8, 3, 0:T], w_forget[:, kt, :], h[:, kt, :],
                                                start=kt == 0, stop=kt == KT - 1)
                    last.then_inc(fd_mm, 1)
                    pe.wait_ge(fd_in, 1)
                pe.wait_ge(bank_free, BANK_AT[f"qk{layer}"] + 8)
                attention(layer)
                if layer == 0:
                    base = SQ_AT["heads"]
                    for i in range(4):
                        pe.wait_ge(sq_ready, base + i + 1)
                        nc.tensor.matmul(half(2 + i // 2, i % 2), ones, sq[:, i % 2, :], start=True,
                                         stop=True).then_inc(sq_used, 1)
                n_o = 12 if layer == 0 else 28

                def wait_o(kt, layer=layer, n_o=n_o):
                    if layer == 0 and kt == 0:
                        pe.wait_ge(o_ready, 4)
                    if kt == 0:
                        pe.wait_ge(o_copied, n_o)
                to_y(f"wo{layer}", o, wait_o)
                layer_norm(2 * layer)
                to_features(f"fi{layer}", 22, hv + 8)
                ffn_out(f"fo{layer}", BANK_AT[f"fi{layer}"])
                layer_norm(2 * layer + 1)

            sum_squares("mix", half(3, 0), KT)
            to_features("z", 8, 32)
            slot = unit(UNIT_AT["ple"], 0, None)
            pe.wait_ge(ple_in, 16)
            for n in range(KT):
                for kt in range(2):
                    last = nc.tensor.matmul(y_ps(n), wring[:, slot, kt * D + n * P:kt * D + (n + 1) * P],
                                            pt_in[:, kt, :], start=kt == 0, stop=kt == 1)
            last.then_inc(unit_done, 1)

            def convolve_tile(k):
                pe.wait_ge(z_in, 3 + k)
                pe.wait_ge(bank_free, BANK_AT["z"] + 8)
                for t in range(CONV_W):
                    pe.wait_ge(diag_ready, CONV_W * k + t + 1)
                    last = nc.tensor.matmul(half(k, 0), diag[:, (CONV_W * k + t) % DIAGS, :], u_pad[:, 2 + k, t:t + T],
                                            start=t == 0, stop=t == CONV_W - 1)
                    last.then_inc(diag_used, 1)

            convolve_tile(0)
            sum_squares("ple_proj", half(3, 0), KT)
            pe.wait_ge(blk_in, 64)
            pe.wait_ge(z_in, 8)
            pe.wait_ge(bank_free, BANK_AT["z"] + 8)
            pe.wait_ge(e_copied, 1)
            for g in range(2):
                for j in range(CT):
                    if g == 0:
                        pe.wait_ge(xr_ready, j + 1)
                    last = nc.tensor.matmul(half(4 + 2 * g + j // 2, j % 2), blk_w[:, g, j, :], lru_x[:, j, :],
                                            start=True, stop=True)
                last.then_inc(gates_mm, 1)
            convolve_tile(1)
            pe.wait_ge(conv_done, 4)
            for j in range(CT):
                last = nc.tensor.matmul(half(2, 0), ones, conv[:, j, :], start=j == 0, stop=j == CT - 1)
            last.then_inc(mean_mm, 1)
            sum_squares("conv", half(3, 0), CT)

            def wait_cat(kt):
                if kt == 0:
                    pe.wait_ge(cat_ready, 4)
                    pe.wait_ge(lru_u, 8)
            to_y("wout", cat, wait_cat)
            sum_squares("ffn", half(3, 0), KT)
            for t in range(TT):
                for kt in range(KT):
                    if t == 0:
                        pe.wait_ge(h_ready, 40 + kt + 1)
                    last = nc.tensor.matmul(psum[:, 0, t * 64:t * 64 + 36], h[:, kt, t * P:(t + 1) * P],
                                            w_route[:, kt, :], start=kt == 0, stop=kt == KT - 1)
            last.then_inc(route_mm, 1)
            for b in range(4):
                t, lo = b // 2, (b % 2) * 4
                for k in range(4):
                    last = nc.tensor.transpose(psum[:, 4 + b, k * P:(k + 1) * P],
                                               h[:, lo + k, t * P:(t + 1) * P], ident)
                last.then_inc(tok_mm, 1)
            pe.wait_ge(route_m, 1)
            pe.wait_ge(rc_in, 32)
            hot_m = r_hot_m
            tri = rc[:, RC_TRI:RC_TRI + P]
            nc.tensor.matmul(psum[:, 1, 0:NE], tri, hot_m[:, 0, :], start=True, stop=True)
            nc.tensor.matmul(psum[:, 1, 64:64 + NE], tri, hot_m[:, 1, :], start=True, stop=False)
            nc.tensor.matmul(psum[:, 1, 64:64 + NE], ones, hot_m[:, 0, :], start=False, stop=True)
            nc.tensor.matmul(psum[:, 1, 128:128 + NE], ones, hot_m[:, 0, :], start=True, stop=False)
            nc.tensor.matmul(psum[:, 1, 128:128 + NE], ones, hot_m[:, 1, :], start=False, stop=True).then_inc(rank_mm, 1)

            G, TR = 2, 3

            def gather(n_half, bank_no):
                for k in range(4):
                    kt = 4 * n_half + k
                    for t in range(TT):
                        last = nc.tensor.matmul(psum[:, bank_no, k * P:(k + 1) * P], hf_t(t, kt),
                                                hot_s[:, t, :, :], start=t == 0, stop=t == TT - 1)
                return last

            def scatter(start, stop):
                for n in range(KT):
                    last = nc.tensor.matmul(y_ps(n), y_e[:, n * P:(n + 1) * P], hot_gt,
                                            start=start and n % 2 == 0, stop=stop, skip_group_check=True)
                return last

            pe.wait_ge(routed, 2)
            rounds = pe.value_load(rounds_i[0:1, 0:1], min_val=1, max_val=4)
            pe.wait_ge(tok_copied, 4)
            pe.wait_ge(s_ready, 1)
            gather(0, G).then_inc(gat0, 1)
            gather(1, TR).then_inc(gat1, 1)
            pe.wait_ge(y1_c, 1)
            pe.wait_ge(sgt_c, 1)
            scatter(True, False)
            with pe.Fori(0, rounds) as r:
                with pe.Fori(0, PAIRS) as p:
                    n = r * PAIRS + p
                    pe.wait_ge(gat0_c, n + 1)
                    pe.wait_ge(gat1_c, n + 1)
                    pe.wait_ge(w13_loaded[0], n * 32 + 32)
                    pe.wait_ge(y0_c, n + 1)
                    for w in range(2):
                        if w:
                            pe.wait_ge(w13_loaded[1], n * 32 + 32)
                            pe.wait_ge(y1_c, n + 1)
                        for kt in range(KT):
                            for s in range(2):
                                last = nc.tensor.matmul(psum[s * CAP:(s + 1) * CAP, w, :],
                                                        xe_t[:, kt, s * CAP:(s + 1) * CAP],
                                                        w13[:, 2 * w + s, kt * FE:(kt + 1) * FE],
                                                        start=kt == 0, stop=kt == KT - 1)
                        last.then_inc((up1, up3)[w], 1)
                    pe.wait_ge(sgt_c, n + 1)
                    scatter(False, False).then_inc(scattered, 1)
                    pe.wait_ge(act_ready, n + 1)
                    for f in range(4):
                        last = nc.tensor.transpose(psum[:, TR, f * P:(f + 1) * P], act_e[:, f * P:(f + 1) * P], ident)
                    last.then_inc(actt_mm, 1)
                    pe.wait_ge(s_ready, n + 2)
                    gather(0, G).then_inc(gat0, 1)
                    pe.wait_ge(actt_c, n + 1)
                    gather(1, TR).then_inc(gat1, 1)
                    pe.wait_ge(sg_ready, n + 1)
                    pe.wait_ge(gat0_c, n + 2)
                    for t in range(TT):
                        last = nc.tensor.transpose(psum[:, G, t * P:(t + 1) * P],
                                                   hot_g[:, t, :, :].rearrange("p e c -> p (e c)"), ident)
                    last.then_inc(sgt_mm, 1)
                    pe.wait_ge(w2_loaded, n * 32 + 32)
                    for c in range(2):
                        for f in range(4):
                            for s in range(2):
                                last = nc.tensor.matmul(psum[s * CAP:(s + 1) * CAP, c, :],
                                                        act_t[:, f, s * CAP:(s + 1) * CAP],
                                                        arena[:, s * 4096 + f * D + c * 512:s * 4096 + f * D + c * 512 + 512],
                                                        start=f == 0, stop=f == 3)
                        last.then_inc((y0_mm, y1_mm)[c], 1)
            n_all = rounds * PAIRS
            pe.wait_ge(y0_c, n_all + 1)
            pe.wait_ge(y1_c, n_all + 1)
            pe.wait_ge(sgt_c, n_all + 1)
            scatter(False, True).then_inc(scattered, 1)

            sum_squares("gate", half(3, 0), KT)
            pe.wait_ge(x_ready, 49)
            to_y("pg", h, lambda kt: pe.wait_ge(h_ready, 48 + kt + 1))
            sum_squares("final", half(3, 0), KT)

        @block.scalar
        def _(act_e_):
            act = act_e_
            seq = [0]
            f_act = ctx_act = None
            Id, Cp = ACT.Identity, ACT.Copy

            def A(out_ap, in_ap, func, **kw):
                return nc.scalar.activation(out_ap, in_ap, func, **kw)

            def square(norm, kt, src):
                g = SQ_AT[norm] + kt
                if g >= 2:
                    act.wait_ge(sq_used, g - 1)
                A(sq[:, kt % 2, :], src, ACT.Square).then_inc(sq_ready, 1)

            def deviation(norm, n, features, eps):
                act.wait_ge(sq_used, SQ_AT[norm] + n)
                A(rstd[:], half(3, 0), ACT.Sqrt, scale=1.0 / features, bias=eps).then_inc(std_ready, 1)

            eps_ln, eps_rms = small[:, 60:61], small[:, 61:62]

            act.dma_start(cb[:], a["c_rows"]).then_inc(silu_c, 16)
            act.wait_ge(silu_c, 16)
            A(cb[:], cb[:], ACT.Silu).then_inc(silu_c, 1)
            act.wait_ge(bias_row, 1)
            act.dma_start(scratch, bias_rows).then_inc(bias_out, 16)
            act.wait_ge(bias_out, 16)
            toeplitz = bass.AP(scratch.tensor, 0, [[1, P], [384, 16], [1, 256]])
            act.dma_start(arena[:, 0:4096].rearrange("p (n t) -> p n t", t=256), toeplitz).then_inc(bias_in, 16)
            for n in range(2):
                act.wait_ge(flip_mm, n + 1)
                A(arena2[:, n * 2048:(n + 1) * 2048], psum[:, 4:8, :].rearrange("p b n -> p (b n)"), Cp).then_inc(flipped, 1)
            act.wait_ge(lam_sum, 2)
            A(small[:, 12:14], small[:, 10:12], ACT.Exp).then_inc(lam_exp, 1)
            act.wait_ge(drv_ready, 1)
            act.wait_ge(consts_in, CONSTS)
            for kt in range(KT):
                A(h[:, kt, :], x[:, kt, :], Id, scale=small[:, kt:kt + 1], bias=ada[:, 0, kt:kt + 1]).then_inc(h_ready, 1)

            def attention(layer):
                items = [(0, [2 * i, 2 * i + 1]) for i in range(4)] if layer == 0 else [(1, [i]) for i in range(8)]
                items += [(1, [8 + i]) for i in range(8)]

                def exps(maps):
                    for m in maps:
                        act.wait_ge(score_rd, MAPS * layer + m + 1)
                        s = score[:, m % 4, :]
                        A(s[:, 0:256], s[:, 0:256], ACT.Exp, scale=-1.0, bias=mins[:, m, 0:1], accum_out=den[:, m, 0:1])
                        A(s[:, 256:384], s[:, 256:384], ACT.Exp, scale=-1.0, bias=mins[:, m, 1:2],
                          accum_out=den[:, m, 1:2]).then_inc(exp_done, 1)

                exps(items[0][1])
                for i in range(len(items)):
                    n = 12 * layer + i
                    if i + 1 < len(items):
                        exps(items[i + 1][1])
                    act.wait_ge(pt_mm, n + 1)
                    if i >= 2:
                        act.wait_ge(o_mm, n - 1)
                    A(prob_t[:, i % 2, :], psum[:, 4 + i % 2, 0:384], Cp).then_inc(pt_copied, 1)

            def layer_norm(q):
                for kt in range(KT):
                    act.wait_ge(centred, 8 * q + kt + 1)
                    square(f"ln{q}", kt, d[:, kt, :])
                deviation(f"ln{q}", KT, D, eps_ln)
                if q < 3:
                    for kt in range(KT):
                        act.wait_ge(normed, 8 * q + kt + 1)
                        A(h[:, kt, :], d[:, kt, :], Id, scale=drv[:, q, 1, kt:kt + 1],
                          bias=drv[:, q, 2, kt:kt + 1]).then_inc(h_ready, 1)

            for layer in range(DEPTH):
                for j in range(4):
                    act.wait_ge(unit_done, UNIT_AT[f"v{layer}"] + j + 1)
                    A(val[:, :, j * 256:(j + 1) * 256], psum[:, j % 2, :].rearrange("p (a n) -> p a n", a=TT),
                      Cp).then_inc(bank_free, 1)

                def take_qk(j, i, idx, layer=layer):
                    act.wait_ge(unit_done, UNIT_AT[f"qk{layer}"] + idx + 1)
                    dst = (arena[:, bass.ds(idx * 512, 512)] if i is not None else arena[:, j * 512:(j + 1) * 512])
                    A(dst, psum[:, j % 2, :], Cp, scale=-DH ** -0.5 if j % 4 < 2 else 1.0).then_inc(bank_free, 1)
                each_unit(act, 8, 0, take_qk)
                if layer == 1:
                    act.wait_ge(fd_mm, 1)
                    act.wait_ge(x_ready, 17)
                    A(f_x[0:8, :], psum[0:8, 3, 0:T], Id, bias=fsmall[0:8, 0:1]).then_inc(fd_in, 1)
                    act.wait_ge(fd_in, 1)
                    A(f_e[0:8, :], f_x[0:8, :], ACT.Abs).then_inc(fd_abs, 1)
                    act.wait_ge(fd_abs, 1)
                    A(f_e[0:8, :], f_e[0:8, :], ACT.Exp, scale=-1.0).then_inc(fd_exp, 1)
                attention(layer)
                if layer == 0:
                    for i in range(4):
                        act.wait_ge(o_copied, i + 1)
                        square("heads", i, o[:, i, :])
                    act.wait_ge(sq_used, 4)
                    A(d_flat[:, 0:1024], psum[:, 2:4, :].rearrange("p b n -> p (b n)"), ACT.Sqrt, scale=1.0 / P,
                      bias=eps_ln).then_inc(std_ready, 1)
                layer_norm(2 * layer)

                def gate(j, i, idx, layer=layer):
                    n = BANK_AT[f"fi{layer}"] + j
                    act.wait_ge(unit_done, UNIT_AT[f"fi{layer}"] + idx + 1)
                    act.wait_ge(bank_free, BANK_AT[f"fi{layer}"] + idx - 1)
                    A(gate_s[:, j % 2, :], half(j % 2, 0), ACT.Silu).then_inc(gate_done, 1)
                each_unit(act, 22, 0, gate)
                layer_norm(2 * layer + 1)

            for kt in range(KT):
                act.wait_ge(x_ready, 25 + kt + 1)
                square("mix", kt, x[:, kt, :])
            deviation("mix", KT, D, eps_rms)
            A(small[:, 28:32], V("lam", 0, 4), ACT.Abs).then_inc(lru_abs, 1)
            act.wait_ge(lru_abs, 1)
            A(small[:, 28:32], small[:, 28:32], ACT.Exp, scale=-1.0).then_inc(lru_abs, 1)
            for j in range(8):
                act.wait_ge(unit_done, UNIT_AT["z"] + j + 1)
                if j < 4:
                    if j >= 2:
                        act.wait_ge(bank_free, BANK_AT["z"] + j - 1)
                    A(gate_s[:, j % 2, :], half(j % 2, 1), ACT.Sigmoid).then_inc(gate_done, 1)
                else:
                    A(lru_g[:, j - 4, :], half(j % 2, 1), ACT.Gelu_apprx_tanh).then_inc(gate_done, 1)
            act.wait_ge(unit_done, UNIT_AT["ple"] + 1)
            act.wait_ge(ada_done, ADA_PIECES)
            A(aring[:, 0, :], psum[:, 4:8, :].rearrange("p b n -> p (b n)"), Cp).then_inc(e_copied, 1)
            act.wait_ge(e_copied, 1)
            for kt in range(KT):
                square("ple_proj", kt, ple_e[:, kt, :])
            deviation("ple_proj", KT, D, eps_rms)
            for g in range(2):
                act.wait_ge(gates_mm, g + 1)
                for j in range(CT):
                    ins = A((g_r, g_i)[g][:, j, :], half(4 + 2 * g + j // 2, j % 2), ACT.Sigmoid,
                            bias=V("b_i" if g else "b_r", j))
                ins.then_inc(gates_act, 1)
            for k in range(2):
                act.wait_ge(diag_used, CONV_W * (k + 1))
                A(conv[:, 2 + k, :], half(k, 0), Id, bias=V("conv_b", 2 + k)).then_inc(conv_done, 1)
            act.wait_ge(lru_l, 1)
            A(t_b, t_a, ACT.Tanh).then_inc(lru_t, 1)
            A(g_r, t_a, ACT.Exp, scale=-1.0).then_inc(lru_t, 1)
            act.wait_ge(lru_u, 1)
            A(t_a, t_b, ACT.Sqrt, scale=2.0).then_inc(lru_t, 1)
            for j in range(CT):
                act.wait_ge(conv_norm, j + 1)
                square("conv", j, conv[:, j, :])
            deviation("conv", CT, 512, eps_rms)
            for j in range(CT):
                act.wait_ge(conv_norm, 4 + j + 1)
                A(cat[:, j, :], conv[:, j, :], ACT.Silu, scale=V("conv_ln_g", j), bias=V("conv_ln_b", j)).then_inc(cat_ready, 1)
            for kt in range(KT):
                act.wait_ge(x_ready, 33 + kt + 1)
                square("ffn", kt, x[:, kt, :])
            deviation("ffn", KT, D, eps_rms)
            for b in range(2):
                act.wait_ge(tok_mm, 2 * b + 2)
                A(d_flat[:, b * 1024:(b + 1) * 1024], psum[:, 4 + 2 * b:6 + 2 * b, :].rearrange("p b n -> p (b n)"),
                  Cp).then_inc(tok_copied, 2)
            act.wait_ge(route_d, 1)
            A(r_gwork, r_gwork, ACT.Exp).then_inc(route_exp, 1)
            act.wait_ge(route_d, 2)
            A(r_s[:, 6, :], r_s[:, 5, :], ACT.Exp).then_inc(route_exp, 1)

            act.wait_ge(y0_c, 1)
            A(y_e[:, 512:1024], y_e[:, 0:512], Cp).then_inc(y1_c, 1)
            A(hot_gt, y_e[:, 0:256], Cp).then_inc(sgt_c, 1)
            act.wait_ge(routed, 2)
            rounds = act.value_load(rounds_i[0:1, 0:1], min_val=1, max_val=4)
            act.wait_ge(gat0, 1)
            A(arena2[:, 0:512], psum[:, 2, :], Cp).then_inc(gat0_c, 1)
            with act.Fori(0, rounds) as r:
                with act.Fori(0, PAIRS) as p:
                    n = r * PAIRS + p
                    act.wait_ge(up1, n + 1)
                    A(silu1, psum[:, 0, :], ACT.Silu).then_inc(silu_e, 1)
                    act.wait_ge(actt_mm, n + 1)
                    A(arena2[:, 2816:3328], psum[:, 3, :], Cp).then_inc(actt_c, 1)
                    act.wait_ge(gat0, n + 2)
                    A(arena2[:, 0:512], psum[:, 2, :], Cp).then_inc(gat0_c, 1)
                    act.wait_ge(sgt_mm, n + 1)
                    A(hot_gt, psum[:, 2, 0:256], Cp).then_inc(sgt_c, 1)
                    act.wait_ge(y1_mm, n + 1)
                    A(y_e[:, 512:1024], psum[:, 1, :], Cp).then_inc(y1_c, 1)
            for kt in range(KT):
                act.wait_ge(x_ready, 41 + kt + 1)
                square("gate", kt, x[:, kt, :])
            deviation("gate", KT, D, eps_rms)
            for n in range(4):
                act.wait_ge(unit_done, UNIT_AT["pg"] + n + 1)
                A(d_flat[:, n * 512:(n + 1) * 512], psum[:, 4 + n, :], ACT.Sigmoid).then_inc(gate_done, 1)
            for kt in range(KT):
                act.wait_ge(x_ready, 49 + kt + 1)
                square("final", kt, x[:, kt, :])
            deviation("final", KT, D, eps_rms)

        @block.vector
        def _(dve):
            seq = [0]
            v = nc.vector

            def link(ins):
                seq[0] += 1
                ins.then_inc(dve_seq, 1)
                dve.wait_ge(dve_seq, seq[0])

            def stt(out_ap, in0, scalar, in1, op0, op1):
                return v.scalar_tensor_tensor(out_ap, in0, scalar, in1, op0, op1)

            def ada_piece(k, slot, turn_, cols, bias_cols):
                dve.wait_ge(a_loaded[slot], (turn_ + 1) * 16)
                for t in range(2):
                    w = aring[:, slot, t * D:(t + 1) * D]
                    v.tensor_tensor_reduce(out=w, in0=w, in1=cb[:], scale=1.0, scalar=0.0, op0=ALU.mult, op1=ALU.add,
                                           accum_out=ada_raw[:, 2 * slot + t:2 * slot + t + 1]).then_inc(ada_sum, 1)
                dve.wait_ge(ada_sum, k * 2 + 2)
                v.tensor_tensor(cols, ada_raw[:, 2 * slot:2 * slot + 2], bias_cols, ALU.add).then_inc(ada_done, 1)

            ada_cols = ada[:].rearrange("p l n -> p (l n)")

            def pieces(lo, hi):
                for k in range(lo, hi):
                    ada_piece(k, k % 2, k // 2, ada_cols[:, 2 * k:2 * k + 2], V("b_ada", 2 * k, 2))

            def derive(q):
                layer = q // 2
                part = lambda l, n: ada[:, l, 8 * n:8 * n + 8]
                g, b = V("ln_g", 8 * q, 8), V("ln_b", 8 * q, 8)
                dve.wait_ge(ada_done, ADA_PIECES if q else 24)
                link(v.tensor_scalar(drv[:, q, 0, :], part(layer, 5 if q % 2 else 2), 1.0, None, ALU.add))
                if q < 3:
                    l, sc, sh = ((0, 4, 3), (1, 1, 0), (1, 4, 3))[q]
                    link(stt(drv[:, q, 1, :], part(l, sc), 1.0, g, ALU.add, ALU.mult))
                    link(stt(drv[:, q, 2, :], part(l, sc), 1.0, b, ALU.add, ALU.mult))
                    link(v.tensor_tensor(drv[:, q, 2, :], drv[:, q, 2, :], part(l, sh), ALU.add))
                alpha = ALPHA if q < 3 else 1.0
                link(v.tensor_scalar(drv[:, q, 3, :], g, alpha, None, ALU.mult))
                v.tensor_scalar(drv[:, q, 4, :], b, alpha, None, ALU.mult).then_inc(drv_ready, 1)
                dve.wait_ge(drv_ready, q + 2)

            def log1p(y, z, w, s):
                link(v.tensor_scalar(z, y, 2.0, None, ALU.add))
                link(v.reciprocal(z, z))
                link(v.tensor_tensor(z, z, y, ALU.mult))
                link(v.tensor_tensor(w, z, z, ALU.mult))
                link(v.tensor_scalar(s, w, 1.0 / 17, None, ALU.mult))
                for n in (15, 13, 11, 9, 7, 5, 3):
                    link(stt(s, s, 1.0 / n, w, ALU.add, ALU.mult))
                link(stt(s, s, 1.0, z, ALU.add, ALU.mult))

            link(v.memset(small[:, 60:61], LN_EPS))
            link(v.memset(small[:, 61:62], RMS_EPS))
            dve.wait_ge(bias_mm, 1)
            dve.wait_ge(consts_in, CONSTS)
            stt(bias_rows, psum[0:16, 2, 0:384], -1.0, added_in, ALU.mult, ALU.add).then_inc(bias_row, 1)
            for n in range(2):
                l0, l1 = lam_in[:, 128 * n:128 * n + 64], lam_in[:, 128 * n + 64:128 * n + 128]
                v.tensor_tensor_reduce(out=l0, in0=l0, in1=l1, scale=1.0, scalar=0.0, op0=ALU.mult, op1=ALU.add,
                                       accum_out=small[:, 10 + n:11 + n]).then_inc(lam_sum, 1)
            dve.wait_ge(silu_c, 17)
            pieces(0, 8)
            dve.wait_ge(ada_done, 8)
            v.tensor_scalar(small[:, 0:8], ada[:, 0, 8:16], 1.0, None, ALU.add).then_inc(drv_ready, 1)
            pieces(8, 24)
            dve.wait_ge(lam_exp, 1)
            link(v.tensor_tensor(small[:, 14:15], small[:, 13:14], small[:, 12:13], ALU.subtract))
            link(v.tensor_scalar(small[:, 14:15], small[:, 14:15], -LAMBDA_INIT, None, ALU.add))
            link(v.tensor_scalar(small[:, 15:16], V("subln_g"), 1.0 - LAMBDA_INIT, None, ALU.mult))
            derive(0)

            def attention(layer):
                items = [(0, [2 * i, 2 * i + 1]) for i in range(4)] if layer == 0 else [(1, [i]) for i in range(8)]
                items += [(1, [8 + i]) for i in range(8)]
                item_of = {m: i for i, (_, maps) in enumerate(items) for m in maps}

                def head_operand(hd):
                    if hd >= 2:
                        dve.wait_ge(score_mm, MAPS * layer + 8 + hd - 1)
                    v.tensor_scalar(f_vh[hd % 2], f_v, fsmall[:, 1 + hd:2 + hd], None,
                                    ALU.mult).then_inc(fd_head, 1)

                def shift(maps):
                    for m in maps:
                        n = MAPS * layer + m
                        dve.wait_ge(score_mm, n + 1)
                        if m >= 4:
                            dve.wait_ge(pt_mm, 12 * layer + item_of[m - 4] + 1)
                        if m < 8:
                            bt = bias[:, m // 2 if layer == 0 else m, :]
                        else:
                            bt = bias[:, m if layer == 0 else 16, :]
                        s, b = score[:, m % 4, :], m % 4
                        v.tensor_tensor_reduce(out=s[:, 0:256], in0=psum[:, b, 0:256], in1=bt, scale=1.0,
                                               scalar=3e38, op0=ALU.add, op1=ALU.min, accum_out=mins[:, m, 0:1])
                        v.tensor_tensor_reduce(out=s[:, 256:384], in0=psum[:, b, 256:384], in1=bt[:, P:2 * P],
                                               scale=1.0, scalar=3e38, op0=ALU.add, op1=ALU.min,
                                               accum_out=mins[:, m, 1:2]).then_inc(score_rd, 1)

                def normalise(i, single, maps):
                    m = maps[-1]
                    n = 12 * layer + i
                    dve.wait_ge(exp_done, MAPS * layer + m + 1)
                    s = score[:, maps[0] % 4, :]
                    if single:
                        link(v.reciprocal(den[:, m, :], den[:, m, :]))
                        v.tensor_scalar(s[:, 0:256], s[:, 0:256], den[:, m, 0:1], None, ALU.mult)
                        v.tensor_scalar(s[:, 256:384], s[:, 256:384], den[:, m, 1:2], None, ALU.mult).then_inc(prob_ready, 1)
                    else:
                        s1, m0 = score[:, m % 4, :], maps[0]
                        link(v.reciprocal(den[:, m0:m + 1, :], den[:, m0:m + 1, :]))
                        link(v.tensor_scalar(den[:, m, :], den[:, m, :], small[:, 14:15], None, ALU.mult))
                        v.tensor_scalar(s1[:, 0:256], s1[:, 0:256], den[:, m, 0:1], None, ALU.mult)
                        link(v.tensor_scalar(s1[:, 256:384], s1[:, 256:384], den[:, m, 1:2], None, ALU.mult))
                        stt(s[:, 0:256], s[:, 0:256], den[:, m0, 0:1], s1[:, 0:256], ALU.mult, ALU.add)
                        stt(s[:, 256:384], s[:, 256:384], den[:, m0, 1:2], s1[:, 256:384], ALU.mult,
                            ALU.add).then_inc(prob_ready, 1)

                def take_o(i, single, maps):
                    dve.wait_ge(o_mm, 12 * layer + i + 1)
                    tile, at, width = (maps[0] // 2, (maps[0] % 2) * DH, DH) if single else (i, 0, P)
                    v.tensor_copy(o[at:at + width, tile, :], psum[at:at + width, 6 + i % 2, 0:T]).then_inc(o_copied, 1)

                if layer == 1:
                    head_operand(0)
                    head_operand(1)
                shift(items[0][1])
                for i, (single, maps) in enumerate(items):
                    if i + 1 < len(items):
                        shift(items[i + 1][1])
                        nxt = items[i + 1][1][0]
                        if layer == 1 and 8 <= nxt < 14:
                            head_operand(nxt - 8 + 2)
                    normalise(i, single, maps)
                    if i:
                        take_o(i - 1, *items[i - 1])
                take_o(len(items) - 1, *items[-1])

            def invert(norm):
                dve.wait_ge(std_ready, NORM_NO[norm] + 1)
                link(v.reciprocal(rstd[:], rstd[:]))

            def layer_norm(q):
                if q % 2:
                    dve.wait_ge(unit_done, UNIT_AT[f"fo{q // 2}"] + 11)
                dve.wait_ge(x_ready, 1 + 8 * q)
                dve.wait_ge(h_ready, 8 * q + 8)
                for kt in range(KT):
                    if q % 2 == 0:
                        dve.wait_ge(unit_done, UNIT_AT[f"wo{q // 2}"] + kt // 2 + 1)
                    stt(d[:, kt, :], y_ps(kt), drv[:, q, 0, kt:kt + 1], x[:, kt, :], ALU.mult, ALU.add).then_inc(resid, 1)
                dve.wait_ge(mean_mm, q + 1)
                for kt in range(KT):
                    stt(d[:, kt, :], half(2, 0), -1.0 / D, d[:, kt, :], ALU.mult, ALU.add).then_inc(centred, 1)
                invert(f"ln{q}")
                for kt in range(KT):
                    v.tensor_tensor(d[:, kt, :], d[:, kt, :], rstd[:], ALU.mult).then_inc(normed, 1)

            def rms(norm, src, gain, dst, signal):
                invert(norm)
                for kt in range(KT):
                    stt(dst[:, kt, :], src[:, kt, :], V(gain, kt), rstd[:], ALU.mult, ALU.mult).then_inc(signal, 1)

            for layer in range(DEPTH):
                if layer == 1:
                    derive(2)
                    derive(3)
                    dve.wait_ge(fd_exp, 1)
                    f8 = lambda ap: ap[0:8, :]
                    link(v.memset(f_u, 0.0))
                    link(v.memset(f_v, 0.0))
                    log1p(f8(f_e), f8(f_z), f8(f_w), f8(f_vh[0]))
                    link(v.tensor_scalar(f8(f_x), f8(f_x), 0.0, None, ALU.min))
                    link(stt(f8(f_x), f8(f_vh[0]), -2.0, f8(f_x), ALU.mult, ALU.add))
                    link(v.memset(f8(f_z), 1.0))
                    link(v.tensor_tensor_scan(f8(f_u), f8(f_z), f8(f_x), 0.0, ALU.mult, ALU.add))
                    for at in (32, 96):
                        link(v.tensor_copy(f_v[at:at + 8, :], f8(f_u)))
                        link(v.memset(f_u[at:at + 8, :], 1.0))
                        link(v.memset(f_v[at - 32:at - 24, :], -1.0))
                    link(v.tensor_copy(f_u[64:72, :], f8(f_u)))
                else:
                    dve.wait_ge(flipped, 2)
                attention(layer)
                if layer == 0:
                    dve.wait_ge(std_ready, 1)
                    link(v.reciprocal(d_flat[:, 0:1024], d_flat[:, 0:1024]))
                    for i in range(4):
                        stt(o[:, i, :], o[:, i, :], small[:, 15:16], d[:, i, :], ALU.mult, ALU.mult).then_inc(o_ready, 1)
                layer_norm(2 * layer)

                def gated(j, i, idx, layer=layer):
                    dve.wait_ge(gate_done, 22 * layer + idx + 1)
                    dst = act[:, bass.ds(idx, 1), :] if i is not None else act[:, j, :]
                    v.tensor_tensor(dst, gate_s[:, j % 2, :], half(j % 2, 1), ALU.mult).then_inc(bank_free, 1)
                    if layer == 0:
                        if i is None:
                            pieces(24 + j, 25 + j)
                        else:
                            k = idx + 24
                            ada_piece(k, j % 2, (24 + j) // 2 + i * 2, ada_cols[:, bass.ds(k * 2, 2)],
                                      vec[:, bass.ds(k * 2 + VEC_AT["b_ada"], 2)])
                each_unit(dve, 22, 0, gated)
                if layer == 0:
                    pieces(46, 48)
                    derive(1)
                layer_norm(2 * layer + 1)

            rms("mix", x, "g_mix", h, h_ready)
            dve.wait_ge(lru_abs, 2)
            log1p(small[:, 28:32], small[:, 32:36], small[:, 36:40], small[:, 40:44])
            link(v.tensor_scalar(small[:, 20:24], V("lam", 0, 4), -1.0, 0.0, ALU.mult, ALU.max))
            link(stt(small[:, 20:24], small[:, 40:44], 2.0, small[:, 20:24], ALU.mult, ALU.add))
            link(v.tensor_scalar(small[:, 20:24], small[:, 20:24], 8.0, None, ALU.mult))
            dve.wait_ge(pad_zero, 2)
            for j in range(8):
                dve.wait_ge(gate_done, 44 + j + 1)
                if j < 4:
                    v.tensor_tensor(u_pad[:, j, PU:PU + T], gate_s[:, j % 2, :], half(j % 2, 0), ALU.mult).then_inc(bank_free, 1)
                    dve.wait_ge(bank_free, BANK_AT["z"] + j + 1)
                    dve.sem_inc(z_in, 1)
                else:
                    v.tensor_copy(l_pad[:, j - 4, PL:PL + T], half(j % 2, 0)).then_inc(bank_free, 1)
                    dve.wait_ge(bank_free, BANK_AT["z"] + j + 1)
                    dve.sem_inc(z_in, 1)
            for j in range(CT):
                for t in range(LRU_W):
                    w = V("lru_w", j * LRU_W + t)
                    if t:
                        ins = stt(lru_x[:, j, :], l_pad[:, j, t:t + T], w, lru_x[:, j, :], ALU.mult, ALU.add)
                    else:
                        ins = v.tensor_scalar(lru_x[:, j, :], l_pad[:, j, 0:T], w, V("lru_b", j), ALU.mult, ALU.add)
                    if t < LRU_W - 1:
                        link(ins)
                    else:
                        ins.then_inc(xr_ready, 1)
            rms("ple_proj", ple_e, "g_ple_proj", ple_e, ple_scaled)
            dve.wait_ge(gates_act, 1)
            for j in range(CT):
                ins = v.tensor_scalar(t_a[:, j, :], g_r[:, j, :], small[:, 20 + j:21 + j], None, ALU.mult)
            ins.then_inc(lru_l, 1)
            convolve(dve, v, (0, 1), dve_taps)
            dve.wait_ge(lru_t, 2)
            link(v.tensor_scalar(t_c, t_b, 1.0, None, ALU.add))
            link(v.reciprocal(t_c, t_c))
            v.tensor_tensor(t_b, t_b, t_c, ALU.mult).then_inc(lru_u, 1)
            dve.wait_ge(gates_act, 2)
            v.tensor_tensor(g_i, g_i, lru_x, ALU.mult).then_inc(lru_u, 1)
            dve.wait_ge(lru_t, 3)
            dve.wait_ge(lru_u, 2)
            v.tensor_tensor(t_b, t_a, g_i, ALU.mult).then_inc(lru_u, 1)
            dve.wait_ge(lru_u, 3)
            for j in range(CT):
                link(v.tensor_tensor_scan(t_c[:, j, :], g_r[:, j, :], t_b[:, j, :], 0.0, ALU.mult, ALU.add))
            v.tensor_tensor(cat[:, CT:2 * CT, :], t_c, lru_g, ALU.mult).then_inc(lru_u, 5)
            dve.wait_ge(mean_mm, 5)
            for j in range(CT):
                stt(conv[:, j, :], half(2, 0), -1.0 / 512, conv[:, j, :], ALU.mult, ALU.add).then_inc(conv_norm, 1)
            invert("conv")
            for j in range(CT):
                v.tensor_tensor(conv[:, j, :], conv[:, j, :], rstd[:], ALU.mult).then_inc(conv_norm, 1)
            for kt in range(KT):
                dve.wait_ge(unit_done, UNIT_AT["wout"] + kt // 2 + 1)
                v.tensor_tensor(x[:, kt, :], x[:, kt, :], y_ps(kt), ALU.add).then_inc(x_ready, 1)
            rms("ffn", x, "g_ffn", h, h_ready)

            dve.wait_ge(rc_in, 32)
            dve.wait_ge(route_mm, 1)
            tiles = lambda ap, n: ap.unsqueeze(1).to_broadcast([P, TT, n])
            along = lambda ap, n: ap.unsqueeze(2).to_broadcast([P, TT, n])
            S = lambda i: r_s[:, i, :]
            w4, w32 = rc[:, RC_W4:RC_W4 + NG], rc[:, RC_W32:RC_W32 + NE]

            def first_max(values, best, n, weights, work, hot):
                link(v.tensor_reduce(best, values, AX_X, ALU.max))
                link(v.tensor_tensor(work, values, along(best, n), ALU.is_equal))
                link(v.tensor_tensor(work, work, tiles(weights, n), ALU.mult))
                link(v.tensor_reduce(S(10), work, AX_X, ALU.max))
                link(v.tensor_tensor(hot, work, along(S(10), n), ALU.is_equal))

            link(v.tensor_tensor(r_logit, psum[:, 0, 0:128].rearrange("p (a n) -> p a n", a=TT)[:, :, 0:36],
                                 tiles(b_route, 36), ALU.add))
            gl, el = r_logit[:, :, 0:NG], r_logit[:, :, NG:NG + NE]
            first_max(gl, S(0), NG, w4, r_gwork, r_ghot)
            v.tensor_tensor(r_gwork, gl, along(S(0), NG), ALU.subtract).then_inc(route_d, 1)
            link(v.tensor_scalar(r_pen, r_ghot, -1.0, 1e30, ALU.add, ALU.mult))
            for t in range(TT):
                link(v.tensor_tensor(r_el[:, t, :].rearrange("p (g e) -> p g e", g=NG),
                                     el[:, t, :].rearrange("p (g e) -> p g e", g=NG),
                                     r_pen[:, t, :].unsqueeze(2).to_broadcast([P, NG, EPG]), ALU.add))
            first_max(r_el, S(3), NE, w32, r_work, r_first)
            link(stt(r_el, r_first, -1e30, r_el, ALU.mult, ALU.add))
            first_max(r_el, S(4), NE, w32, r_work, r_hot_m)
            v.tensor_tensor(S(5), S(4), S(3), ALU.subtract).then_inc(route_d, 1)
            dve.wait_ge(route_exp, 1)
            link(v.tensor_reduce(S(1), r_gwork, AX_X, ALU.add))
            link(v.reciprocal(S(1), S(1)))
            dve.wait_ge(route_exp, 2)
            link(v.tensor_scalar(S(7), S(6), 1.0, None, ALU.add))
            link(v.reciprocal(S(7), S(7)))
            link(v.tensor_tensor(S(7), S(7), S(1), ALU.mult))
            link(v.tensor_tensor(S(8), S(7), S(6), ALU.mult))
            link(v.tensor_tensor(r_gate, r_first, along(S(7), NE), ALU.mult))
            link(v.tensor_tensor(r_work, r_hot_m, along(S(8), NE), ALU.mult))
            link(v.tensor_tensor(r_gate, r_gate, r_work, ALU.add))
            v.tensor_tensor(r_hot_m, r_hot_m, r_first, ALU.add).then_inc(route_m, 1)
            dve.wait_ge(rank_mm, 1)
            link(v.tensor_scalar(r_work, r_hot_m, -1.0, 1e6, ALU.add, ALU.mult))
            for t in range(TT):
                link(v.tensor_tensor(r_rank[:, t, 0:NE], psum[:, 1, t * 64:t * 64 + NE], r_hot_m[:, t, :], ALU.mult))
            link(v.tensor_tensor(r_rank[:, :, 0:NE], r_rank[:, :, 0:NE], r_work, ALU.add))
            link(v.tensor_scalar(r_rank[:, :, NE:NE + 2], r_rank[:, :, 0:2], -float(CAP), None, ALU.add))
            link(v.tensor_reduce(r_s[:, 11, 0:1], psum[:, 1, 128:128 + NE], AX_X, ALU.max))
            link(v.tensor_scalar(r_s[:, 12, 0:1], r_s[:, 11, 0:1], float(CAP), 1.0, ALU.is_gt, ALU.add))
            for n in (2, 3):
                link(v.tensor_scalar(r_s[:, 13, 0:1], r_s[:, 11, 0:1], float(n * CAP), None, ALU.is_gt))
                link(v.tensor_tensor(r_s[:, 12, 0:1], r_s[:, 12, 0:1], r_s[:, 13, 0:1], ALU.add))
            link(v.tensor_copy(rounds_i[:], r_s[:, 12, 0:1]))
            dve.sem_inc(routed, 2)
            rounds = dve.value_load(rounds_i[0:1, 0:1], min_val=1, max_val=4)

            slots4 = rc[:, RC_SLOT:RC_SLOT + CAP].unsqueeze(1).to_broadcast([P, 2, CAP])

            def choose(first):
                for t in range(TT):
                    rank = r_rank[:, t, first].unsqueeze(2).to_broadcast([P, 2, CAP])
                    ins = v.tensor_tensor(hot_s[:, t, :, :], slots4, rank, ALU.is_equal)
                return ins

            v.memset(y_e[:, 0:512], 0.0).then_inc(y0_c, 1)
            choose(slice(0, 2)).then_inc(s_ready, 1)
            dve.wait_ge(gat1, 1)
            v.tensor_copy(arena2[:, 512:1024], psum[:, 3, :]).then_inc(gat1_c, 1)
            with dve.Fori(0, rounds) as r:
                with dve.Fori(0, PAIRS) as p:
                    n = r * PAIRS + p
                    dve.wait_ge(up1, n + 1)
                    dve.wait_ge(s_ready, n + 1)
                    for t in range(TT):
                        gates = r_gate[:, t, bass.ds(p * 2, 2)].unsqueeze(2).to_broadcast([P, 2, CAP])
                        ins = v.tensor_tensor(hot_g[:, t, :, :], hot_s[:, t, :, :], gates, ALU.mult)
                    ins.then_inc(sg_ready, 1)
                    dve.wait_ge(sg_ready, n + 1)
                    choose(bass.ds(p * 2 + 2, 2)).then_inc(s_ready, 1)
                    dve.wait_ge(silu_e, n + 1)
                    dve.wait_ge(up3, n + 1)
                    v.tensor_tensor(act_e, silu1, psum[:, 1, :], ALU.mult).then_inc(act_ready, 1)
                    dve.wait_ge(gat1, n + 2)
                    v.tensor_copy(arena2[:, 512:1024], psum[:, 3, :]).then_inc(gat1_c, 1)
                    dve.wait_ge(y0_mm, n + 1)
                    v.tensor_copy(y_e[:, 0:512], psum[:, 0, :]).then_inc(y0_c, 1)
                dve.wait_ge(s_ready, r * PAIRS + (PAIRS + 1))
                v.tensor_scalar(r_rank, r_rank, -float(CAP), None, ALU.add).then_inc(next_round, 1)
                dve.wait_ge(next_round, r + 1)
            dve.wait_ge(scattered, rounds * PAIRS + 1)
            for kt in range(KT):
                v.tensor_tensor(x[:, kt, :], x[:, kt, :], y_ps(kt), ALU.add).then_inc(x_ready, 1)
            rms("gate", x, "g_ple", h, h_ready)
            dve.wait_ge(ple_scaled, 8)
            for kt in range(KT):
                dve.wait_ge(gate_done, 52 + kt // 2 + 1)
                link(v.tensor_tensor(d[:, kt, :], d[:, kt, :], ple_e[:, kt, :], ALU.mult))
                v.tensor_tensor(x[:, kt, :], x[:, kt, :], d[:, kt, :], ALU.add).then_inc(x_ready, 1)
            rms("final", x, "g_final", d, out_ready)


INPUTS = ["x_t", "c_rows", "table", "vecs", "ada", "units", "lam_in", "w_forget", "forget_b", "p_t", "w_r", "w_i",
          "w_route", "b_route", "w1", "w3", "w2"]


def lay_out(i):
    f = {k: np.asarray(v) for k, v in i.items()}

    def features(m):
        return np.ascontiguousarray(m.reshape(-1, P, m.shape[1]).transpose(1, 0, 2))

    def cols(v):
        return v.reshape(-1, P).T

    def col_units(w):
        k, n = w.shape
        return w.reshape(KT, P, n // 256, 256).transpose(2, 1, 0, 3).reshape(n // 256, P, UNIT)

    def row_units(w):
        k, n = w.shape
        return w.reshape(k // 256, 2, P, n).transpose(0, 2, 1, 3).reshape(k // 256, P, UNIT)

    def pairs(w):
        k, n = w.shape
        return w.reshape(k, 2, n // 256, P).transpose(0, 2, 1, 3).reshape(k, n)

    ab, cd = f["w_in_ab"][0], f["w_in_cd"][0]
    units = []
    for layer, w in enumerate((ab, cd)):
        units += [col_units(np.concatenate([w[:, 1024:1536], w[:, 2560:3072]], axis=1)),
                  col_units(np.concatenate([w[:, 0:1024], w[:, 1536:2560]], axis=1)),
                  col_units(f["w_o"][layer]), col_units(pairs(f["w_ffn_in"][layer])), row_units(f["w_ffn_out"][layer])]
    w = f["w_in_2"][0]
    units += [col_units(np.concatenate([pairs(w[:, 0:1024]), pairs(w[:, 1024:2048])], axis=1)),
              row_units(f["w_ple_2"][0]), col_units(f["w_out_2"][0]), col_units(f["w_ple_gate_2"][0])]
    vecs = {
        "b_ada": cols(f["b_ada"]), "ln_g": cols(f["ln_g"]), "ln_b": cols(f["ln_b"]), "subln_g": cols(f["diff_subln_g"]),
        "conv_w": f["conv_dw_w_2"][0].reshape(CONV_W, CT, P).transpose(2, 1, 0).reshape(P, -1),
        "conv_b": cols(f["conv_dw_b_2"]), "conv_ln_g": cols(f["conv_ln_g_2"]), "conv_ln_b": cols(f["conv_ln_b_2"]),
        "lru_w": f["lru_conv_w_2"][0].reshape(LRU_W, CT, P).transpose(2, 1, 0).reshape(P, -1),
        "lru_b": cols(f["lru_conv_b_2"]), "b_r": cols(f["lru_b_r_2"]), "b_i": cols(f["lru_b_i_2"]),
        "lam": cols(f["lru_lambda_2"]), "g_mix": cols(f["g_mix_2"]), "g_ffn": cols(f["g_ffn_2"]),
        "g_ple": cols(f["g_ple_2"]), "g_ple_proj": cols(f["g_ple_proj_2"]), "g_final": cols(f["g_final_2"]),
    }
    ada = f["w_ada"].reshape(DEPTH, D, 24, 2, P).transpose(0, 2, 4, 3, 1).reshape(ADA_PIECES, P, UNIT)
    up = lambda w: w[0].reshape(PAIRS, 2, KT, P, FE).transpose(0, 1, 3, 2, 4).reshape(PAIRS, 2, P, 4096)
    blocks = lambda w: w[0].reshape(CT, 2, 64, 64).transpose(1, 2, 0, 3).reshape(P, CT, 64)
    laid = {
        "x_t": features(f["x"][0].T), "c_rows": np.broadcast_to(f["c"], (P, D)),
        "table": np.concatenate([f["rel_bias"][:, 0:8], f["rel_bias"][:, 4:12]], axis=1),
        "vecs": np.concatenate([vecs[n] for n, _ in VECS], axis=1), "ada": ada, "units": np.concatenate(units),
        "lam_in": np.broadcast_to(f["diff_lambda"][0].reshape(1, 256), (P, 256)),
        "w_forget": cd[:, 3072:3080].reshape(KT, P, 8).transpose(1, 0, 2), "forget_b": f["forget_b"].T,
        "p_t": features(f["p_2"][0, 0].T), "w_r": blocks(f["lru_w_r_2"]), "w_i": blocks(f["lru_w_i_2"]),
        "w_route": np.concatenate([f["w_group_2"][0], f["w_expert_2"][0]], axis=1).reshape(KT, P, 36).transpose(1, 0, 2),
        "b_route": np.broadcast_to(np.concatenate([f["b_group_2"][0], f["b_expert_2"][0]])[None], (P, 36)),
        "w1": up(f["w1_2"]), "w3": up(f["w3_2"]),
        "w2": f["w2_2"][0].reshape(PAIRS, 2, 4, P, D).transpose(0, 1, 3, 2, 4).reshape(PAIRS, 2, P, 4096),
    }
    laid.update(shape_constants())
    return {k: np.ascontiguousarray(v) for k, v in laid.items()}


def kernel(**inputs):
    import concourse.bacc as bacc
    from concourse.bass_utils import run_bass_kernel_spmd

    arrays = lay_out(inputs)
    nc = bacc.Bacc("TRN2", target_bir_lowering=False, num_devices=1)
    a = {n: nc.dram_tensor(f"in_{n}", v.shape, mybir.dt.from_np(v.dtype), kind="ExternalInput").ap() for n, v in arrays.items()}
    out = nc.dram_tensor("out", (P, KT, T), F32, kind="ExternalOutput").ap()
    build(nc, a, out)
    r = run_bass_kernel_spmd(nc, [{f"in_{n}": v for n, v in arrays.items()}], core_ids=[0])
    return np.ascontiguousarray(r.results[0]["out"].transpose(2, 1, 0).reshape(1, T, D))
```

```python
import math
from contextlib import ExitStack

import numpy as np

import concourse.bass as bass
from concourse import mybir
from concourse.alu_op_type import AluOpType as ALU

ACT = mybir.ActivationFunctionType
F32 = mybir.dt.float32
F32R = mybir.dt.float32r
I32 = mybir.dt.int32
AX_X = mybir.AxisListType.X

P = 128
T = 256
TT = T // P
D = 1024
KT = D // P
DEPTH = 2
DH = 64
D_FF = 2816
FT = D_FF // P
ALPHA = (2 * DEPTH) ** 0.25
LN_EPS = 1e-5
RMS_EPS = 1e-6
LAMBDA_INIT = 0.8 - 0.6 * math.exp(0.0)
MASKED = 1e30
MAPS = 16
BUCKETS = 32
CONV_W, LRU_W = 31, 4
CT = 4
NE, NG, EPG = 32, 4, 8
FE = 512
CAP = 64
PAIRS = NE // 2

RING = 4
UNIT = 2048
ARING = 2

VECS = [("b_ada", 96), ("ln_g", 32), ("ln_b", 32), ("subln_g", 1), ("conv_w", CT * CONV_W),
        ("conv_b", 4), ("conv_ln_g", 4), ("conv_ln_b", 4), ("lru_w", CT * LRU_W), ("lru_b", 4),
        ("b_r", 4), ("b_i", 4), ("lam", 4), ("g_mix", 8), ("g_ffn", 8), ("g_ple", 8),
        ("g_ple_proj", 8), ("g_final", 8)]
VEC_AT = {}
_at = 0
for _name, _n in VECS:
    VEC_AT[_name] = _at
    _at += _n
N_VEC = _at

RC_TRI, RC_SLOT, RC_W4, RC_W32, N_RC = 0, 128, 192, 196, 228

STAGES = [("v0", 4), ("qk0", 8), ("wo0", 4), ("fi0", 22), ("fo0", 11),
          ("v1", 4), ("qk1", 8), ("wo1", 4), ("fi1", 22), ("fo1", 11),
          ("z", 8), ("ple", 1), ("wout", 4), ("pg", 4)]
UNIT_AT = {}
_at = 0
for _name, _n in STAGES:
    UNIT_AT[_name] = _at
    _at += _n
N_UNITS = _at
BANK_AT = {"v0": 0, "qk0": 4, "fi0": 12, "v1": 34, "qk1": 38, "fi1": 46, "z": 68}

NORMS = [("heads", 4), ("ln0", 8), ("ln1", 8), ("ln2", 8), ("ln3", 8), ("mix", 8), ("ple_proj", 8),
         ("conv", 4), ("ffn", 8), ("gate", 8), ("final", 8)]
SQ_AT = {}
_at = 0
for _name, _n in NORMS:
    SQ_AT[_name] = _at
    _at += _n
NORM_NO = {name: i for i, (name, _) in enumerate(NORMS)}

CONSTS, LATER = 6 * 16, 6 * 16
STAGED = 8
ADA_PIECES = 48


def shape_constants():
    ident = np.eye(P, dtype=np.float32)
    consts = np.concatenate([ident, np.ones((P, P), np.float32)], axis=1)
    n = 255 - np.arange(384)
    past = np.maximum(n, 0)
    large = 16 + (np.log(np.maximum(past, 1).astype(np.float32) / 16) / np.float32(math.log(128 / 16)) * 16).astype(np.int32)
    bucket = np.where(past < 16, past, np.minimum(large, BUCKETS - 1))
    hot = ((bucket[None, :] == np.arange(BUCKETS)[:, None]) & (n >= 0)[None, :]).astype(np.float32)
    times = (n <= 128).astype(np.float32) + (n % 4 == 0) + (n % 16 == 0)
    plain = np.where(n >= 0, 0.0, MASKED).astype(np.float32)
    dilated = np.where((n >= 0) & (times > 0), -np.log(np.maximum(times, 1)), MASKED).astype(np.float32)
    added = np.concatenate([np.tile(plain, (8, 1)), np.tile(dilated, (8, 1))]).astype(np.float32)
    q, k = np.arange(P)[:, None], np.arange(P)[None, :]
    causal = np.concatenate([np.zeros((P, P)), np.where(k <= q, 0.0, MASKED)], axis=1).astype(np.float32)
    router = np.zeros((P, N_RC), np.float32)
    router[:, RC_TRI:RC_TRI + P] = (q < k)
    router[:, RC_SLOT:RC_SLOT + CAP] = np.arange(CAP)
    router[:, RC_W4:RC_W4 + NG] = 8 - np.arange(NG)
    router[:, RC_W32:RC_W32 + NE] = 64 - np.arange(NE)
    rows = np.zeros((4, 32, 8), np.float32)
    rows[:, np.arange(8), np.arange(8)] = 1
    rows = rows.reshape(P, 8)
    return {"consts": consts, "hot": hot, "added": added, "causal": causal, "router_consts": router,
            "head_rows": rows, "flip": np.ascontiguousarray(ident[::-1])}


def build(nc, a, out):
    ctx = ExitStack()
    with ctx:
        where = {}

        def sb(name, shape, dt=F32):
            where[name] = (nc.sbuf_base + 31) // 32 * 32
            return ctx.enter_context(nc.sbuf_tensor(name, shape, dt))

        def sem(name):
            return ctx.enter_context(nc.semaphore(name))

        wring = sb("wring", [P, RING, UNIT])
        aring = sb("aring", [P, ARING, UNIT])
        w13 = sb("w13", [P, 4, 4096])
        arena = sb("arena", [P, 8192])
        arena2 = sb("arena2", [P, 6656])
        x = sb("x", [P, KT, T])
        h = sb("h", [P, KT, T])
        d = sb("d", [P, KT, T])
        sq = sb("sq", [P, 2, T])
        rstd = sb("rstd", [P, T])
        vec = sb("vec", [P, N_VEC])
        cb = sb("cb", [P, D])
        lam_in = sb("lam_in", [P, 256])
        cst = sb("cst", [P, 2 * P])
        w_route = sb("w_route", [P, KT, 36])
        w_forget = sb("w_forget", [P, KT, 8])
        ada = sb("ada", [P, DEPTH, 48])
        ada_raw = sb("ada_raw", [P, 4])
        drv = sb("drv", [P, 4, 5, 8])
        mins = sb("mins", [P, MAPS, 2])
        den = sb("den", [P, MAPS, 2])
        small = sb("small", [P, 64])
        fsmall = sb("fsmall", [P, 16])

        ident = cst[:, 0:P]
        ones = cst[:, P:2 * P]
        h_tile = lambda kt: h[:, kt, :]
        qk = arena[:, 0:4096].rearrange("p (n t) -> p n t", t=T)
        val = arena[:, 4096:6144].rearrange("p (a n) -> p a n", a=TT)
        o = arena[:, 6144:8192].rearrange("p (n t) -> p n t", t=T)
        bias = arena2[:, 0:17 * 256].rearrange("p (n t) -> p n t", t=256)
        score = arena2[:, 4352:4352 + 4 * 384].rearrange("p (n t) -> p n t", t=384)
        prob_t = arena2[:, 5888:5888 + 2 * 384].rearrange("p (n t) -> p n t", t=384)
        act = arena[:, 0:FT * T].rearrange("p (n t) -> p n t", t=T)
        gate_s = arena[:, FT * T:(FT + 2) * T].rearrange("p (n t) -> p n t", t=T)
        f_u, f_v = d[:, 0, :], d[:, 1, :]
        f_vh = [d[:, 2, :], d[:, 3, :]]
        f_x, f_e, f_z, f_w = (d[:, i, :] for i in (4, 5, 6, 7))
        PU, PL = CONV_W - 1, LRU_W - 1
        u_pad = arena2[:, 0:CT * (PU + T)].rearrange("p (n t) -> p n t", t=PU + T)
        l_pad = arena2[:, 1144:1144 + CT * (PL + T)].rearrange("p (n t) -> p n t", t=PL + T)
        lru_g = arena2[:, 2180:2180 + 1024].rearrange("p (n t) -> p n t", t=T)
        conv = arena2[:, 3204:3204 + 1024].rearrange("p (n t) -> p n t", t=T)
        lru_x = arena2[:, 4228:4228 + 1024].rearrange("p (n t) -> p n t", t=T)
        pt_in = arena2[:, 5252:5252 + 512].rearrange("p (n t) -> p n t", t=T)
        DIAGS = 8
        diag = arena[:, 7168:7168 + DIAGS * P].rearrange("p (n j) -> p n j", j=P)
        cat = arena[:, 0:2048].rearrange("p (n t) -> p n t", t=T)
        g_r, g_i, t_a, t_b, t_c = (arena[:, 2048 + 1024 * i:3072 + 1024 * i].rearrange(
            "p (n t) -> p n t", t=T) for i in range(5))
        blk_w = cb[:, :].rearrange("p (g n j) -> p g n j", g=2, n=CT)
        ple_e = aring[:, 0, :].rearrange("p (n t) -> p n t", t=T)
        E0 = 0
        xe_t = arena2[:, E0:E0 + 1024].rearrange("p (k c) -> p k c", k=KT)
        hot_s = arena2[:, 1024:1280].rearrange("p (a e c) -> p a e c", a=TT, e=2)
        hot_g = arena2[:, 1280:1536].rearrange("p (a e c) -> p a e c", a=TT, e=2)
        hot_gt = arena2[:, 1536:1792]
        silu1 = arena2[:, 1792:2304]
        act_e = arena2[:, 2304:2816]
        act_t = arena2[:, 2816:3328].rearrange("p (f c) -> p f c", f=4)
        y_e = arena2[:, 3328:4352]
        rc = arena2[:, 5764:5764 + N_RC]
        rt = arena2[:, 5992:6656]
        b_route = rt[:, 0:36]
        by_tile = lambda lo, n: rt[:, lo:lo + TT * n].rearrange("p (a e) -> p a e", a=TT)
        r_logit, r_hot_m, r_gate = by_tile(36, 36), by_tile(108, NE), by_tile(172, NE)
        r_rank = by_tile(236, NE + 2)
        r_first, r_work, r_el = by_tile(304, NE), by_tile(368, NE), by_tile(432, NE)
        r_ghot, r_gwork, r_pen = by_tile(496, NG), by_tile(504, NG), by_tile(512, NG)
        r_s = rt[:, 528:576].rearrange("p (n a) -> p n a", a=TT)
        d_flat = d[:].rearrange("p k t -> p (k t)")

        def hf_t(t, kt):
            return d_flat[:, t * D + kt * P:t * D + (kt + 1) * P]

        table_in, hot_in = d_flat[0:BUCKETS, 1024:1040], d_flat[0:BUCKETS, 0:384]
        flip_in = d_flat[:, 384:512]
        added_in, bias_rows = d_flat[0:16, 512:896], d_flat[0:16, 1536:1920]

        psum = ctx.enter_context(nc.psum_tensor("psum", [P, 8, 512], F32))

        def staged(k):
            return w13[:, k // 2, (k % 2) * UNIT:(k % 2 + 1) * UNIT]

        reversed_rows = w13[:].rearrange("p a n -> p (a n)")[:, 10240:14336]

        def view(name, tensor, at, shape, dt=F32R):
            return nc.alloc_sbuf_tensor_at(name, shape, dt, offset=where[tensor] + at)

        w_hi, w_lo = view("w_hi", "w13", 0, [P, 2, UNIT]), view("w_lo", "w13", 16384, [P, 2, UNIT])
        h_hi, h_lo = view("h_hi", "h", 0, [P, KT, T]), view("h_lo", "w13", 32768, [P, KT, T])
        h_lo32 = view("h_lo32", "w13", 32768, [P, KT, T], F32)
        act_hi, act_lo = view("act_hi", "arena", 0, [P, FT, T]), view("act_lo", "w13", 40960, [P, FT, T])

        def half(bank, i):
            return psum[:, bank, i * T:(i + 1) * T]

        def y_ps(n):
            return half(4 + n // 2, n % 2)

        consts_in = sem("consts_in")
        x_in = sem("x_in")
        later_in = sem("later_in")
        staged_in = [sem(f"staged_in{i}") for i in range(STAGED)]
        w_loaded = [sem(f"w_loaded{i}") for i in range(RING)]
        w_hi_ready, w_split = sem("w_hi_ready"), sem("w_split")
        hi_ready, lo_ready = sem("hi_ready"), sem("lo_ready")
        act_split = sem("act_split")
        unit_done = sem("unit_done")
        bank_free = sem("bank_free")
        a_loaded = [sem(f"a_loaded{i}") for i in range(ARING)]
        ada_done = sem("ada_done")
        silu_c = sem("silu_c")
        dve_seq, act_seq, pool_seq = sem("dve_seq"), sem("act_seq"), sem("pool_seq")
        bias_mm, bias_row, bias_out, bias_in = sem("bias_mm"), sem("bias_row"), sem("bias_out"), sem("bias_in")
        flip_mm, flipped = sem("flip_mm"), sem("flipped")
        drv_ready = sem("drv_ready")
        h_whole, act_high = sem("h_whole"), sem("act_high")
        h_ready = sem("h_ready")
        x_ready = sem("x_ready")
        score_mm, score_rd, exp_done = sem("score_mm"), sem("score_rd"), sem("exp_done")
        prob_ready, pt_mm, pt_copied, o_mm, o_copied = (sem(n) for n in (
            "prob_ready", "pt_mm", "pt_copied", "o_mm", "o_copied"))
        fd_mm, fd_in, fd_abs, fd_exp, fd_ready, fd_head = (sem(n) for n in (
            "fd_mm", "fd_in", "fd_abs", "fd_exp", "fd_ready", "fd_head"))
        head_std, o_ready = sem("head_std"), sem("o_ready")
        resid, centred, normed = sem("resid"), sem("centred"), sem("normed")
        sq_ready, sq_used = sem("sq_ready"), sem("sq_used")
        mean_mm = sem("mean_mm")
        std_ready = sem("std_ready")
        gate_done = sem("gate_done")
        pad_zero = sem("pad_zero")
        blk_in, blk_zero = sem("blk_in"), sem("blk_zero")
        ple_in = sem("ple_in")
        conv_done, dve_taps = sem("conv_done"), sem("dve_taps")
        diag_ready, diag_used = sem("diag_ready"), sem("diag_used")
        ada_sum = sem("ada_sum")
        lam_sum, lam_exp, lru_abs = sem("lam_sum"), sem("lam_exp"), sem("lru_abs")
        conv_norm, cat_ready = sem("conv_norm"), sem("cat_ready")
        xr_ready, gates_mm, gates_act, lru_l, lru_t, lru_u, gelu_a, gelu_b = (sem(n) for n in (
            "xr_ready", "gates_mm", "gates_act", "lru_l", "lru_t", "lru_u", "gelu_a", "gelu_b"))
        e_copied = sem("e_copied")
        route_mm, route_d, route_exp, route_m, rank_mm, routed = (sem(n) for n in (
            "route_mm", "route_d", "route_exp", "route_m", "rank_mm", "routed"))
        rc_in = sem("rc_in")
        tok_mm, tok_copied = sem("tok_mm"), sem("tok_copied")
        w13_loaded = [sem("w1_loaded"), sem("w3_loaded")]
        w2_loaded = sem("w2_loaded")
        s_ready, sg_ready, gat0, gat1, gat0_c, gat1_c = (sem(n) for n in (
            "s_ready", "sg_ready", "gat0", "gat1", "gat0_c", "gat1_c"))
        up1, up3, silu_e, act_ready, actt_mm, actt_c = (sem(n) for n in (
            "up1", "up3", "silu_e", "act_ready", "actt_mm", "actt_c"))
        sgt_mm, sgt_c, y0_mm, y1_mm, y0_c, y1_c, scattered = (sem(n) for n in (
            "sgt_mm", "sgt_c", "y0_mm", "y1_mm", "y0_c", "y1_c", "scattered"))
        ple_scaled, next_round = sem("ple_scaled"), sem("next_round")
        out_ready, stored = sem("out_ready"), sem("stored")

        scratch = nc.dram_tensor("bias_rows", (16, 384), F32, kind="Internal").ap()
        rounds_i = sb("rounds_i", [P, 1], I32)

        def V(name, i=0, n=1):
            return vec[:, VEC_AT[name] + i:VEC_AT[name] + i + n]

        def each_unit(eng, n, first, body, peel=0):
            for j in range(peel):
                body(j, None, j)
            whole = (n - peel) // RING
            if whole >= 2:
                with eng.Fori(0, whole) as i:
                    for k in range(RING):
                        body(peel + k, i, peel + k + i * RING)
                at = peel + whole * RING
            else:
                at = peel
            for j in range(at, n):
                body(j, None, j)

        def turn(j, i, base, period):
            t = (base + j) // period
            return t if i is None else t + i * (RING // period)

        PLE, PG = UNIT_AT["ple"], UNIT_AT["pg"]

        def split_no(k):
            return k if k < PLE else k - 1

        def unit_of(n):
            return n if n < PLE else n + 1

        def split_waits(eng, k, i):
            n = split_no(k)
            if n >= 2:
                done = unit_of(n - 2) + 1
                eng.wait_ge(unit_done, done if i is None else i * RING + done)
            return n

        def convolve(eng, nce, tiles, taps, between):
            for t in range(CONV_W):
                between(t)
                for k, j in enumerate(tiles):
                    if t:
                        eng.wait_ge(taps, 2 * (t - 1) + k + 1)
                        ins = nce.scalar_tensor_tensor(conv[:, j, :], u_pad[:, j, t:t + T],
                                                       V("conv_w", j * CONV_W + t), conv[:, j, :], ALU.mult, ALU.add)
                    else:
                        ins = nce.tensor_scalar(conv[:, j, :], u_pad[:, j, 0:T], V("conv_w", j * CONV_W),
                                                V("conv_b", j), ALU.mult, ALU.add)
                    ins.then_inc(conv_done if t == CONV_W - 1 else taps, 1)

        block = ctx.enter_context(nc.Block())

        @block.sync
        def _(sp):
            def small_loads(loads, signal):
                for dst, src in loads:
                    sp.dma_start(dst, src).then_inc(signal, 16)

            small_loads(((table_in, a["table"]), (hot_in, a["hot"]), (added_in, a["added"]), (flip_in, a["flip"]),
                         (vec[:], a["vecs"]), (cst[:], a["consts"])), consts_in)

            def load_unit(k):
                if k >= RING:
                    if k - RING == PLE:
                        sp.wait_ge(unit_done, PLE + 1)
                    else:
                        sp.wait_ge(w_split, split_no(k - RING) + 1)
                sp.dma_start(wring[:, k % RING, :], a["units"][k]).then_inc(w_loaded[k % RING], 16)

            def load_w13(e2, which):
                for s in range(2):
                    sp.dma_start(w13[:, 2 * which + s, :], a["w3" if which else "w1"][e2, s]).then_inc(
                        w13_loaded[which], 16)

            def load_w2(e2):
                for s in range(2):
                    sp.dma_start(arena[:, 4096 * s:4096 * (s + 1)], a["w2"][e2, s]).then_inc(w2_loaded, 16)

            for k in range(STAGED):
                sp.dma_start(staged(k), a["ada"][k]).then_inc(staged_in[k], 16)
            sp.dma_start(x[:], a["x_t"]).then_inc(x_in, 16)
            for k in range(RING):
                load_unit(k)
            small_loads(((lam_in[:], a["lam_in"]), (bias[:, 16, :], a["causal"]), (w_forget[:], a["w_forget"]),
                         (w_route[:], a["w_route"]), (fsmall[0:8, 0:1], a["forget_b"]),
                         (fsmall[:, 1:9], a["head_rows"])), later_in)

            def unit_groups(lo, hi):
                with sp.Fori(lo, hi) as i:
                    for k in range(RING):
                        sp.wait_ge(w_split, i * RING + (k - RING + 1))
                        sp.dma_start(wring[:, k, :], a["units"][i * RING + k]).then_inc(w_loaded[k], 16)

            groups = PLE // RING
            unit_groups(1, groups)
            for k in range(RING * groups, N_UNITS):
                load_unit(k)
            sp.wait_ge(unit_done, UNIT_AT["wout"] + 4)
            load_w13(0, 0)
            load_w13(0, 1)
            load_w2(0)

            def load_pair(e2, n):
                sp.wait_ge(up1, n)
                load_w13(e2, 0)
                sp.wait_ge(up3, n)
                load_w13(e2, 1)
                sp.wait_ge(y1_mm, n)
                load_w2(e2)

            with sp.Fori(1, PAIRS) as p:
                load_pair(p, p)
            sp.wait_ge(routed, 2)
            rounds = sp.value_load(rounds_i[0:1, 0:1], min_val=1, max_val=4)
            with sp.If(rounds > 1):
                with sp.Fori(1, rounds) as r:
                    with sp.Fori(0, PAIRS) as p:
                        load_pair(p, r * PAIRS + p)
            sp.wait_ge(out_ready, 8)
            sp.dma_start(out, d[:]).then_inc(stored, 16)
            sp.wait_ge(stored, 16)

        @block.gpsimd
        def _(pool):
            seq = [0]

            def link(ins):
                seq[0] += 1
                ins.then_inc(pool_seq, 1)
                pool.wait_ge(pool_seq, seq[0])

            def ada_piece(k):
                if k >= STAGED + ARING:
                    pool.wait_ge(ada_done, k - ARING + 1)
                pool.dma_start(aring[:, k % ARING, :], a["ada"][k]).then_inc(a_loaded[k % ARING], 16)

            def pieces(lo, hi):
                for k in range(lo, hi):
                    ada_piece(k)

            pool.wait_ge(staged_in[STAGED - 1], 16)
            pieces(8, 10)
            pool.wait_ge(hi_ready, 8)
            pool.wait_ge(lo_ready, 8)
            nc.gpsimd.tensor_scalar(x[:], x[:], ALPHA, None, ALU.mult).then_inc(x_ready, 1)
            pieces(10, 22)

            def layer_norm_x(q):
                pool.wait_ge(drv_ready, q + 2)
                for kt in range(KT):
                    pool.wait_ge(normed, 8 * q + kt + 1)
                    nc.gpsimd.tensor_scalar(x[:, kt, :], d[:, kt, :], drv[:, q, 3, kt:kt + 1],
                                            drv[:, q, 4, kt:kt + 1], ALU.mult, ALU.add).then_inc(x_ready, 1)

            layer_norm_x(0)
            with pool.Fori(0, 11) as i:
                for s in range(ARING):
                    pool.wait_ge(ada_done, i * 2 + (22 + s - ARING + 1))
                    pool.dma_start(aring[:, s, :], a["ada"][i * 2 + (22 + s)]).then_inc(a_loaded[s], 16)
            layer_norm_x(1)
            pieces(44, 48)
            layer_norm_x(2)
            layer_norm_x(3)

            pool.wait_ge(ada_done, ADA_PIECES)
            link(nc.gpsimd.memset(cb[:], 0.0))
            for g, name in enumerate(("w_r", "w_i")):
                for s in range(2):
                    pool.dma_start(blk_w[64 * s:64 * s + 64, g, :, 64 * s:64 * s + 64],
                                   a[name][64 * s:64 * s + 64]).then_inc(blk_in, 16)
            pool.wait_ge(o_copied, 28)
            pool.dma_start(pt_in, a["p_t"]).then_inc(ple_in, 16)
            nc.gpsimd.memset(u_pad[:, :, 0:PU], 0.0).then_inc(pad_zero, 1)
            nc.gpsimd.memset(l_pad[:, :, 0:PL], 0.0).then_inc(pad_zero, 1)

            for n in range(2 * CONV_W):
                if n >= DIAGS:
                    pool.wait_ge(diag_used, n - DIAGS + 1)
                nc.gpsimd.tensor_scalar(diag[:, n % DIAGS, :], ident, V("conv_w", 2 * CONV_W + n), None,
                                        ALU.mult).then_inc(diag_ready, 1)
            pool.dma_start(rc, a["router_consts"]).then_inc(rc_in, 16)
            pool.dma_start(b_route, a["b_route"]).then_inc(rc_in, 16)

        @block.tensor
        def _(pe):
            def unit(base, j, i):
                slot = (base + j) % RING
                pe.wait_ge(w_loaded[slot], (turn(j, i, base, RING) + 1) * 16)
                return slot

            def bank(stage, j, i):
                n = BANK_AT[stage] + j
                if n >= 2:
                    pe.wait_ge(bank_free, n - 1 if i is None else i * RING + (n - 1))
                return n % 2

            def split_unit(base, j, i):
                n = split_no(base + j) + 1
                pe.wait_ge(w_split, n if i is None else i * RING + n)
                return split_no(base + j) % 2

            def high(version, kt, first):
                if first:
                    pe.wait_ge(hi_ready, 8 * version + kt + 1)

            def low(version, kt, first):
                if first:
                    pe.wait_ge(lo_ready, 8 * version + kt + 1)

            def to_features(stage, n_units, version):
                base = UNIT_AT[stage]

                def body(j, i, idx):
                    slot, b = split_unit(base, j, i), bank(stage, j, i)
                    w = lambda part, kt, s: part[:, slot, kt * 256 + s * P:kt * 256 + (s + 1) * P]
                    for s in range(2):
                        for kt in range(KT):
                            high(version, kt, j == 0 and s == 0)
                            nc.tensor.matmul(half(b, s), w(w_hi, kt, s), h_hi[:, kt, :], start=kt == 0 and s == 0,
                                             stop=False, skip_group_check=True)
                            nc.tensor.matmul(half(b, s), w(w_lo, kt, s), h_hi[:, kt, :], start=False, stop=False,
                                             skip_group_check=True)
                    for s in range(2):
                        for kt in range(KT):
                            low(version, kt, j == 0 and s == 0)
                            last = nc.tensor.matmul(half(b, s), w(w_hi, kt, s), h_lo[:, kt, :], start=False,
                                                    stop=kt == KT - 1, skip_group_check=True)
                    last.then_inc(unit_done, 1)

                each_unit(pe, n_units, base, body)

            def to_tokens(stage, n_units, version):
                base = UNIT_AT[stage]

                def body(j, i, idx):
                    slot, b = split_unit(base, j, i), bank(stage, j, i)
                    w = lambda part, kt: part[:, slot, kt * 256:(kt + 1) * 256]
                    tok = lambda part, kt, t: part[:, kt, t * P:(t + 1) * P]
                    for t in range(TT):
                        for kt in range(KT):
                            high(version, kt, j == 0 and t == 0)
                            nc.tensor.matmul(half(b, t), tok(h_hi, kt, t), w(w_hi, kt), start=kt == 0 and t == 0,
                                             stop=False, skip_group_check=True)
                            nc.tensor.matmul(half(b, t), tok(h_hi, kt, t), w(w_lo, kt), start=False, stop=False,
                                             skip_group_check=True)
                    for t in range(TT):
                        for kt in range(KT):
                            low(version, kt, j == 0 and t == 0)
                            last = nc.tensor.matmul(half(b, t), tok(h_lo, kt, t), w(w_hi, kt), start=False,
                                                    stop=kt == KT - 1, skip_group_check=True)
                    last.then_inc(unit_done, 1)

                each_unit(pe, n_units, base, body)

            def to_y(stage, version):
                base = UNIT_AT[stage]
                for j in range(4):
                    slot = split_unit(base, j, None)
                    w = lambda part, kt, s: part[:, slot, kt * 256 + s * P:kt * 256 + (s + 1) * P]
                    for s in range(2):
                        for kt in range(KT):
                            high(version, kt, j == 0 and s == 0)
                            nc.tensor.matmul(y_ps(2 * j + s), w(w_hi, kt, s), h_hi[:, kt, :],
                                             start=kt == 0 and s == 0, stop=False, skip_group_check=True)
                            nc.tensor.matmul(y_ps(2 * j + s), w(w_lo, kt, s), h_hi[:, kt, :], start=False,
                                             stop=False, skip_group_check=True)
                    for s in range(2):
                        for kt in range(KT):
                            low(version, kt, j == 0 and s == 0)
                            last = nc.tensor.matmul(y_ps(2 * j + s), w(w_hi, kt, s), h_lo[:, kt, :], start=False,
                                                    stop=kt == KT - 1, skip_group_check=True)
                    last.then_inc(unit_done, 1)

            def ffn_out(stage, layer):
                base = UNIT_AT[stage]

                def body(j, i, idx):
                    slot = split_unit(base, j, i)
                    pe.wait_ge(act_split, FT * layer + 2 * idx + 2)
                    for s in range(2):
                        tile = lambda part: part[:, bass.ds(idx * 2 + s, 1), :] if i is not None else part[:, 2 * j + s, :]
                        for n in range(KT):
                            w = lambda part: part[:, slot, s * D + n * P:s * D + (n + 1) * P]
                            for part_w, part_a in ((w_hi, act_hi), (w_lo, act_hi), (w_hi, act_lo)):
                                last = nc.tensor.matmul(
                                    y_ps(n), w(part_w), tile(part_a),
                                    start=j == 0 and s == 0 and n % 2 == 0 and part_w is w_hi and part_a is act_hi,
                                    stop=i is None and j == FT // 2 - 1 and s == 1 and part_a is act_lo,
                                    skip_group_check=True)
                    last.then_inc(unit_done, 1)

                each_unit(pe, FT // 2, base, body, peel=1)

            def sum_squares(norm, out_ap, n):
                base = SQ_AT[norm]
                for kt in range(n):
                    pe.wait_ge(sq_ready, base + kt + 1)
                    nc.tensor.matmul(out_ap, ones, sq[:, kt % 2, :], start=kt == 0, stop=kt == n - 1).then_inc(sq_used, 1)

            def layer_norm(q):
                for kt in range(KT):
                    pe.wait_ge(resid, 8 * q + kt + 1)
                    last = nc.tensor.matmul(half(2, 0), ones, d[:, kt, :], start=kt == 0, stop=kt == KT - 1)
                last.then_inc(mean_mm, 1)
                sum_squares(f"ln{q}", half(3, 0), KT)

            def attention(layer):
                items = [(0, [2 * i, 2 * i + 1]) for i in range(4)] if layer == 0 else [(1, [i]) for i in range(8)]
                items += [(1, [8 + i]) for i in range(8)]
                item0 = 12 * layer
                map0 = MAPS * layer

                def scores(maps):
                    for m in maps:
                        n = map0 + m
                        if m >= 4:
                            pe.wait_ge(score_rd, n - 3)
                        qt, at = (m // 8) * 8 + (m % 8) // 2, (m % 2) * DH
                        q, k = qk[at:at + DH, qt, :], qk[at:at + DH, qt + 4, :]
                        b = m % 4
                        forget = layer == 1 and m >= 8
                        if forget:
                            pe.wait_ge(fd_head, m - 8 + 1)
                        for dst, tok, keys in ((psum[:, b, 0:256], slice(P, T), T), (psum[:, b, 256:384], slice(0, P), P)):
                            last = nc.tensor.matmul(dst, q[:, tok], k[:, 0:keys], start=True, stop=not forget)
                            if forget:
                                last = nc.tensor.matmul(dst, f_u[at:at + DH, tok], f_vh[m % 2][at:at + DH, 0:keys],
                                                        start=False, stop=True)
                        last.then_inc(score_mm, 1)

                def transposes(i):
                    n = item0 + i
                    s = score[:, items[i][1][0] % 4, :]
                    pe.wait_ge(prob_ready, n + 1)
                    if i >= 2:
                        pe.wait_ge(pt_copied, n - 1)
                    b = 4 + i % 2
                    nc.tensor.transpose(psum[:, b, 0:P], s[:, 256:384], ident)
                    nc.tensor.transpose(psum[:, b, P:2 * P], s[:, 0:P], ident)
                    nc.tensor.transpose(psum[:, b, 2 * P:3 * P], s[:, P:2 * P], ident).then_inc(pt_mm, 1)

                def outputs(i):
                    single, maps = items[i]
                    n = item0 + i
                    pe.wait_ge(pt_copied, n + 1)
                    if i >= 2:
                        pe.wait_ge(o_copied, n - 1)
                    b = 6 + i % 2
                    lo, width, at = (maps[0] * DH, DH, (maps[0] % 2) * DH) if single else (i * P, P, 0)
                    nc.tensor.matmul(psum[at:at + width, b, 0:T], val[:, 0, lo:lo + width], prob_t[:, i % 2, 0:T],
                                     start=True, stop=False)
                    nc.tensor.matmul(psum[at:at + width, b, P:T], val[:, 1, lo:lo + width], prob_t[:, i % 2, T:T + P],
                                     start=False, stop=True).then_inc(o_mm, 1)

                scores(items[0][1])
                scores(items[1][1])
                for i in range(len(items)):
                    if i + 2 < len(items):
                        scores(items[i + 2][1])
                    transposes(i)
                    if i:
                        outputs(i - 1)
                outputs(len(items) - 1)

            pe.wait_ge(consts_in, CONSTS)
            nc.tensor.matmul(psum[0:16, 2, 0:384], table_in, hot_in, start=True, stop=True).then_inc(bias_mm, 1)

            for layer in range(DEPTH):
                version = 3 * layer
                to_tokens(f"v{layer}", 4, version)
                to_features(f"qk{layer}", 8, version)
                if layer == 1:
                    pe.wait_ge(later_in, LATER)
                    for part in (h_hi, h_lo):
                        for kt in range(KT):
                            last = nc.tensor.matmul(psum[0:8, 3, 0:T], w_forget[:, kt, :], part[:, kt, :].bitcast(F32),
                                                    start=kt == 0 and part is h_hi, stop=kt == KT - 1 and part is h_lo)
                    last.then_inc(fd_mm, 1)
                    pe.wait_ge(fd_in, 1)
                else:
                    pe.wait_ge(bias_in, 16)
                    for n in range(2):
                        if n:
                            pe.wait_ge(flipped, 1)
                        for b in range(4):
                            last = nc.tensor.matmul(psum[:, 4 + b, :], flip_in, reversed_rows[:, (4 * n + b) * 512:(4 * n + b + 1) * 512],
                                                    start=True, stop=True)
                        last.then_inc(flip_mm, 1)
                pe.wait_ge(bank_free, BANK_AT[f"qk{layer}"] + 8)
                attention(layer)
                if layer == 0:
                    base = SQ_AT["heads"]
                    for i in range(4):
                        pe.wait_ge(sq_ready, base + i + 1)
                        nc.tensor.matmul(half(2 + i // 2, i % 2), ones, sq[:, i % 2, :], start=True,
                                         stop=True).then_inc(sq_used, 1)
                to_y(f"wo{layer}", version + 1)
                layer_norm(2 * layer)
                to_features(f"fi{layer}", 22, version + 2)
                ffn_out(f"fo{layer}", layer)
                layer_norm(2 * layer + 1)

            sum_squares("mix", half(3, 0), KT)
            to_features("z", 8, 6)
            slot = unit(UNIT_AT["ple"], 0, None)
            pe.wait_ge(ple_in, 16)
            for n in range(KT):
                for kt in range(2):
                    last = nc.tensor.matmul(y_ps(n), wring[:, slot, kt * D + n * P:kt * D + (n + 1) * P],
                                            pt_in[:, kt, :], start=kt == 0, stop=kt == 1)
            last.then_inc(unit_done, 1)

            def convolve_tile(k):
                pe.wait_ge(bank_free, BANK_AT["z"] + 8)
                for t in range(CONV_W):
                    pe.wait_ge(diag_ready, CONV_W * k + t + 1)
                    last = nc.tensor.matmul(half(k, 0), diag[:, (CONV_W * k + t) % DIAGS, :], u_pad[:, 2 + k, t:t + T],
                                            start=t == 0, stop=t == CONV_W - 1)
                    last.then_inc(diag_used, 1)

            convolve_tile(0)
            sum_squares("ple_proj", half(3, 0), KT)
            pe.wait_ge(blk_in, 64)
            pe.wait_ge(bank_free, BANK_AT["z"] + 8)
            pe.wait_ge(e_copied, 1)
            for g in range(2):
                for j in range(CT):
                    if g == 0:
                        pe.wait_ge(xr_ready, j + 1)
                    last = nc.tensor.matmul(half(4 + 2 * g + j // 2, j % 2), blk_w[:, g, j, :], lru_x[:, j, :],
                                            start=True, stop=True)
                last.then_inc(gates_mm, 1)
            convolve_tile(1)
            pe.wait_ge(conv_done, 4)
            for j in range(CT):
                last = nc.tensor.matmul(half(2, 0), ones, conv[:, j, :], start=j == 0, stop=j == CT - 1)
            last.then_inc(mean_mm, 1)
            sum_squares("conv", half(3, 0), CT)

            to_y("wout", 7)
            sum_squares("ffn", half(3, 0), KT)
            for t in range(TT):
                for kt in range(KT):
                    if t == 0:
                        pe.wait_ge(h_ready, kt + 1)
                    last = nc.tensor.matmul(psum[:, 0, t * 64:t * 64 + 36], h[:, kt, t * P:(t + 1) * P],
                                            w_route[:, kt, :], start=kt == 0, stop=kt == KT - 1)
            last.then_inc(route_mm, 1)
            for b in range(4):
                t, lo = b // 2, (b % 2) * 4
                for k in range(4):
                    last = nc.tensor.transpose(psum[:, 4 + b, k * P:(k + 1) * P],
                                               h[:, lo + k, t * P:(t + 1) * P], ident)
                last.then_inc(tok_mm, 1)
            pe.wait_ge(route_m, 1)
            pe.wait_ge(rc_in, 32)
            hot_m = r_hot_m
            tri = rc[:, RC_TRI:RC_TRI + P]
            nc.tensor.matmul(psum[:, 1, 0:NE], tri, hot_m[:, 0, :], start=True, stop=True)
            nc.tensor.matmul(psum[:, 1, 64:64 + NE], tri, hot_m[:, 1, :], start=True, stop=False)
            nc.tensor.matmul(psum[:, 1, 64:64 + NE], ones, hot_m[:, 0, :], start=False, stop=True)
            nc.tensor.matmul(psum[:, 1, 128:128 + NE], ones, hot_m[:, 0, :], start=True, stop=False)
            nc.tensor.matmul(psum[:, 1, 128:128 + NE], ones, hot_m[:, 1, :], start=False, stop=True).then_inc(rank_mm, 1)

            G, TR = 2, 3

            def gather(n_half, bank_no):
                for k in range(4):
                    kt = 4 * n_half + k
                    for t in range(TT):
                        last = nc.tensor.matmul(psum[:, bank_no, k * P:(k + 1) * P], hf_t(t, kt),
                                                hot_s[:, t, :, :], start=t == 0, stop=t == TT - 1)
                return last

            def scatter(start, stop):
                for n in range(KT):
                    last = nc.tensor.matmul(y_ps(n), y_e[:, n * P:(n + 1) * P], hot_gt,
                                            start=start and n % 2 == 0, stop=stop, skip_group_check=True)
                return last

            pe.wait_ge(routed, 2)
            rounds = pe.value_load(rounds_i[0:1, 0:1], min_val=1, max_val=4)
            pe.wait_ge(tok_copied, 4)
            pe.wait_ge(s_ready, 1)
            gather(0, G).then_inc(gat0, 1)
            gather(1, TR).then_inc(gat1, 1)
            pe.wait_ge(y1_c, 1)
            pe.wait_ge(sgt_c, 1)
            scatter(True, False)
            with pe.Fori(0, rounds) as r:
                with pe.Fori(0, PAIRS) as p:
                    n = r * PAIRS + p
                    pe.wait_ge(gat0_c, n + 1)
                    pe.wait_ge(gat1_c, n + 1)
                    pe.wait_ge(w13_loaded[0], n * 32 + 32)
                    pe.wait_ge(y0_c, n + 1)
                    for w in range(2):
                        if w:
                            pe.wait_ge(w13_loaded[1], n * 32 + 32)
                            pe.wait_ge(y1_c, n + 1)
                        for kt in range(KT):
                            for s in range(2):
                                last = nc.tensor.matmul(psum[s * CAP:(s + 1) * CAP, w, :],
                                                        xe_t[:, kt, s * CAP:(s + 1) * CAP],
                                                        w13[:, 2 * w + s, kt * FE:(kt + 1) * FE],
                                                        start=kt == 0, stop=kt == KT - 1)
                        last.then_inc((up1, up3)[w], 1)
                    pe.wait_ge(sgt_c, n + 1)
                    scatter(False, False).then_inc(scattered, 1)
                    pe.wait_ge(act_ready, n + 1)
                    for f in range(4):
                        last = nc.tensor.transpose(psum[:, TR, f * P:(f + 1) * P], act_e[:, f * P:(f + 1) * P], ident)
                    last.then_inc(actt_mm, 1)
                    pe.wait_ge(s_ready, n + 2)
                    gather(0, G).then_inc(gat0, 1)
                    pe.wait_ge(actt_c, n + 1)
                    gather(1, TR).then_inc(gat1, 1)
                    pe.wait_ge(sg_ready, n + 1)
                    pe.wait_ge(gat0_c, n + 2)
                    for t in range(TT):
                        last = nc.tensor.transpose(psum[:, G, t * P:(t + 1) * P],
                                                   hot_g[:, t, :, :].rearrange("p e c -> p (e c)"), ident)
                    last.then_inc(sgt_mm, 1)
                    pe.wait_ge(w2_loaded, n * 32 + 32)
                    for c in range(2):
                        for f in range(4):
                            for s in range(2):
                                last = nc.tensor.matmul(psum[s * CAP:(s + 1) * CAP, c, :],
                                                        act_t[:, f, s * CAP:(s + 1) * CAP],
                                                        arena[:, s * 4096 + f * D + c * 512:s * 4096 + f * D + c * 512 + 512],
                                                        start=f == 0, stop=f == 3)
                        last.then_inc((y0_mm, y1_mm)[c], 1)
            n_all = rounds * PAIRS
            pe.wait_ge(y0_c, n_all + 1)
            pe.wait_ge(y1_c, n_all + 1)
            pe.wait_ge(sgt_c, n_all + 1)
            scatter(False, True).then_inc(scattered, 1)

            sum_squares("gate", half(3, 0), KT)
            pe.wait_ge(x_ready, 49)
            for j in range(4):
                slot = unit(PG, j, None)
                for s in range(2):
                    for kt in range(KT):
                        if j == 0 and s == 0:
                            pe.wait_ge(h_ready, 8 + kt + 1)
                        last = nc.tensor.matmul(y_ps(2 * j + s), wring[:, slot, kt * 256 + s * P:kt * 256 + (s + 1) * P],
                                                h[:, kt, :], start=kt == 0, stop=kt == KT - 1)
                last.then_inc(unit_done, 1)
            sum_squares("final", half(3, 0), KT)

        @block.scalar
        def _(act_e_):
            act = act_e_
            seq = [0]
            f_act = ctx_act = None
            Id, Cp = ACT.Identity, ACT.Copy

            def A(out_ap, in_ap, func, **kw):
                return nc.scalar.activation(out_ap, in_ap, func, **kw)

            def square(norm, kt, src):
                g = SQ_AT[norm] + kt
                if g >= 2:
                    act.wait_ge(sq_used, g - 1)
                A(sq[:, kt % 2, :], src, ACT.Square).then_inc(sq_ready, 1)

            def deviation(norm, n, features, eps):
                act.wait_ge(sq_used, SQ_AT[norm] + n)
                A(rstd[:], half(3, 0), ACT.Sqrt, scale=1.0 / features, bias=eps).then_inc(std_ready, 1)

            eps_ln, eps_rms = small[:, 60:61], small[:, 61:62]

            act.dma_start(cb[:], a["c_rows"]).then_inc(silu_c, 16)
            act.wait_ge(silu_c, 16)
            A(cb[:], cb[:], ACT.Silu).then_inc(silu_c, 1)
            act.wait_ge(bias_row, 1)
            act.dma_start(scratch, bias_rows).then_inc(bias_out, 16)
            act.wait_ge(drv_ready, 1)
            act.wait_ge(x_in, 16)
            for kt in range(KT):
                A(h_hi[:, kt, :], x[:, kt, :], Id, scale=small[:, kt:kt + 1], bias=ada[:, 0, kt:kt + 1]).then_inc(hi_ready, 1)
            for k in range(2):
                act.wait_ge(w_loaded[k], 16)
                A(w_hi[:, k, :], wring[:, k, :], Cp).then_inc(w_hi_ready, 1)
            act.wait_ge(bias_out, 16)
            toeplitz = bass.AP(scratch.tensor, 0, [[1, P], [384, 16], [1, 256]])
            act.dma_start(reversed_rows.rearrange("p (n t) -> p n t", t=256), toeplitz).then_inc(bias_in, 16)
            act.wait_ge(lam_sum, 2)
            A(small[:, 12:14], small[:, 10:12], ACT.Exp).then_inc(lam_exp, 1)

            def split(k, i=None):
                if k == PLE or k >= PG:
                    return
                n = split_waits(act, k, i)
                act.wait_ge(w_loaded[k % RING], ((k // RING + 1) if i is None else i + (k // RING + 1)) * 16)
                A(w_hi[:, n % 2, :], wring[:, k % RING, :], Cp).then_inc(w_hi_ready, 1)

            def high_parts(src, wait):
                for kt in range(KT):
                    wait(kt)
                    A(h_hi[:, kt, :], src[:, kt, :], Cp).then_inc(hi_ready, 1)

            def attention(layer):
                items = [(0, [2 * i, 2 * i + 1]) for i in range(4)] if layer == 0 else [(1, [i]) for i in range(8)]
                items += [(1, [8 + i]) for i in range(8)]

                def exps(maps):
                    for m in maps:
                        act.wait_ge(score_rd, MAPS * layer + m + 1)
                        s = score[:, m % 4, :]
                        A(s[:, 0:256], s[:, 0:256], ACT.Exp, scale=-1.0, bias=mins[:, m, 0:1], accum_out=den[:, m, 0:1])
                        A(s[:, 256:384], s[:, 256:384], ACT.Exp, scale=-1.0, bias=mins[:, m, 1:2],
                          accum_out=den[:, m, 1:2]).then_inc(exp_done, 1)

                exps(items[0][1])
                for i in range(len(items)):
                    n = 12 * layer + i
                    if i + 1 < len(items):
                        exps(items[i + 1][1])
                    act.wait_ge(pt_mm, n + 1)
                    if i >= 2:
                        act.wait_ge(o_mm, n - 1)
                    A(prob_t[:, i % 2, :], psum[:, 4 + i % 2, 0:384], Cp).then_inc(pt_copied, 1)

            def layer_norm(q):
                for kt in range(KT):
                    act.wait_ge(centred, 8 * q + kt + 1)
                    square(f"ln{q}", kt, d[:, kt, :])
                deviation(f"ln{q}", KT, D, eps_ln)
                if q < 3:
                    for kt in range(KT):
                        act.wait_ge(normed, 8 * q + kt + 1)
                        A(h_hi[:, kt, :], d[:, kt, :], Id, scale=drv[:, q, 1, kt:kt + 1],
                          bias=drv[:, q, 2, kt:kt + 1]).then_inc(hi_ready, 1)

            for layer in range(DEPTH):
                for j in range(4):
                    act.wait_ge(unit_done, UNIT_AT[f"v{layer}"] + j + 1)
                    A(val[:, :, j * 256:(j + 1) * 256], psum[:, j % 2, :].rearrange("p (a n) -> p a n", a=TT),
                      Cp).then_inc(bank_free, 1)
                    split(UNIT_AT[f"v{layer}"] + j + 2)

                def take_qk(j, i, idx, layer=layer):
                    act.wait_ge(unit_done, UNIT_AT[f"qk{layer}"] + idx + 1)
                    dst = (arena[:, bass.ds(idx * 512, 512)] if i is not None else arena[:, j * 512:(j + 1) * 512])
                    A(dst, psum[:, j % 2, :], Cp, scale=-DH ** -0.5 if j % 4 < 2 else 1.0).then_inc(bank_free, 1)
                    split(UNIT_AT[f"qk{layer}"] + j + 2, i)
                each_unit(act, 8, 0, take_qk)
                if layer == 1:
                    act.wait_ge(fd_mm, 1)
                    act.wait_ge(later_in, LATER)
                    act.wait_ge(x_ready, 17)
                    A(f_x[0:8, :], psum[0:8, 3, 0:T], Id, bias=fsmall[0:8, 0:1]).then_inc(fd_in, 1)
                    act.wait_ge(fd_in, 1)
                    A(f_e[0:8, :], f_x[0:8, :], ACT.Abs).then_inc(fd_abs, 1)
                    act.wait_ge(fd_abs, 1)
                    A(f_e[0:8, :], f_e[0:8, :], ACT.Exp, scale=-1.0).then_inc(fd_exp, 1)
                else:
                    for n in range(2):
                        act.wait_ge(flip_mm, n + 1)
                        A(arena2[:, n * 2048:(n + 1) * 2048], psum[:, 4:8, :].rearrange("p b n -> p (b n)"), Cp).then_inc(flipped, 1)
                attention(layer)
                if layer == 0:
                    for i in range(4):
                        act.wait_ge(o_copied, i + 1)
                        square("heads", i, o[:, i, :])
                    act.wait_ge(sq_used, 4)
                    A(d_flat[:, 0:1024], psum[:, 2:4, :].rearrange("p b n -> p (b n)"), ACT.Sqrt, scale=1.0 / P,
                      bias=eps_ln).then_inc(std_ready, 1)

                def wait_o(kt, layer=layer):
                    if kt == 0:
                        act.wait_ge(o_copied, 28 if layer else 12)
                    if layer == 0 and kt < 4:
                        act.wait_ge(o_ready, kt + 1)
                high_parts(o, wait_o)
                for j in range(4):
                    split(UNIT_AT[f"wo{layer}"] + j + 2)
                layer_norm(2 * layer)

                def gate(j, i, idx, layer=layer):
                    n = BANK_AT[f"fi{layer}"] + j
                    act.wait_ge(unit_done, UNIT_AT[f"fi{layer}"] + idx + 1)
                    if i is not None or j >= 2:
                        act.wait_ge(act_split, FT * layer + idx - 1)
                    A(gate_s[:, j % 2, :], half(j % 2, 0), ACT.Silu).then_inc(gate_done, 1)
                    split(UNIT_AT[f"fi{layer}"] + j + 2, i)
                each_unit(act, 22, 0, gate, peel=2)
                each_unit(act, FT // 2, 0, lambda j, i, idx, layer=layer: split(UNIT_AT[f"fo{layer}"] + j + 2, i), peel=1)
                layer_norm(2 * layer + 1)

            for kt in range(KT):
                act.wait_ge(x_ready, 25 + kt + 1)
                square("mix", kt, x[:, kt, :])
            deviation("mix", KT, D, eps_rms)
            high_parts(h_lo32, lambda kt: act.wait_ge(h_whole, kt + 1))
            A(small[:, 28:32], V("lam", 0, 4), ACT.Abs).then_inc(lru_abs, 1)
            act.wait_ge(lru_abs, 1)
            A(small[:, 28:32], small[:, 28:32], ACT.Exp, scale=-1.0).then_inc(lru_abs, 1)
            act.wait_ge(pad_zero, 2)
            for j in range(8):
                act.wait_ge(unit_done, UNIT_AT["z"] + j + 1)
                if j < 4:
                    if j >= 2:
                        act.wait_ge(bank_free, BANK_AT["z"] + j - 1)
                    A(gate_s[:, j % 2, :], half(j % 2, 1), ACT.Sigmoid).then_inc(gate_done, 1)
                else:
                    act.wait_ge(bank_free, BANK_AT["z"] + 4)
                    A(l_pad[:, j - 4, PL:PL + T], half(j % 2, 0), Cp)
                    A(lru_g[:, j - 4, :], half(j % 2, 1), ACT.Gelu_apprx_tanh).then_inc(bank_free, 1)
                split(UNIT_AT["z"] + j + 2)
            split(UNIT_AT["wout"] + 1)
            act.wait_ge(unit_done, UNIT_AT["ple"] + 1)
            act.wait_ge(ada_done, ADA_PIECES)
            A(aring[:, 0, :], psum[:, 4:8, :].rearrange("p b n -> p (b n)"), Cp).then_inc(e_copied, 1)
            act.wait_ge(e_copied, 1)
            for kt in range(KT):
                square("ple_proj", kt, ple_e[:, kt, :])
            deviation("ple_proj", KT, D, eps_rms)
            for g in range(2):
                act.wait_ge(gates_mm, g + 1)
                for j in range(CT):
                    ins = A((g_r, g_i)[g][:, j, :], half(4 + 2 * g + j // 2, j % 2), ACT.Sigmoid,
                            bias=V("b_i" if g else "b_r", j))
                ins.then_inc(gates_act, 1)
            for k in range(2):
                act.wait_ge(diag_used, CONV_W * (k + 1))
                A(conv[:, 2 + k, :], half(k, 0), Id, bias=V("conv_b", 2 + k)).then_inc(conv_done, 1)
            act.wait_ge(lru_l, 1)
            A(t_b, t_a, ACT.Tanh).then_inc(lru_t, 1)
            A(g_r, t_a, ACT.Exp, scale=-1.0).then_inc(lru_t, 1)
            act.wait_ge(lru_u, 1)
            A(t_a, t_b, ACT.Sqrt, scale=2.0).then_inc(lru_t, 1)
            for j in range(CT):
                act.wait_ge(conv_norm, j + 1)
                square("conv", j, conv[:, j, :])
            deviation("conv", CT, 512, eps_rms)
            for j in range(CT):
                act.wait_ge(conv_norm, 4 + j + 1)
                A(cat[:, j, :], conv[:, j, :], ACT.Silu, scale=V("conv_ln_g", j), bias=V("conv_ln_b", j)).then_inc(cat_ready, 1)

            def wait_cat(kt):
                if kt < CT:
                    act.wait_ge(cat_ready, kt + 1)
                else:
                    act.wait_ge(lru_u, 8)
            high_parts(cat, wait_cat)
            split(UNIT_AT["wout"] + 2)
            split(UNIT_AT["wout"] + 3)
            for kt in range(KT):
                act.wait_ge(x_ready, 33 + kt + 1)
                square("ffn", kt, x[:, kt, :])
            deviation("ffn", KT, D, eps_rms)
            for b in range(2):
                act.wait_ge(tok_mm, 2 * b + 2)
                A(d_flat[:, b * 1024:(b + 1) * 1024], psum[:, 4 + 2 * b:6 + 2 * b, :].rearrange("p b n -> p (b n)"),
                  Cp).then_inc(tok_copied, 2)
            act.wait_ge(route_d, 1)
            A(r_gwork, r_gwork, ACT.Exp).then_inc(route_exp, 1)
            act.wait_ge(route_d, 2)
            A(r_s[:, 6, :], r_s[:, 5, :], ACT.Exp).then_inc(route_exp, 1)

            act.wait_ge(y0_c, 1)
            A(y_e[:, 512:1024], y_e[:, 0:512], Cp).then_inc(y1_c, 1)
            A(hot_gt, y_e[:, 0:256], Cp).then_inc(sgt_c, 1)
            act.wait_ge(routed, 2)
            rounds = act.value_load(rounds_i[0:1, 0:1], min_val=1, max_val=4)
            act.wait_ge(gat0, 1)
            A(arena2[:, 0:512], psum[:, 2, :], Cp).then_inc(gat0_c, 1)
            with act.Fori(0, rounds) as r:
                with act.Fori(0, PAIRS) as p:
                    n = r * PAIRS + p
                    act.wait_ge(up1, n + 1)
                    A(silu1, psum[:, 0, :], ACT.Silu).then_inc(silu_e, 1)
                    act.wait_ge(actt_mm, n + 1)
                    A(arena2[:, 2816:3328], psum[:, 3, :], Cp).then_inc(actt_c, 1)
                    act.wait_ge(gat0, n + 2)
                    A(arena2[:, 0:512], psum[:, 2, :], Cp).then_inc(gat0_c, 1)
                    act.wait_ge(sgt_mm, n + 1)
                    A(hot_gt, psum[:, 2, 0:256], Cp).then_inc(sgt_c, 1)
                    act.wait_ge(y1_mm, n + 1)
                    A(y_e[:, 512:1024], psum[:, 1, :], Cp).then_inc(y1_c, 1)
            for kt in range(KT):
                act.wait_ge(x_ready, 41 + kt + 1)
                square("gate", kt, x[:, kt, :])
            deviation("gate", KT, D, eps_rms)
            for n in range(4):
                act.wait_ge(unit_done, UNIT_AT["pg"] + n + 1)
                A(d_flat[:, n * 512:(n + 1) * 512], psum[:, 4 + n, :], ACT.Sigmoid).then_inc(gate_done, 1)
            for kt in range(KT):
                act.wait_ge(x_ready, 49 + kt + 1)
                square("final", kt, x[:, kt, :])
            deviation("final", KT, D, eps_rms)

        @block.vector
        def _(dve):
            seq = [0]
            v = nc.vector

            def link(ins):
                seq[0] += 1
                ins.then_inc(dve_seq, 1)
                dve.wait_ge(dve_seq, seq[0])

            def stt(out_ap, in0, scalar, in1, op0, op1):
                return v.scalar_tensor_tensor(out_ap, in0, scalar, in1, op0, op1)

            def ada_piece(k, slot, turn_, cols, bias_cols):
                if turn_ is None:
                    dve.wait_ge(staged_in[k], 16)
                else:
                    dve.wait_ge(a_loaded[slot], (turn_ + (1 - STAGED // ARING)) * 16)
                for t in range(2):
                    w = (staged(k) if turn_ is None else aring[:, slot, :])[:, t * D:(t + 1) * D]
                    v.tensor_tensor_reduce(out=w, in0=w, in1=cb[:], scale=1.0, scalar=0.0, op0=ALU.mult, op1=ALU.add,
                                           accum_out=ada_raw[:, 2 * slot + t:2 * slot + t + 1]).then_inc(ada_sum, 1)
                dve.wait_ge(ada_sum, k * 2 + 2)
                v.tensor_tensor(cols, ada_raw[:, 2 * slot:2 * slot + 2], bias_cols, ALU.add).then_inc(ada_done, 1)

            ada_cols = ada[:].rearrange("p l n -> p (l n)")

            def pieces(lo, hi):
                for k in range(lo, hi):
                    ada_piece(k, k % 2, None if k < STAGED else k // 2, ada_cols[:, 2 * k:2 * k + 2], V("b_ada", 2 * k, 2))

            def split(k, i=None):
                if k == PLE or k >= PG:
                    return
                n = split_waits(dve, k, i)
                dve.wait_ge(w_hi_ready, n + 1 if i is None else i * RING + (n + 1))
                v.tensor_tensor(w_lo[:, n % 2, :], wring[:, k % RING, :], w_hi[:, n % 2, :].bitcast(F32),
                                ALU.subtract).then_inc(w_split, 1)

            def low_parts(version, src):
                for kt in range(KT):
                    dve.wait_ge(hi_ready, 8 * version + kt + 1)
                    v.tensor_tensor(h_lo[:, kt, :], src[:, kt, :], h_hi[:, kt, :].bitcast(F32), ALU.subtract).then_inc(lo_ready, 1)

            def scaled_low_parts(version, src, scale, shift):
                for kt in range(KT):
                    seq[0] += 1
                    v.tensor_scalar(h_lo32[:, kt, :], src[:, kt, :], scale[:, kt:kt + 1], shift[:, kt:kt + 1], ALU.mult,
                                    ALU.add).then_inc(dve_seq, 1)
                for kt in range(KT):
                    dve.wait_ge(dve_seq, seq[0] - KT + kt + 1)
                    dve.wait_ge(hi_ready, 8 * version + kt + 1)
                    v.tensor_tensor(h_lo[:, kt, :], h_lo32[:, kt, :], h_hi[:, kt, :].bitcast(F32), ALU.subtract).then_inc(lo_ready, 1)

            def piece_at(k, i, step=RING // 2):
                if i is None:
                    return pieces(k, k + 1)
                ada_piece(i * step + k, k % 2, i * (step // 2) + k // 2, ada_cols[:, bass.ds(i * (2 * step) + 2 * k, 2)],
                          vec[:, bass.ds(i * (2 * step) + (VEC_AT["b_ada"] + 2 * k), 2)])

            def derive(q):
                layer = q // 2
                part = lambda l, n: ada[:, l, 8 * n:8 * n + 8]
                g, b = V("ln_g", 8 * q, 8), V("ln_b", 8 * q, 8)
                dve.wait_ge(ada_done, (20, 32, 48, 48)[q])
                link(v.tensor_scalar(drv[:, q, 0, :], part(layer, 5 if q % 2 else 2), 1.0, None, ALU.add))
                if q < 3:
                    l, sc, sh = ((0, 4, 3), (1, 1, 0), (1, 4, 3))[q]
                    link(stt(drv[:, q, 1, :], part(l, sc), 1.0, g, ALU.add, ALU.mult))
                    link(stt(drv[:, q, 2, :], part(l, sc), 1.0, b, ALU.add, ALU.mult))
                    link(v.tensor_tensor(drv[:, q, 2, :], drv[:, q, 2, :], part(l, sh), ALU.add))
                alpha = ALPHA if q < 3 else 1.0
                link(v.tensor_scalar(drv[:, q, 3, :], g, alpha, None, ALU.mult))
                v.tensor_scalar(drv[:, q, 4, :], b, alpha, None, ALU.mult).then_inc(drv_ready, 1)
                dve.wait_ge(drv_ready, q + 2)

            def log1p(y, z, w, s):
                link(v.tensor_scalar(z, y, 2.0, None, ALU.add))
                link(v.reciprocal(z, z))
                link(v.tensor_tensor(z, z, y, ALU.mult))
                link(v.tensor_tensor(w, z, z, ALU.mult))
                link(v.tensor_scalar(s, w, 1.0 / 17, None, ALU.mult))
                for n in (15, 13, 11, 9, 7, 5, 3):
                    link(stt(s, s, 1.0 / n, w, ALU.add, ALU.mult))
                link(stt(s, s, 1.0, z, ALU.add, ALU.mult))

            link(v.memset(small[:, 60:61], LN_EPS))
            link(v.memset(small[:, 61:62], RMS_EPS))
            dve.wait_ge(bias_mm, 1)
            dve.wait_ge(consts_in, CONSTS)
            stt(bias_rows, psum[0:16, 2, 0:384], -1.0, added_in, ALU.mult, ALU.add).then_inc(bias_row, 1)
            dve.wait_ge(silu_c, 17)
            pieces(0, 8)
            dve.wait_ge(ada_done, 8)
            v.tensor_scalar(small[:, 0:8], ada[:, 0, 8:16], 1.0, None, ALU.add).then_inc(drv_ready, 1)
            dve.wait_ge(drv_ready, 1)
            dve.wait_ge(x_in, 16)
            scaled_low_parts(0, x, small[:, 0:8], ada[:, 0, 0:8])
            split(0)
            split(1)
            dve.wait_ge(later_in, LATER)
            for n in range(2):
                l0, l1 = lam_in[:, 128 * n:128 * n + 64], lam_in[:, 128 * n + 64:128 * n + 128]
                v.tensor_tensor_reduce(out=l0, in0=l0, in1=l1, scale=1.0, scalar=0.0, op0=ALU.mult, op1=ALU.add,
                                       accum_out=small[:, 10 + n:11 + n]).then_inc(lam_sum, 1)
            for j in range(12):
                split(UNIT_AT["v0"] + j + 2)
                if j < 10:
                    pieces(8 + j, 9 + j)
            dve.wait_ge(lam_exp, 1)
            link(v.tensor_tensor(small[:, 14:15], small[:, 13:14], small[:, 12:13], ALU.subtract))
            link(v.tensor_scalar(small[:, 14:15], small[:, 14:15], -LAMBDA_INIT, None, ALU.add))
            link(v.tensor_scalar(small[:, 15:16], V("subln_g"), 1.0 - LAMBDA_INIT, None, ALU.mult))

            def attention(layer):
                items = [(0, [2 * i, 2 * i + 1]) for i in range(4)] if layer == 0 else [(1, [i]) for i in range(8)]
                items += [(1, [8 + i]) for i in range(8)]
                item_of = {m: i for i, (_, maps) in enumerate(items) for m in maps}

                def head_operand(hd):
                    if hd >= 2:
                        dve.wait_ge(score_mm, MAPS * layer + 8 + hd - 1)
                    v.tensor_scalar(f_vh[hd % 2], f_v, fsmall[:, 1 + hd:2 + hd], None,
                                    ALU.mult).then_inc(fd_head, 1)

                def shift(maps):
                    for m in maps:
                        n = MAPS * layer + m
                        dve.wait_ge(score_mm, n + 1)
                        if m >= 4:
                            dve.wait_ge(pt_mm, 12 * layer + item_of[m - 4] + 1)
                        if m < 8:
                            bt = bias[:, m // 2 if layer == 0 else m, :]
                        else:
                            bt = bias[:, m if layer == 0 else 16, :]
                        s, b = score[:, m % 4, :], m % 4
                        v.tensor_tensor_reduce(out=s[:, 0:256], in0=psum[:, b, 0:256], in1=bt, scale=1.0,
                                               scalar=3e38, op0=ALU.add, op1=ALU.min, accum_out=mins[:, m, 0:1])
                        v.tensor_tensor_reduce(out=s[:, 256:384], in0=psum[:, b, 256:384], in1=bt[:, P:2 * P],
                                               scale=1.0, scalar=3e38, op0=ALU.add, op1=ALU.min,
                                               accum_out=mins[:, m, 1:2]).then_inc(score_rd, 1)

                def normalise(i, single, maps):
                    m = maps[-1]
                    n = 12 * layer + i
                    dve.wait_ge(exp_done, MAPS * layer + m + 1)
                    s = score[:, maps[0] % 4, :]
                    if single:
                        link(v.reciprocal(den[:, m, :], den[:, m, :]))
                        v.tensor_scalar(s[:, 0:256], s[:, 0:256], den[:, m, 0:1], None, ALU.mult)
                        v.tensor_scalar(s[:, 256:384], s[:, 256:384], den[:, m, 1:2], None, ALU.mult).then_inc(prob_ready, 1)
                    else:
                        s1, m0 = score[:, m % 4, :], maps[0]
                        link(v.reciprocal(den[:, m0:m + 1, :], den[:, m0:m + 1, :]))
                        link(v.tensor_scalar(den[:, m, :], den[:, m, :], small[:, 14:15], None, ALU.mult))
                        v.tensor_scalar(s1[:, 0:256], s1[:, 0:256], den[:, m, 0:1], None, ALU.mult)
                        link(v.tensor_scalar(s1[:, 256:384], s1[:, 256:384], den[:, m, 1:2], None, ALU.mult))
                        stt(s[:, 0:256], s[:, 0:256], den[:, m0, 0:1], s1[:, 0:256], ALU.mult, ALU.add)
                        stt(s[:, 256:384], s[:, 256:384], den[:, m0, 1:2], s1[:, 256:384], ALU.mult,
                            ALU.add).then_inc(prob_ready, 1)

                def take_o(i, single, maps):
                    dve.wait_ge(o_mm, 12 * layer + i + 1)
                    tile, at, width = (maps[0] // 2, (maps[0] % 2) * DH, DH) if single else (i, 0, P)
                    v.tensor_copy(o[at:at + width, tile, :], psum[at:at + width, 6 + i % 2, 0:T]).then_inc(o_copied, 1)

                if layer == 1:
                    head_operand(0)
                    head_operand(1)
                shift(items[0][1])
                for i, (single, maps) in enumerate(items):
                    if i + 1 < len(items):
                        shift(items[i + 1][1])
                        nxt = items[i + 1][1][0]
                        if layer == 1 and 8 <= nxt < 14:
                            head_operand(nxt - 8 + 2)
                    normalise(i, single, maps)
                    if i >= 2:
                        take_o(i - 2, *items[i - 2])
                for i in (len(items) - 2, len(items) - 1):
                    take_o(i, *items[i])

            def invert(norm):
                dve.wait_ge(std_ready, NORM_NO[norm] + 1)
                link(v.reciprocal(rstd[:], rstd[:]))

            H_BEFORE = (2, 3, 5, 6)

            def layer_norm(q):
                if q % 2:
                    dve.wait_ge(unit_done, UNIT_AT[f"fo{q // 2}"] + 11)
                dve.wait_ge(x_ready, 1 + 8 * q)
                dve.wait_ge(hi_ready, 8 * H_BEFORE[q])
                for kt in range(KT):
                    if q % 2 == 0:
                        dve.wait_ge(unit_done, UNIT_AT[f"wo{q // 2}"] + kt // 2 + 1)
                    stt(d[:, kt, :], y_ps(kt), drv[:, q, 0, kt:kt + 1], x[:, kt, :], ALU.mult, ALU.add).then_inc(resid, 1)
                dve.wait_ge(mean_mm, q + 1)
                for kt in range(KT):
                    stt(d[:, kt, :], half(2, 0), -1.0 / D, d[:, kt, :], ALU.mult, ALU.add).then_inc(centred, 1)
                invert(f"ln{q}")
                for kt in range(KT):
                    v.tensor_tensor(d[:, kt, :], d[:, kt, :], rstd[:], ALU.mult).then_inc(normed, 1)
                if q < 3:
                    dve.wait_ge(normed, 8 * q + 8)
                    scaled_low_parts(H_BEFORE[q], d, drv[:, q, 1, :], drv[:, q, 2, :])

            def rms(norm, src, gain, dst, signal):
                invert(norm)
                for kt in range(KT):
                    stt(dst[:, kt, :], src[:, kt, :], V(gain, kt), rstd[:], ALU.mult, ALU.mult).then_inc(signal, 1)

            for layer in range(DEPTH):
                if layer == 1:
                    for j in range(12):
                        split(UNIT_AT["v1"] + j + 2)
                        if j < 6:
                            pieces(42 + j, 43 + j)
                    derive(2)
                    derive(3)
                    dve.wait_ge(fd_exp, 1)
                    f8 = lambda ap: ap[0:8, :]
                    link(v.memset(f_u, 0.0))
                    link(v.memset(f_v, 0.0))
                    log1p(f8(f_e), f8(f_z), f8(f_w), f8(f_vh[0]))
                    link(v.tensor_scalar(f8(f_x), f8(f_x), 0.0, None, ALU.min))
                    link(stt(f8(f_x), f8(f_vh[0]), -2.0, f8(f_x), ALU.mult, ALU.add))
                    link(v.memset(f8(f_z), 1.0))
                    link(v.tensor_tensor_scan(f8(f_u), f8(f_z), f8(f_x), 0.0, ALU.mult, ALU.add))
                    for at in (32, 96):
                        link(v.tensor_copy(f_v[at:at + 8, :], f8(f_u)))
                        link(v.memset(f_u[at:at + 8, :], 1.0))
                        link(v.memset(f_v[at - 32:at - 24, :], -1.0))
                    link(v.tensor_copy(f_u[64:72, :], f8(f_u)))
                else:
                    dve.wait_ge(flipped, 2)
                attention(layer)
                if layer == 0:
                    dve.wait_ge(std_ready, 1)
                    link(v.reciprocal(d_flat[:, 0:1024], d_flat[:, 0:1024]))
                    for i in range(4):
                        stt(o[:, i, :], o[:, i, :], small[:, 15:16], d[:, i, :], ALU.mult, ALU.mult).then_inc(o_ready, 1)
                low_parts(3 * layer + 1, o)
                for j in range(4):
                    split(UNIT_AT[f"wo{layer}"] + j + 2)
                    if layer == 0 and j < 2:
                        pieces(18 + j, 19 + j)
                if layer == 0:
                    derive(0)
                layer_norm(2 * layer)

                def gated(j, i, idx, layer=layer):
                    dve.wait_ge(gate_done, 22 * layer + idx + 1)
                    tile = lambda part: part[:, bass.ds(idx, 1), :] if i is not None else part[:, j, :]
                    n = FT * layer + idx
                    v.tensor_tensor(gate_s[:, j % 2, :], gate_s[:, j % 2, :], half(j % 2, 1), ALU.mult).then_inc(bank_free, 1)
                    dve.wait_ge(bank_free, BANK_AT[f"fi{layer}"] + idx + 1)
                    v.tensor_copy(tile(act_hi), gate_s[:, j % 2, :]).then_inc(act_high, 1)
                    dve.wait_ge(act_high, n + 1)
                    v.tensor_tensor(tile(act_lo), gate_s[:, j % 2, :], tile(act_hi).bitcast(F32), ALU.subtract).then_inc(act_split, 1)
                    split(UNIT_AT[f"fi{layer}"] + j + 2, i)
                    if layer == 0 and j % 2 == 0:
                        piece_at(20 + j // 2, i)
                each_unit(dve, FT, 0, gated, peel=2)

                def behind_ffn_out(j, i, idx, layer=layer):
                    split(UNIT_AT[f"fo{layer}"] + j + 2, i)
                    if layer == 0:
                        piece_at(31 + j, i, RING)
                each_unit(dve, FT // 2, 0, behind_ffn_out, peel=1)
                if layer == 0:
                    derive(1)
                layer_norm(2 * layer + 1)

            rms("mix", x, "g_mix", h_lo32, h_whole)
            dve.wait_ge(h_whole, 8)
            low_parts(6, h_lo32)
            dve.wait_ge(lru_abs, 2)
            log1p(small[:, 28:32], small[:, 32:36], small[:, 36:40], small[:, 40:44])
            link(v.tensor_scalar(small[:, 20:24], V("lam", 0, 4), -1.0, 0.0, ALU.mult, ALU.max))
            link(stt(small[:, 20:24], small[:, 40:44], 2.0, small[:, 20:24], ALU.mult, ALU.add))
            link(v.tensor_scalar(small[:, 20:24], small[:, 20:24], 8.0, None, ALU.mult))
            dve.wait_ge(pad_zero, 2)
            for j in range(CT):
                dve.wait_ge(gate_done, 44 + j + 1)
                v.tensor_tensor(u_pad[:, j, PU:PU + T], gate_s[:, j % 2, :], half(j % 2, 0), ALU.mult).then_inc(bank_free, 1)
                split(UNIT_AT["z"] + j + 2)
            dve.wait_ge(bank_free, BANK_AT["z"] + 4)
            convolve(dve, v, (0, 1), dve_taps, between=lambda t: split(UNIT_AT["z"] + 6 + t // 8) if t in (4, 12) else None)
            split(UNIT_AT["wout"])
            split(UNIT_AT["wout"] + 1)
            dve.wait_ge(bank_free, BANK_AT["z"] + 8)
            for j in range(CT):
                for t in range(LRU_W):
                    w = V("lru_w", j * LRU_W + t)
                    if t:
                        ins = stt(lru_x[:, j, :], l_pad[:, j, t:t + T], w, lru_x[:, j, :], ALU.mult, ALU.add)
                    else:
                        ins = v.tensor_scalar(lru_x[:, j, :], l_pad[:, j, 0:T], w, V("lru_b", j), ALU.mult, ALU.add)
                    if t < LRU_W - 1:
                        link(ins)
                    else:
                        ins.then_inc(xr_ready, 1)
            rms("ple_proj", ple_e, "g_ple_proj", ple_e, ple_scaled)
            dve.wait_ge(gates_act, 1)
            for j in range(CT):
                ins = v.tensor_scalar(t_a[:, j, :], g_r[:, j, :], small[:, 20 + j:21 + j], None, ALU.mult)
            ins.then_inc(lru_l, 1)
            dve.wait_ge(lru_t, 2)
            link(v.tensor_scalar(t_c, t_b, 1.0, None, ALU.add))
            link(v.reciprocal(t_c, t_c))
            v.tensor_tensor(t_b, t_b, t_c, ALU.mult).then_inc(lru_u, 1)
            dve.wait_ge(gates_act, 2)
            v.tensor_tensor(g_i, g_i, lru_x, ALU.mult).then_inc(lru_u, 1)
            dve.wait_ge(lru_t, 3)
            dve.wait_ge(lru_u, 2)
            v.tensor_tensor(t_b, t_a, g_i, ALU.mult).then_inc(lru_u, 1)
            dve.wait_ge(lru_u, 3)
            for j in range(CT):
                link(v.tensor_tensor_scan(t_c[:, j, :], g_r[:, j, :], t_b[:, j, :], 0.0, ALU.mult, ALU.add))
            v.tensor_tensor(cat[:, CT:2 * CT, :], t_c, lru_g, ALU.mult).then_inc(lru_u, 5)
            dve.wait_ge(mean_mm, 5)
            for j in range(CT):
                stt(conv[:, j, :], half(2, 0), -1.0 / 512, conv[:, j, :], ALU.mult, ALU.add).then_inc(conv_norm, 1)
            invert("conv")
            for j in range(CT):
                v.tensor_tensor(conv[:, j, :], conv[:, j, :], rstd[:], ALU.mult).then_inc(conv_norm, 1)
            low_parts(7, cat)
            split(UNIT_AT["wout"] + 2)
            split(UNIT_AT["wout"] + 3)
            for kt in range(KT):
                dve.wait_ge(unit_done, UNIT_AT["wout"] + kt // 2 + 1)
                v.tensor_tensor(x[:, kt, :], x[:, kt, :], y_ps(kt), ALU.add).then_inc(x_ready, 1)
            rms("ffn", x, "g_ffn", h, h_ready)

            dve.wait_ge(rc_in, 32)
            dve.wait_ge(route_mm, 1)
            tiles = lambda ap, n: ap.unsqueeze(1).to_broadcast([P, TT, n])
            along = lambda ap, n: ap.unsqueeze(2).to_broadcast([P, TT, n])
            S = lambda i: r_s[:, i, :]
            w4, w32 = rc[:, RC_W4:RC_W4 + NG], rc[:, RC_W32:RC_W32 + NE]

            def first_max(values, best, n, weights, work, hot):
                link(v.tensor_reduce(best, values, AX_X, ALU.max))
                link(v.tensor_tensor(work, values, along(best, n), ALU.is_equal))
                link(v.tensor_tensor(work, work, tiles(weights, n), ALU.mult))
                link(v.tensor_reduce(S(10), work, AX_X, ALU.max))
                link(v.tensor_tensor(hot, work, along(S(10), n), ALU.is_equal))

            link(v.tensor_tensor(r_logit, psum[:, 0, 0:128].rearrange("p (a n) -> p a n", a=TT)[:, :, 0:36],
                                 tiles(b_route, 36), ALU.add))
            gl, el = r_logit[:, :, 0:NG], r_logit[:, :, NG:NG + NE]
            first_max(gl, S(0), NG, w4, r_gwork, r_ghot)
            v.tensor_tensor(r_gwork, gl, along(S(0), NG), ALU.subtract).then_inc(route_d, 1)
            link(v.tensor_scalar(r_pen, r_ghot, -1.0, 1e30, ALU.add, ALU.mult))
            for t in range(TT):
                link(v.tensor_tensor(r_el[:, t, :].rearrange("p (g e) -> p g e", g=NG),
                                     el[:, t, :].rearrange("p (g e) -> p g e", g=NG),
                                     r_pen[:, t, :].unsqueeze(2).to_broadcast([P, NG, EPG]), ALU.add))
            first_max(r_el, S(3), NE, w32, r_work, r_first)
            link(stt(r_el, r_first, -1e30, r_el, ALU.mult, ALU.add))
            first_max(r_el, S(4), NE, w32, r_work, r_hot_m)
            v.tensor_tensor(S(5), S(4), S(3), ALU.subtract).then_inc(route_d, 1)
            dve.wait_ge(route_exp, 1)
            link(v.tensor_reduce(S(1), r_gwork, AX_X, ALU.add))
            link(v.reciprocal(S(1), S(1)))
            dve.wait_ge(route_exp, 2)
            link(v.tensor_scalar(S(7), S(6), 1.0, None, ALU.add))
            link(v.reciprocal(S(7), S(7)))
            link(v.tensor_tensor(S(7), S(7), S(1), ALU.mult))
            link(v.tensor_tensor(S(8), S(7), S(6), ALU.mult))
            link(v.tensor_tensor(r_gate, r_first, along(S(7), NE), ALU.mult))
            link(v.tensor_tensor(r_work, r_hot_m, along(S(8), NE), ALU.mult))
            link(v.tensor_tensor(r_gate, r_gate, r_work, ALU.add))
            v.tensor_tensor(r_hot_m, r_hot_m, r_first, ALU.add).then_inc(route_m, 1)
            dve.wait_ge(rank_mm, 1)
            link(v.tensor_scalar(r_work, r_hot_m, -1.0, 1e6, ALU.add, ALU.mult))
            for t in range(TT):
                link(v.tensor_tensor(r_rank[:, t, 0:NE], psum[:, 1, t * 64:t * 64 + NE], r_hot_m[:, t, :], ALU.mult))
            link(v.tensor_tensor(r_rank[:, :, 0:NE], r_rank[:, :, 0:NE], r_work, ALU.add))
            link(v.tensor_scalar(r_rank[:, :, NE:NE + 2], r_rank[:, :, 0:2], -float(CAP), None, ALU.add))
            link(v.tensor_reduce(r_s[:, 11, 0:1], psum[:, 1, 128:128 + NE], AX_X, ALU.max))
            link(v.tensor_scalar(r_s[:, 12, 0:1], r_s[:, 11, 0:1], float(CAP), 1.0, ALU.is_gt, ALU.add))
            for n in (2, 3):
                link(v.tensor_scalar(r_s[:, 13, 0:1], r_s[:, 11, 0:1], float(n * CAP), None, ALU.is_gt))
                link(v.tensor_tensor(r_s[:, 12, 0:1], r_s[:, 12, 0:1], r_s[:, 13, 0:1], ALU.add))
            link(v.tensor_copy(rounds_i[:], r_s[:, 12, 0:1]))
            dve.sem_inc(routed, 2)
            rounds = dve.value_load(rounds_i[0:1, 0:1], min_val=1, max_val=4)

            slots4 = rc[:, RC_SLOT:RC_SLOT + CAP].unsqueeze(1).to_broadcast([P, 2, CAP])

            def choose(first):
                for t in range(TT):
                    rank = r_rank[:, t, first].unsqueeze(2).to_broadcast([P, 2, CAP])
                    ins = v.tensor_tensor(hot_s[:, t, :, :], slots4, rank, ALU.is_equal)
                return ins

            v.memset(y_e[:, 0:512], 0.0).then_inc(y0_c, 1)
            choose(slice(0, 2)).then_inc(s_ready, 1)
            dve.wait_ge(gat1, 1)
            v.tensor_copy(arena2[:, 512:1024], psum[:, 3, :]).then_inc(gat1_c, 1)
            with dve.Fori(0, rounds) as r:
                with dve.Fori(0, PAIRS) as p:
                    n = r * PAIRS + p
                    dve.wait_ge(up1, n + 1)
                    dve.wait_ge(s_ready, n + 1)
                    for t in range(TT):
                        gates = r_gate[:, t, bass.ds(p * 2, 2)].unsqueeze(2).to_broadcast([P, 2, CAP])
                        ins = v.tensor_tensor(hot_g[:, t, :, :], hot_s[:, t, :, :], gates, ALU.mult)
                    ins.then_inc(sg_ready, 1)
                    dve.wait_ge(sg_ready, n + 1)
                    choose(bass.ds(p * 2 + 2, 2)).then_inc(s_ready, 1)
                    dve.wait_ge(silu_e, n + 1)
                    dve.wait_ge(up3, n + 1)
                    v.tensor_tensor(act_e, silu1, psum[:, 1, :], ALU.mult).then_inc(act_ready, 1)
                    dve.wait_ge(gat1, n + 2)
                    v.tensor_copy(arena2[:, 512:1024], psum[:, 3, :]).then_inc(gat1_c, 1)
                    dve.wait_ge(y0_mm, n + 1)
                    v.tensor_copy(y_e[:, 0:512], psum[:, 0, :]).then_inc(y0_c, 1)
                dve.wait_ge(s_ready, r * PAIRS + (PAIRS + 1))
                v.tensor_scalar(r_rank, r_rank, -float(CAP), None, ALU.add).then_inc(next_round, 1)
                dve.wait_ge(next_round, r + 1)
            dve.wait_ge(scattered, rounds * PAIRS + 1)
            for kt in range(KT):
                v.tensor_tensor(x[:, kt, :], x[:, kt, :], y_ps(kt), ALU.add).then_inc(x_ready, 1)
            rms("gate", x, "g_ple", h, h_ready)
            dve.wait_ge(ple_scaled, 8)
            for kt in range(KT):
                dve.wait_ge(gate_done, 48 + kt // 2 + 1)
                link(v.tensor_tensor(d[:, kt, :], d[:, kt, :], ple_e[:, kt, :], ALU.mult))
                v.tensor_tensor(x[:, kt, :], x[:, kt, :], d[:, kt, :], ALU.add).then_inc(x_ready, 1)
            rms("final", x, "g_final", d, out_ready)


INPUTS = ["x_t", "c_rows", "table", "vecs", "ada", "units", "lam_in", "w_forget", "forget_b", "p_t", "w_r", "w_i",
          "w_route", "b_route", "w1", "w3", "w2"]


def lay_out(i):
    f = {k: np.asarray(v) for k, v in i.items()}

    def features(m):
        return np.ascontiguousarray(m.reshape(-1, P, m.shape[1]).transpose(1, 0, 2))

    def cols(v):
        return v.reshape(-1, P).T

    def col_units(w):
        k, n = w.shape
        return w.reshape(KT, P, n // 256, 256).transpose(2, 1, 0, 3).reshape(n // 256, P, UNIT)

    def row_units(w):
        k, n = w.shape
        return w.reshape(k // 256, 2, P, n).transpose(0, 2, 1, 3).reshape(k // 256, P, UNIT)

    def pairs(w):
        k, n = w.shape
        return w.reshape(k, 2, n // 256, P).transpose(0, 2, 1, 3).reshape(k, n)

    ab, cd = f["w_in_ab"][0], f["w_in_cd"][0]
    units = []
    for layer, w in enumerate((ab, cd)):
        units += [col_units(np.concatenate([w[:, 1024:1536], w[:, 2560:3072]], axis=1)),
                  col_units(np.concatenate([w[:, 0:1024], w[:, 1536:2560]], axis=1)),
                  col_units(f["w_o"][layer]), col_units(pairs(f["w_ffn_in"][layer])), row_units(f["w_ffn_out"][layer])]
    w = f["w_in_2"][0]
    units += [col_units(np.concatenate([pairs(w[:, 0:1024]), pairs(w[:, 1024:2048])], axis=1)),
              row_units(f["w_ple_2"][0]), col_units(f["w_out_2"][0]), col_units(f["w_ple_gate_2"][0])]
    vecs = {
        "b_ada": cols(f["b_ada"]), "ln_g": cols(f["ln_g"]), "ln_b": cols(f["ln_b"]), "subln_g": cols(f["diff_subln_g"]),
        "conv_w": f["conv_dw_w_2"][0].reshape(CONV_W, CT, P).transpose(2, 1, 0).reshape(P, -1),
        "conv_b": cols(f["conv_dw_b_2"]), "conv_ln_g": cols(f["conv_ln_g_2"]), "conv_ln_b": cols(f["conv_ln_b_2"]),
        "lru_w": f["lru_conv_w_2"][0].reshape(LRU_W, CT, P).transpose(2, 1, 0).reshape(P, -1),
        "lru_b": cols(f["lru_conv_b_2"]), "b_r": cols(f["lru_b_r_2"]), "b_i": cols(f["lru_b_i_2"]),
        "lam": cols(f["lru_lambda_2"]), "g_mix": cols(f["g_mix_2"]), "g_ffn": cols(f["g_ffn_2"]),
        "g_ple": cols(f["g_ple_2"]), "g_ple_proj": cols(f["g_ple_proj_2"]), "g_final": cols(f["g_final_2"]),
    }
    ada = f["w_ada"].reshape(DEPTH, D, 24, 2, P).transpose(0, 2, 4, 3, 1).reshape(ADA_PIECES, P, UNIT)
    up = lambda w: w[0].reshape(PAIRS, 2, KT, P, FE).transpose(0, 1, 3, 2, 4).reshape(PAIRS, 2, P, 4096)
    blocks = lambda w: w[0].reshape(CT, 2, 64, 64).transpose(1, 2, 0, 3).reshape(P, CT, 64)
    laid = {
        "x_t": features(f["x"][0].T), "c_rows": np.broadcast_to(f["c"], (P, D)),
        "table": np.concatenate([f["rel_bias"][:, 0:8], f["rel_bias"][:, 4:12]], axis=1),
        "vecs": np.concatenate([vecs[n] for n, _ in VECS], axis=1), "ada": ada, "units": np.concatenate(units),
        "lam_in": np.broadcast_to(f["diff_lambda"][0].reshape(1, 256), (P, 256)),
        "w_forget": cd[:, 3072:3080].reshape(KT, P, 8).transpose(1, 0, 2), "forget_b": f["forget_b"].T,
        "p_t": features(f["p_2"][0, 0].T), "w_r": blocks(f["lru_w_r_2"]), "w_i": blocks(f["lru_w_i_2"]),
        "w_route": np.concatenate([f["w_group_2"][0], f["w_expert_2"][0]], axis=1).reshape(KT, P, 36).transpose(1, 0, 2),
        "b_route": np.broadcast_to(np.concatenate([f["b_group_2"][0], f["b_expert_2"][0]])[None], (P, 36)),
        "w1": up(f["w1_2"]), "w3": up(f["w3_2"]),
        "w2": f["w2_2"][0].reshape(PAIRS, 2, 4, P, D).transpose(0, 1, 3, 2, 4).reshape(PAIRS, 2, P, 4096),
    }
    laid.update(shape_constants())
    return {k: np.ascontiguousarray(v) for k, v in laid.items()}


def kernel(**inputs):
    import concourse.bacc as bacc
    from concourse.bass_utils import run_bass_kernel_spmd

    arrays = lay_out(inputs)
    nc = bacc.Bacc("TRN2", target_bir_lowering=False, num_devices=1)
    a = {n: nc.dram_tensor(f"in_{n}", v.shape, mybir.dt.from_np(v.dtype), kind="ExternalInput").ap() for n, v in arrays.items()}
    out = nc.dram_tensor("out", (P, KT, T), F32, kind="ExternalOutput").ap()
    build(nc, a, out)
    r = run_bass_kernel_spmd(nc, [{f"in_{n}": v for n, v in arrays.items()}], core_ids=[0])
    return np.ascontiguousarray(r.results[0]["out"].transpose(2, 1, 0).reshape(1, T, D))
```

```python
import math
from contextlib import ExitStack

import numpy as np

import concourse.bass as bass
from concourse import mybir
from concourse.alu_op_type import AluOpType as ALU

ACT = mybir.ActivationFunctionType
F32 = mybir.dt.float32
F32R = mybir.dt.float32r
I32 = mybir.dt.int32
AX_X = mybir.AxisListType.X

P = 128
T = 256
TT = T // P
D = 1024
KT = D // P
LRU_FIRST = (4, 5, 6, 7, 0, 1, 2, 3)
HEADS_LAST = (4, 5, 6, 7, 0, 1, 2, 3)
DEPTH = 2
DH = 64
D_FF = 2816
FT = D_FF // P
ALPHA = (2 * DEPTH) ** 0.25
LN_EPS = 1e-5
RMS_EPS = 1e-6
LAMBDA_INIT = 0.8 - 0.6 * math.exp(0.0)
MASKED = 1e30
MAPS = 16
BUCKETS = 32
CONV_W, LRU_W = 31, 4
CT = 4
NE, NG, EPG = 32, 4, 8
FE = 512
CAP = 64
PAIRS = NE // 2

RING = 4
UNIT = 2048
SQS = 3
ARING = 2

VECS = [("b_ada", 96), ("ln_g", 32), ("ln_b", 32), ("subln_g", 1), ("conv_w", CT * CONV_W),
        ("conv_b", 4), ("conv_ln_g", 4), ("conv_ln_b", 4), ("lru_w", CT * LRU_W), ("lru_b", 4),
        ("b_r", 4), ("b_i", 4), ("lam", 4), ("g_mix", 8), ("g_ffn", 8), ("g_ple", 8),
        ("g_ple_proj", 8), ("g_final", 8)]
VEC_AT = {}
_at = 0
for _name, _n in VECS:
    VEC_AT[_name] = _at
    _at += _n
N_VEC = _at

RC_TRI, RC_SLOT, RC_W4, RC_W32, N_RC = 0, 128, 192, 196, 228

STAGES = [("v0", 4), ("qk0", 8), ("wo0", 4), ("fi0", 22), ("fo0", 11),
          ("v1", 4), ("qk1", 8), ("wo1", 4), ("fi1", 22), ("fo1", 11),
          ("z", 8), ("ple", 1), ("wout", 4), ("pg", 4)]
UNIT_AT = {}
_at = 0
for _name, _n in STAGES:
    UNIT_AT[_name] = _at
    _at += _n
N_UNITS = _at
BANK_AT = {"v0": 0, "qk0": 4, "fi0": 12, "v1": 34, "qk1": 38, "fi1": 46, "z": 68}

NORMS = [("heads", 4), ("ln0", 8), ("ln1", 8), ("ln2", 8), ("ln3", 8), ("mix", 8), ("ple_proj", 8),
         ("conv", 4), ("ffn", 8), ("gate", 8), ("final", 8)]
SQ_AT = {}
_at = 0
for _name, _n in NORMS:
    SQ_AT[_name] = _at
    _at += _n
NORM_NO = {name: i for i, (name, _) in enumerate(NORMS)}

CONSTS, LATER = 6 * 16, 6 * 16
STAGED = 8
QKV_PIECES = (0, 1, 3, 4, 6, 7, 9, 10)
ADA_PIECES = 48


def shape_constants():
    ident = np.eye(P, dtype=np.float32)
    consts = np.concatenate([ident, np.ones((P, P), np.float32)], axis=1)
    n = 255 - np.arange(384)
    past = np.maximum(n, 0)
    large = 16 + (np.log(np.maximum(past, 1).astype(np.float32) / 16) / np.float32(math.log(128 / 16)) * 16).astype(np.int32)
    bucket = np.where(past < 16, past, np.minimum(large, BUCKETS - 1))
    hot = ((bucket[None, :] == np.arange(BUCKETS)[:, None]) & (n >= 0)[None, :]).astype(np.float32)
    times = (n <= 128).astype(np.float32) + (n % 4 == 0) + (n % 16 == 0)
    plain = np.where(n >= 0, 0.0, MASKED).astype(np.float32)
    dilated = np.where((n >= 0) & (times > 0), -np.log(np.maximum(times, 1)), MASKED).astype(np.float32)
    added = np.concatenate([np.tile(plain, (8, 1)), np.tile(dilated, (8, 1))]).astype(np.float32)
    q, k = np.arange(P)[:, None], np.arange(P)[None, :]
    causal = np.concatenate([np.zeros((P, P)), np.where(k <= q, 0.0, MASKED)], axis=1).astype(np.float32)
    router = np.zeros((P, N_RC), np.float32)
    router[:, RC_TRI:RC_TRI + P] = (q < k)
    router[:, RC_SLOT:RC_SLOT + CAP] = np.arange(CAP)
    router[:, RC_W4:RC_W4 + NG] = 8 - np.arange(NG)
    router[:, RC_W32:RC_W32 + NE] = 64 - np.arange(NE)
    rows = np.zeros((4, 32, 8), np.float32)
    rows[:, np.arange(8), np.arange(8)] = 1
    rows = rows.reshape(P, 8)
    return {"consts": consts, "hot": hot, "added": added, "causal": causal, "router_consts": router,
            "head_rows": rows, "flip": np.ascontiguousarray(ident[::-1])}


def build(nc, a, out):
    ctx = ExitStack()
    with ctx:
        where = {}

        def sb(name, shape, dt=F32):
            where[name] = (nc.sbuf_base + 31) // 32 * 32
            return ctx.enter_context(nc.sbuf_tensor(name, shape, dt))

        def sem(name):
            return ctx.enter_context(nc.semaphore(name))

        wring = sb("wring", [P, RING, UNIT])
        aring = sb("aring", [P, ARING, UNIT])
        w13 = sb("w13", [P, 4, 4096])
        arena = sb("arena", [P, 8192])
        arena2 = sb("arena2", [P, 6656])
        x = sb("x", [P, KT, T])
        h = sb("h", [P, KT, T])
        d = sb("d", [P, KT, T])
        sq = sb("sq", [P, SQS, T])
        rstd = sb("rstd", [P, T])
        vec = sb("vec", [P, N_VEC])
        cb = sb("cb", [P, D])
        cst = sb("cst", [P, 2 * P])
        w_route = sb("w_route", [P, KT, 36])
        w_forget = sb("w_forget", [P, KT, 8])
        ada = sb("ada", [P, DEPTH, 48])
        ada_raw = sb("ada_raw", [P, 4])
        drv = sb("drv", [P, 4, 5, 8])
        mins = sb("mins", [P, MAPS, 2])
        den = sb("den", [P, MAPS, 2])
        small = sb("small", [P, 64])
        fsmall = sb("fsmall", [P, 16])

        ident = cst[:, 0:P]
        ones = cst[:, P:2 * P]
        qk = arena[:, 0:4096].rearrange("p (n t) -> p n t", t=T)
        val = arena[:, 4096:6144].rearrange("p (a n) -> p a n", a=TT)
        o = arena[:, 6144:8192].rearrange("p (n t) -> p n t", t=T)
        bias = arena2[:, 0:17 * 256].rearrange("p (n t) -> p n t", t=256)
        score = arena2[:, 4352:4352 + 4 * 384].rearrange("p (n t) -> p n t", t=384)
        lam_in = arena2[:, 4352:4608]
        prob_t = arena2[:, 5888:5888 + 2 * 384].rearrange("p (n t) -> p n t", t=384)
        act = arena[:, 0:FT * T].rearrange("p (n t) -> p n t", t=T)
        gate_s = arena[:, FT * T:(FT + 2) * T].rearrange("p (n t) -> p n t", t=T)
        f_u, f_v = d[:, 0, :], d[:, 1, :]
        f_vh = [d[:, 2, :], d[:, 3, :]]
        f_x, f_e, f_z, f_w = (d[:, i, :] for i in (4, 5, 6, 7))
        PU, PL = CONV_W - 1, LRU_W - 1
        u_pad = arena2[:, 0:CT * (PU + T)].rearrange("p (n t) -> p n t", t=PU + T)
        l_pad = arena2[:, 1144:1144 + CT * (PL + T)].rearrange("p (n t) -> p n t", t=PL + T)
        lru_g = arena2[:, 2180:2180 + 1024].rearrange("p (n t) -> p n t", t=T)
        conv = arena2[:, 3204:3204 + 1024].rearrange("p (n t) -> p n t", t=T)
        lru_x = arena2[:, 4228:4228 + 1024].rearrange("p (n t) -> p n t", t=T)
        pt_in = arena2[:, 5252:5252 + 512].rearrange("p (n t) -> p n t", t=T)
        DIAGS = (16, 8)
        diag = (w13[:, 2, UNIT:2 * UNIT].rearrange("p (n j) -> p n j", j=P),
                arena[:, 7168:8192].rearrange("p (n j) -> p n j", j=P))
        cat = arena[:, 0:2048].rearrange("p (n t) -> p n t", t=T)
        g_r, g_i, t_a, t_b, t_c = (arena[:, 2048 + 1024 * i:3072 + 1024 * i].rearrange(
            "p (n t) -> p n t", t=T) for i in range(5))
        blk_w = cb[:, :].rearrange("p (g n j) -> p g n j", g=2, n=CT)
        ple_e = aring[:, 0, :].rearrange("p (n t) -> p n t", t=T)
        xe_t = arena2[:, 0:1024].rearrange("p (k c) -> p k c", k=KT)
        hot_s = arena2[:, 1024:1280].rearrange("p (a e c) -> p a e c", a=TT, e=2)
        hot_g = arena2[:, 1280:1536].rearrange("p (a e c) -> p a e c", a=TT, e=2)
        hot_gt = arena2[:, 1536:1792]
        silu1 = arena2[:, 1792:2304]
        act_e = arena2[:, 2304:2816]
        act_t = arena2[:, 2816:3328].rearrange("p (f c) -> p f c", f=4)
        y_e = arena2[:, 3328:4352]
        rc = arena2[:, 5764:5764 + N_RC]
        rt = arena2[:, 5992:6656]
        b_route = rt[:, 0:36]
        by_tile = lambda lo, n: rt[:, lo:lo + TT * n].rearrange("p (a e) -> p a e", a=TT)
        r_logit, r_hot_m, r_gate = by_tile(36, 36), by_tile(108, NE), by_tile(172, NE)
        r_rank = by_tile(236, NE + 2)
        r_first, r_work, r_el = by_tile(304, NE), by_tile(368, NE), by_tile(432, NE)
        r_both = r_el
        r_ghot, r_gwork, r_pen = by_tile(496, NG), by_tile(504, NG), by_tile(512, NG)
        r_s = rt[:, 528:576].rearrange("p (n a) -> p n a", a=TT)
        d_flat = d[:].rearrange("p k t -> p (k t)")

        def hf_t(t, kt):
            return d_flat[:, t * D + kt * P:t * D + (kt + 1) * P]

        table_in, hot_in = d_flat[0:BUCKETS, 1024:1040], d_flat[0:BUCKETS, 0:384]
        flip_in = d_flat[:, 384:512]
        added_in, bias_rows = d_flat[0:16, 512:896], d_flat[0:16, 1536:1920]

        psum = ctx.enter_context(nc.psum_tensor("psum", [P, 8, 512], F32))

        def staged(k):
            return w13[:, k // 2, (k % 2) * UNIT:(k % 2 + 1) * UNIT]

        reversed_rows = w13[:].rearrange("p a n -> p (a n)")[:, 10240:14336]

        def view(name, tensor, at, shape, dt=F32R):
            return nc.alloc_sbuf_tensor_at(name, shape, dt, offset=where[tensor] + at)

        w_hi, w_lo = view("w_hi", "w13", 0, [P, 2, UNIT]), view("w_lo", "w13", 16384, [P, 2, UNIT])
        h_hi, h_lo = view("h_hi", "h", 0, [P, KT, T]), view("h_lo", "w13", 32768, [P, KT, T])
        h_lo32 = view("h_lo32", "w13", 32768, [P, KT, T], F32)
        pg_hi, pg_lo = view("pg_hi", "w13", 0, [P, 4, UNIT]), view("pg_lo", "wring", 0, [P, 4, UNIT])
        g_lo, g_lo32 = view("g_lo", "aring", UNIT * 4, [P, KT, T]), view("g_lo32", "aring", UNIT * 4, [P, KT, T], F32)
        act_hi, act_lo = view("act_hi", "arena", 0, [P, FT, T]), view("act_lo", "w13", 40960, [P, FT, T])

        w2_at = [wring[:].rearrange("p s n -> p (s n)"), arena[:]]

        def pg_in(j):
            return w13[:, 2 + j // 2, (j % 2) * UNIT:(j % 2 + 1) * UNIT]

        def half(bank, i):
            return psum[:, bank, i * T:(i + 1) * T]

        def y_ps(n):
            return half(4 + n // 2, n % 2)

        consts_in = sem("consts_in")
        x_in = sem("x_in")
        later_in = sem("later_in")
        staged_in = [sem(f"staged_in{i}") for i in range(STAGED)]
        w_loaded = [sem(f"w_loaded{i}") for i in range(RING)]
        w_hi_ready, w_split = sem("w_hi_ready"), sem("w_split")
        hi_ready, lo_ready = sem("hi_ready"), sem("lo_ready")
        act_split = sem("act_split")
        unit_done = sem("unit_done")
        bank_free = sem("bank_free")
        a_loaded = [sem(f"a_loaded{i}") for i in range(ARING)]
        ada_done = sem("ada_done")
        silu_c = sem("silu_c")
        dve_seq, pool_seq = sem("dve_seq"), sem("pool_seq")
        bias_mm, bias_row, bias_out, bias_in = sem("bias_mm"), sem("bias_row"), sem("bias_out"), sem("bias_in")
        flip_mm, flipped = sem("flip_mm"), sem("flipped")
        drv_ready = sem("drv_ready")
        h_whole, act_high, g_whole = sem("h_whole"), sem("act_high"), sem("g_whole")
        gate_scaled = sem("gate_scaled")
        h_ready = sem("h_ready")
        x_ready = sem("x_ready")
        score_mm, score_rd, exp_done = sem("score_mm"), sem("score_rd"), sem("exp_done")
        prob_ready, pt_mm, pt_copied, o_mm, o_copied = (sem(n) for n in (
            "prob_ready", "pt_mm", "pt_copied", "o_mm", "o_copied"))
        fd_mm, fd_in, fd_abs, fd_exp, fd_head = (sem(n) for n in (
            "fd_mm", "fd_in", "fd_abs", "fd_exp", "fd_head"))
        head_std, o_ready = sem("head_std"), sem("o_ready")
        resid, centred, normed = sem("resid"), sem("centred"), sem("normed")
        sq_ready, sq_used = sem("sq_ready"), sem("sq_used")
        mean_mm = sem("mean_mm")
        std_ready = sem("std_ready")
        gate_done = sem("gate_done")
        pad_zero = sem("pad_zero")
        blk_in = sem("blk_in")
        ple_in = sem("ple_in")
        conv_done, dve_taps = sem("conv_done"), sem("dve_taps")
        diag_ready = [sem("diag_ready0"), sem("diag_ready1")]
        diag_used = [sem("diag_used0"), sem("diag_used1")]
        ada_sum = sem("ada_sum")
        lam_sum, lam_exp, lru_abs = sem("lam_sum"), sem("lam_exp"), sem("lru_abs")
        conv_norm, cat_ready = sem("conv_norm"), sem("cat_ready")
        xr_ready, gates_mm, gates_act, lru_l, lru_t, lru_u = (sem(n) for n in (
            "xr_ready", "gates_mm", "gates_act", "lru_l", "lru_t", "lru_u"))
        e_copied = sem("e_copied")
        route_mm, route_d, route_exp, route_m, rank_mm, routed = (sem(n) for n in (
            "route_mm", "route_d", "route_exp", "route_m", "rank_mm", "routed"))
        rc_in = sem("rc_in")
        tok_mm, tok_copied = sem("tok_mm"), sem("tok_copied")
        w13_loaded = [sem("w1_loaded"), sem("w3_loaded")]
        w2_loaded = [sem("w2_loaded0"), sem("w2_loaded1")]
        pg_hi_ready, pg_split = sem("pg_hi_ready"), sem("pg_split")
        s_ready, sg_ready, gat0, gat1, gat0_c, gat1_c = (sem(n) for n in (
            "s_ready", "sg_ready", "gat0", "gat1", "gat0_c", "gat1_c"))
        up1, up3, silu_e, act_ready, actt_mm, actt_c = (sem(n) for n in (
            "up1", "up3", "silu_e", "act_ready", "actt_mm", "actt_c"))
        sgt_mm, sgt_c, y0_mm, y1_mm, y0_c, y1_c, scattered = (sem(n) for n in (
            "sgt_mm", "sgt_c", "y0_mm", "y1_mm", "y0_c", "y1_c", "scattered"))
        ple_scaled, next_round = sem("ple_scaled"), sem("next_round")
        out_ready, stored = sem("out_ready"), sem("stored")

        scratch = nc.dram_tensor("bias_rows", (16, 384), F32, kind="Internal").ap()
        rounds_i = sb("rounds_i", [P, 1], I32)

        def V(name, i=0, n=1):
            return vec[:, VEC_AT[name] + i:VEC_AT[name] + i + n]

        def each_unit(eng, n, first, body, peel=0):
            for j in range(peel):
                body(j, None, j)
            whole = (n - peel) // RING
            if whole >= 2:
                with eng.Fori(0, whole) as i:
                    for k in range(RING):
                        body(peel + k, i, peel + k + i * RING)
                at = peel + whole * RING
            else:
                at = peel
            for j in range(at, n):
                body(j, None, j)

        def turn(j, i, base, period):
            t = (base + j) // period
            return t if i is None else t + i * (RING // period)

        PLE, PG = UNIT_AT["ple"], UNIT_AT["pg"]

        def split_no(k):
            return k if k < PLE else k - 1

        def unit_of(n):
            return n if n < PLE else n + 1

        def split_waits(eng, k, i):
            n = split_no(k)
            if n >= 2:
                done = unit_of(n - 2) + 1
                eng.wait_ge(unit_done, done if i is None else i * RING + done)
            return n

        def convolve(eng, nce, tiles, taps, between):
            for t in range(CONV_W):
                between(t)
                for k, j in enumerate(tiles):
                    if t:
                        eng.wait_ge(taps, 2 * (t - 1) + k + 1)
                        ins = nce.scalar_tensor_tensor(conv[:, j, :], u_pad[:, j, t:t + T],
                                                       V("conv_w", j * CONV_W + t), conv[:, j, :], ALU.mult, ALU.add)
                    else:
                        ins = nce.tensor_scalar(conv[:, j, :], u_pad[:, j, 0:T], V("conv_w", j * CONV_W),
                                                V("conv_b", j), ALU.mult, ALU.add)
                    ins.then_inc(conv_done if t == CONV_W - 1 else taps, 1)

        block = ctx.enter_context(nc.Block())

        @block.sync
        def _(sp):
            def small_loads(loads, signal):
                for dst, src in loads:
                    sp.dma_start(dst, src).then_inc(signal, 16)

            small_loads(((table_in, a["table"]), (hot_in, a["hot"]), (added_in, a["added"]), (flip_in, a["flip"]),
                         (vec[:], a["vecs"]), (cst[:], a["consts"])), consts_in)

            def load_unit(k):
                if k >= RING:
                    if k - RING == PLE:
                        sp.wait_ge(unit_done, PLE + 1)
                    else:
                        sp.wait_ge(w_split, split_no(k - RING) + 1)
                sp.dma_start(wring[:, k % RING, :], a["units"][k]).then_inc(w_loaded[k % RING], 16)

            def load_w13(e2, which, halves=(0, 1)):
                for s in halves:
                    sp.dma_start(w13[:, 2 * which + s, :], a["w3" if which else "w1"][e2, s]).then_inc(
                        w13_loaded[which], 16)

            def load_w2(e2, b):
                for s in range(2):
                    sp.dma_start(w2_at[b][:, 4096 * s:4096 * (s + 1)], a["w2"][e2, s]).then_inc(w2_loaded[b], 16)

            for k in range(STAGED):
                sp.dma_start(staged(k), a["ada"][k]).then_inc(staged_in[k], 16)
            sp.dma_start(x[:], a["x_t"]).then_inc(x_in, 16)
            for k in range(RING):
                load_unit(k)
            small_loads(((lam_in, a["lam_in"]), (bias[:, 16, :], a["causal"]), (w_forget[:], a["w_forget"]),
                         (w_route[:], a["w_route"]), (fsmall[0:8, 0:1], a["forget_b"]),
                         (fsmall[:, 1:9], a["head_rows"])), later_in)

            groups = PLE // RING
            with sp.Fori(1, groups) as i:
                for k in range(RING):
                    sp.wait_ge(w_split, i * RING + (k - RING + 1))
                    sp.dma_start(wring[:, k, :], a["units"][i * RING + k]).then_inc(w_loaded[k], 16)
            for k in range(RING * groups, PG):
                load_unit(k)
            sp.wait_ge(unit_done, UNIT_AT["z"])
            load_w13(0, 1, (1,))
            sp.wait_ge(w_split, split_no(PG - 1) + 1)
            load_w2(0, 0)
            sp.wait_ge(unit_done, UNIT_AT["wout"] + 4)
            load_w13(0, 0)
            load_w13(0, 1, (0,))
            load_w2(1, 1)

            def load_ups(p, n):
                sp.wait_ge(up1, n)
                load_w13(p, 0)
                sp.wait_ge(up3, n)
                load_w13(p, 1)

            def load_pair(p, n, b):
                load_ups(p, n)
                load_w2(p, b)

            load_ups(1, 1)
            with sp.Fori(1, PAIRS // 2) as i:
                for b in range(2):
                    load_pair(i * 2 + b, i * 2 + b, b)
            sp.wait_ge(routed, 2)
            rounds = sp.value_load(rounds_i[0:1, 0:1], min_val=1, max_val=4)
            with sp.If(rounds > 1):
                with sp.Fori(1, rounds) as r:
                    with sp.Fori(0, PAIRS // 2) as i:
                        for b in range(2):
                            load_pair(i * 2 + b, r * PAIRS + (i * 2 + b), b)
            sp.wait_ge(up3, rounds * PAIRS)
            for j in range(4):
                sp.dma_start(pg_in(j), a["units"][PG + j]).then_inc(w_loaded[(PG + j) % RING], 16)
            for k in range(2):
                sp.wait_ge(out_ready, 4 * k + 4)
                sp.dma_start(out[:, 4 * k:4 * k + 4, :], d[:, 4 * k:4 * k + 4, :]).then_inc(stored, 16)
            sp.wait_ge(stored, 32)

        @block.gpsimd
        def _(pool):
            seq = [0]

            def link(ins):
                seq[0] += 1
                ins.then_inc(pool_seq, 1)
                pool.wait_ge(pool_seq, seq[0])

            def ada_piece(k):
                if k >= STAGED + ARING:
                    pool.wait_ge(ada_done, k - ARING + 1)
                pool.dma_start(aring[:, k % ARING, :], a["ada"][k]).then_inc(a_loaded[k % ARING], 16)

            def pieces(lo, hi):
                for k in range(lo, hi):
                    ada_piece(k)

            pool.wait_ge(staged_in[STAGED - 1], 16)
            pieces(8, 10)
            pool.wait_ge(hi_ready, 8)
            pool.wait_ge(lo_ready, 8)
            nc.gpsimd.tensor_scalar(x[:], x[:], ALPHA, None, ALU.mult).then_inc(x_ready, 1)
            pieces(10, 22)

            def layer_norm_x(q):
                pool.wait_ge(drv_ready, q + 2)
                for kt in range(KT):
                    pool.wait_ge(normed, 8 * q + kt + 1)
                    nc.gpsimd.tensor_scalar(x[:, kt, :], d[:, kt, :], drv[:, q, 3, kt:kt + 1],
                                            drv[:, q, 4, kt:kt + 1], ALU.mult, ALU.add).then_inc(x_ready, 1)

            layer_norm_x(0)
            with pool.Fori(0, 7) as i:
                for s in range(ARING):
                    pool.wait_ge(ada_done, i * 2 + (22 + s - ARING + 1))
                    pool.dma_start(aring[:, s, :], a["ada"][i * 2 + (22 + s)]).then_inc(a_loaded[s], 16)
            layer_norm_x(1)
            pieces(36, 46)
            layer_norm_x(2)
            pieces(46, 48)
            layer_norm_x(3)

            pool.wait_ge(ada_done, ADA_PIECES)
            link(nc.gpsimd.memset(cb[:], 0.0))
            for g, name in enumerate(("w_r", "w_i")):
                for s in range(2):
                    pool.dma_start(blk_w[64 * s:64 * s + 64, g, :, 64 * s:64 * s + 64],
                                   a[name][64 * s:64 * s + 64]).then_inc(blk_in, 16)
            pool.wait_ge(o_copied, 28)
            pool.dma_start(pt_in, a["p_t"]).then_inc(ple_in, 16)
            nc.gpsimd.memset(u_pad[:, :, 0:PU], 0.0).then_inc(pad_zero, 1)
            nc.gpsimd.memset(l_pad[:, :, 0:PL], 0.0).then_inc(pad_zero, 1)

            pool.wait_ge(unit_done, UNIT_AT["z"])
            for n in range(CONV_W):
                if n >= DIAGS[0]:
                    pool.wait_ge(diag_used[0], n - DIAGS[0] + 1)
                nc.gpsimd.tensor_scalar(diag[0][:, n % DIAGS[0], :], ident, V("conv_w", 2 * CONV_W + n), None,
                                        ALU.mult).then_inc(diag_ready[0], 1)
            pool.dma_start(rc, a["router_consts"]).then_inc(rc_in, 16)
            pool.dma_start(b_route, a["b_route"]).then_inc(rc_in, 16)

        @block.tensor
        def _(pe):
            def unit(base, j, i):
                slot = (base + j) % RING
                pe.wait_ge(w_loaded[slot], (turn(j, i, base, RING) + 1) * 16)
                return slot

            def bank(stage, j, i):
                n = BANK_AT[stage] + j
                if n >= 2:
                    pe.wait_ge(bank_free, n - 1 if i is None else i * RING + (n - 1))
                return n % 2

            def split_unit(base, j, i):
                n = split_no(base + j) + 1
                pe.wait_ge(w_split, n if i is None else i * RING + n)
                return split_no(base + j) % 2

            def high(version, kt, first):
                if first:
                    pe.wait_ge(hi_ready, 8 * version + kt + 1)

            def low(version, kt, first):
                if first:
                    pe.wait_ge(lo_ready, 8 * version + kt + 1)

            def as_they_come(slot, outs, version, order=range(KT)):
                for part_h, wait in ((h_hi, high), (h_lo, low)):
                    for n, kt in enumerate(order):
                        wait(version, n, True)
                        for part_w in (w_hi, w_lo) if part_h is h_hi else (w_hi,):
                            for s, out_ap in enumerate(outs):
                                last = nc.tensor.matmul(out_ap, part_w[:, slot, kt * 256 + s * P:kt * 256 + (s + 1) * P],
                                                        part_h[:, kt, :], start=n == 0 and s == 0 and part_w is w_hi and part_h is h_hi,
                                                        stop=n == KT - 1 and part_h is h_lo, skip_group_check=True)
                return last

            def to_features(stage, n_units, version):
                base = UNIT_AT[stage]

                def body(j, i, idx):
                    slot, b = split_unit(base, j, i), bank(stage, j, i)
                    if j == 0:
                        as_they_come(slot, (half(b, 0), half(b, 1)), version).then_inc(unit_done, 1)
                        return
                    w = lambda part, kt, s: part[:, slot, kt * 256 + s * P:kt * 256 + (s + 1) * P]
                    for s in range(2):
                        for kt in range(KT):
                            nc.tensor.matmul(half(b, s), w(w_hi, kt, s), h_hi[:, kt, :], start=kt == 0 and s == 0,
                                             stop=False, skip_group_check=True)
                            nc.tensor.matmul(half(b, s), w(w_lo, kt, s), h_hi[:, kt, :], start=False, stop=False,
                                             skip_group_check=True)
                    for s in range(2):
                        for kt in range(KT):
                            last = nc.tensor.matmul(half(b, s), w(w_hi, kt, s), h_lo[:, kt, :], start=False,
                                                    stop=kt == KT - 1, skip_group_check=True)
                    last.then_inc(unit_done, 1)

                each_unit(pe, n_units, base, body)

            def to_tokens(stage, n_units, version):
                base = UNIT_AT[stage]

                def body(j, i, idx):
                    slot, b = split_unit(base, j, i), bank(stage, j, i)
                    w = lambda part, kt: part[:, slot, kt * 256:(kt + 1) * 256]
                    tok = lambda part, kt, t: part[:, kt, t * P:(t + 1) * P]
                    for t in range(TT):
                        for kt in range(KT):
                            high(version, kt, j == 0 and t == 0)
                            nc.tensor.matmul(half(b, t), tok(h_hi, kt, t), w(w_hi, kt), start=kt == 0 and t == 0,
                                             stop=False, skip_group_check=True)
                            nc.tensor.matmul(half(b, t), tok(h_hi, kt, t), w(w_lo, kt), start=False, stop=False,
                                             skip_group_check=True)
                    for t in range(TT):
                        for kt in range(KT):
                            low(version, kt, j == 0 and t == 0)
                            last = nc.tensor.matmul(half(b, t), tok(h_lo, kt, t), w(w_hi, kt), start=False,
                                                    stop=kt == KT - 1, skip_group_check=True)
                    last.then_inc(unit_done, 1)

                each_unit(pe, n_units, base, body)

            def to_y(stage, version, order=range(KT)):
                base = UNIT_AT[stage]
                for j in range(4):
                    slot = split_unit(base, j, None)
                    if j == 0:
                        as_they_come(slot, (y_ps(0), y_ps(1)), version, order).then_inc(unit_done, 1)
                        continue
                    w = lambda part, kt, s: part[:, slot, kt * 256 + s * P:kt * 256 + (s + 1) * P]
                    for s in range(2):
                        for kt in range(KT):
                            nc.tensor.matmul(y_ps(2 * j + s), w(w_hi, kt, s), h_hi[:, kt, :],
                                             start=kt == 0 and s == 0, stop=False, skip_group_check=True)
                            nc.tensor.matmul(y_ps(2 * j + s), w(w_lo, kt, s), h_hi[:, kt, :], start=False,
                                             stop=False, skip_group_check=True)
                    for s in range(2):
                        for kt in range(KT):
                            last = nc.tensor.matmul(y_ps(2 * j + s), w(w_hi, kt, s), h_lo[:, kt, :], start=False,
                                                    stop=kt == KT - 1, skip_group_check=True)
                    last.then_inc(unit_done, 1)

            def ffn_out(stage, layer):
                base = UNIT_AT[stage]

                def body(j, i, idx):
                    slot = split_unit(base, j, i)
                    pe.wait_ge(act_split, FT * layer + 2 * idx + 2)
                    for s in range(2):
                        tile = lambda part: part[:, bass.ds(idx * 2 + s, 1), :] if i is not None else part[:, 2 * j + s, :]
                        for n in range(KT):
                            w = lambda part: part[:, slot, s * D + n * P:s * D + (n + 1) * P]
                            for part_w, part_a in ((w_hi, act_hi), (w_lo, act_hi), (w_hi, act_lo)):
                                last = nc.tensor.matmul(
                                    y_ps(n), w(part_w), tile(part_a),
                                    start=j == 0 and s == 0 and n % 2 == 0 and part_w is w_hi and part_a is act_hi,
                                    stop=i is None and j == FT // 2 - 1 and s == 1 and part_a is act_lo,
                                    skip_group_check=True)
                    last.then_inc(unit_done, 1)

                each_unit(pe, FT // 2, base, body, peel=1)

            def sum_squares(norm, out_ap, n):
                base = SQ_AT[norm]
                for kt in range(n):
                    pe.wait_ge(sq_ready, base + kt + 1)
                    nc.tensor.matmul(out_ap, ones, sq[:, (base + kt) % SQS, :], start=kt == 0, stop=kt == n - 1).then_inc(sq_used, 1)

            def layer_norm(q):
                for kt in range(KT):
                    pe.wait_ge(resid, 8 * q + kt + 1)
                    last = nc.tensor.matmul(half(2, 0), ones, d[:, kt, :], start=kt == 0, stop=kt == KT - 1)
                last.then_inc(mean_mm, 1)
                sum_squares(f"ln{q}", half(3, 0), KT)

            def attention(layer):
                items = [(0, [2 * i, 2 * i + 1]) for i in range(4)] if layer == 0 else [(1, [i]) for i in range(8)]
                items += [(1, [8 + i]) for i in range(8)]
                item0 = 12 * layer
                map0 = MAPS * layer

                def scores(maps):
                    for m in maps:
                        n = map0 + m
                        if m >= 4:
                            pe.wait_ge(score_rd, n - 3)
                        qt, at = (m // 8) * 8 + (m % 8) // 2, (m % 2) * DH
                        q, k = qk[at:at + DH, qt, :], qk[at:at + DH, qt + 4, :]
                        b = m % 4
                        forget = layer == 1 and m >= 8
                        if forget:
                            pe.wait_ge(fd_head, m - 8 + 1)
                        for dst, tok, keys in ((psum[:, b, 0:256], slice(P, T), T), (psum[:, b, 256:384], slice(0, P), P)):
                            last = nc.tensor.matmul(dst, q[:, tok], k[:, 0:keys], start=True, stop=not forget)
                            if forget:
                                last = nc.tensor.matmul(dst, f_u[at:at + DH, tok], f_vh[m % 2][at:at + DH, 0:keys],
                                                        start=False, stop=True)
                        last.then_inc(score_mm, 1)

                def transposes(i):
                    n = item0 + i
                    s = score[:, items[i][1][0] % 4, :]
                    pe.wait_ge(prob_ready, n + 1)
                    if i >= 2:
                        pe.wait_ge(pt_copied, n - 1)
                    b = 4 + i % 2
                    nc.tensor.transpose(psum[:, b, 0:P], s[:, 256:384], ident)
                    nc.tensor.transpose(psum[:, b, P:2 * P], s[:, 0:P], ident)
                    nc.tensor.transpose(psum[:, b, 2 * P:3 * P], s[:, P:2 * P], ident).then_inc(pt_mm, 1)

                def outputs(i):
                    single, maps = items[i]
                    n = item0 + i
                    pe.wait_ge(pt_copied, n + 1)
                    if i >= 2:
                        pe.wait_ge(o_copied, n - 1)
                    b = 6 + i % 2
                    lo, width, at = (maps[0] * DH, DH, (maps[0] % 2) * DH) if single else (i * P, P, 0)
                    nc.tensor.matmul(psum[at:at + width, b, 0:T], val[:, 0, lo:lo + width], prob_t[:, i % 2, 0:T],
                                     start=True, stop=False)
                    nc.tensor.matmul(psum[at:at + width, b, P:T], val[:, 1, lo:lo + width], prob_t[:, i % 2, T:T + P],
                                     start=False, stop=True).then_inc(o_mm, 1)

                scores(items[0][1])
                scores(items[1][1])
                for i in range(len(items)):
                    if i + 2 < len(items):
                        scores(items[i + 2][1])
                    transposes(i)
                    if i:
                        outputs(i - 1)
                outputs(len(items) - 1)

            pe.wait_ge(consts_in, CONSTS)
            nc.tensor.matmul(psum[0:16, 2, 0:384], table_in, hot_in, start=True, stop=True).then_inc(bias_mm, 1)

            for layer in range(DEPTH):
                version = 3 * layer
                to_tokens(f"v{layer}", 4, version)
                if layer == 1:
                    pe.wait_ge(later_in, LATER)
                    for part in (h_hi, h_lo):
                        for kt in range(KT):
                            last = nc.tensor.matmul(psum[0:8, 3, 0:T], w_forget[:, kt, :], part[:, kt, :].bitcast(F32),
                                                    start=kt == 0 and part is h_hi, stop=kt == KT - 1 and part is h_lo)
                    last.then_inc(fd_mm, 1)
                to_features(f"qk{layer}", 8, version)
                if layer == 1:
                    pe.wait_ge(fd_in, 1)
                else:
                    pe.wait_ge(bias_in, 16)
                    for n in range(2):
                        if n:
                            pe.wait_ge(flipped, 1)
                        for b in range(4):
                            last = nc.tensor.matmul(psum[:, 4 + b, :], flip_in, reversed_rows[:, (4 * n + b) * 512:(4 * n + b + 1) * 512],
                                                    start=True, stop=True)
                        last.then_inc(flip_mm, 1)
                pe.wait_ge(bank_free, BANK_AT[f"qk{layer}"] + 8)
                attention(layer)
                if layer == 0:
                    base = SQ_AT["heads"]
                    for i in range(4):
                        pe.wait_ge(sq_ready, base + i + 1)
                        nc.tensor.matmul(half(2 + i // 2, i % 2), ones, sq[:, (base + i) % SQS, :], start=True,
                                         stop=True).then_inc(sq_used, 1)
                to_y(f"wo{layer}", version + 1, HEADS_LAST if layer == 0 else range(KT))
                layer_norm(2 * layer)
                to_features(f"fi{layer}", 22, version + 2)
                ffn_out(f"fo{layer}", layer)
                layer_norm(2 * layer + 1)

            sum_squares("mix", half(3, 0), KT)
            to_features("z", 8, 6)
            slot = unit(UNIT_AT["ple"], 0, None)
            pe.wait_ge(ple_in, 16)
            for n in range(KT):
                for kt in range(2):
                    last = nc.tensor.matmul(y_ps(n), wring[:, slot, kt * D + n * P:kt * D + (n + 1) * P],
                                            pt_in[:, kt, :], start=kt == 0, stop=kt == 1)
            last.then_inc(unit_done, 1)

            def convolve_tile(k):
                pe.wait_ge(bank_free, BANK_AT["z"] + 8)
                for t in range(CONV_W):
                    pe.wait_ge(diag_ready[k], t + 1)
                    last = nc.tensor.matmul(half(k, 0), diag[k][:, t % DIAGS[k], :], u_pad[:, 2 + k, t:t + T],
                                            start=t == 0, stop=t == CONV_W - 1)
                    last.then_inc(diag_used[k], 1)

            convolve_tile(0)
            sum_squares("ple_proj", half(3, 0), KT)
            pe.wait_ge(blk_in, 64)
            pe.wait_ge(bank_free, BANK_AT["z"] + 8)
            pe.wait_ge(e_copied, 1)
            for g in range(2):
                for j in range(CT):
                    if g == 0:
                        pe.wait_ge(xr_ready, j + 1)
                    last = nc.tensor.matmul(half(4 + 2 * g + j // 2, j % 2), blk_w[:, g, j, :], lru_x[:, j, :],
                                            start=True, stop=True)
                last.then_inc(gates_mm, 1)
            convolve_tile(1)
            pe.wait_ge(conv_done, 4)
            for j in range(CT):
                last = nc.tensor.matmul(half(2, 0), ones, conv[:, j, :], start=j == 0, stop=j == CT - 1)
            last.then_inc(mean_mm, 1)
            sum_squares("conv", half(3, 0), CT)

            to_y("wout", 7, LRU_FIRST)
            sum_squares("ffn", half(3, 0), KT)
            for t in range(TT):
                for kt in range(KT):
                    if t == 0:
                        pe.wait_ge(h_ready, kt + 1)
                    last = nc.tensor.matmul(psum[:, 0, t * 64:t * 64 + 36], h[:, kt, t * P:(t + 1) * P],
                                            w_route[:, kt, :], start=kt == 0, stop=kt == KT - 1)
            last.then_inc(route_mm, 1)
            for b in range(4):
                t, lo = b // 2, (b % 2) * 4
                for k in range(4):
                    last = nc.tensor.transpose(psum[:, 4 + b, k * P:(k + 1) * P],
                                               h[:, lo + k, t * P:(t + 1) * P], ident)
                last.then_inc(tok_mm, 1)
            pe.wait_ge(route_m, 1)
            pe.wait_ge(rc_in, 32)
            hot_m = r_both
            tri = rc[:, RC_TRI:RC_TRI + P]
            nc.tensor.matmul(psum[:, 1, 0:NE], tri, hot_m[:, 0, :], start=True, stop=True)
            nc.tensor.matmul(psum[:, 1, 64:64 + NE], tri, hot_m[:, 1, :], start=True, stop=False)
            nc.tensor.matmul(psum[:, 1, 64:64 + NE], ones, hot_m[:, 0, :], start=False, stop=True)
            nc.tensor.matmul(psum[:, 1, 128:128 + NE], ones, hot_m[:, 0, :], start=True, stop=False)
            nc.tensor.matmul(psum[:, 1, 128:128 + NE], ones, hot_m[:, 1, :], start=False, stop=True).then_inc(rank_mm, 1)

            G, TR = 2, 3

            def gather(n_half, bank_no):
                for k in range(4):
                    kt = 4 * n_half + k
                    for t in range(TT):
                        last = nc.tensor.matmul(psum[:, bank_no, k * P:(k + 1) * P], hf_t(t, kt),
                                                hot_s[:, t, :, :], start=t == 0, stop=t == TT - 1)
                return last

            def scatter(start, stop):
                for n in range(KT):
                    last = nc.tensor.matmul(y_ps(n), y_e[:, n * P:(n + 1) * P], hot_gt,
                                            start=start and n % 2 == 0, stop=stop, skip_group_check=True)
                return last

            pe.wait_ge(tok_copied, 4)
            pe.wait_ge(y1_c, 1)
            pe.wait_ge(sgt_c, 1)
            scatter(True, False)
            pe.wait_ge(routed, 2)
            rounds = pe.value_load(rounds_i[0:1, 0:1], min_val=1, max_val=4)
            pe.wait_ge(s_ready, 1)
            gather(0, G).then_inc(gat0, 1)
            gather(1, TR).then_inc(gat1, 1)
            with pe.Fori(0, rounds) as r:
                with pe.Fori(0, PAIRS // 2) as i:
                    for b in range(2):
                        n = r * PAIRS + (i * 2 + b)
                        pe.wait_ge(gat0_c, n + 1)
                        pe.wait_ge(gat1_c, n + 1)
                        pe.wait_ge(w13_loaded[0], n * 32 + 32)
                        pe.wait_ge(y0_c, n + 1)
                        for w in range(2):
                            if w:
                                pe.wait_ge(w13_loaded[1], n * 32 + 32)
                                pe.wait_ge(y1_c, n + 1)
                            for kt in range(KT):
                                for s in range(2):
                                    last = nc.tensor.matmul(psum[s * CAP:(s + 1) * CAP, w, :],
                                                            xe_t[:, kt, s * CAP:(s + 1) * CAP],
                                                            w13[:, 2 * w + s, kt * FE:(kt + 1) * FE],
                                                            start=kt == 0, stop=kt == KT - 1)
                            last.then_inc((up1, up3)[w], 1)
                        pe.wait_ge(sgt_c, n + 1)
                        scatter(False, False).then_inc(scattered, 1)
                        pe.wait_ge(act_ready, n + 1)
                        for f in range(4):
                            last = nc.tensor.transpose(psum[:, TR, f * P:(f + 1) * P], act_e[:, f * P:(f + 1) * P], ident)
                        last.then_inc(actt_mm, 1)
                        pe.wait_ge(s_ready, n + 2)
                        gather(0, G).then_inc(gat0, 1)
                        pe.wait_ge(actt_c, n + 1)
                        gather(1, TR).then_inc(gat1, 1)
                        pe.wait_ge(sg_ready, n + 1)
                        pe.wait_ge(gat0_c, n + 2)
                        for t in range(TT):
                            last = nc.tensor.transpose(psum[:, G, t * P:(t + 1) * P],
                                                       hot_g[:, t, :, :].rearrange("p e c -> p (e c)"), ident)
                        last.then_inc(sgt_mm, 1)
                        pe.wait_ge(w2_loaded[b], r * (PAIRS // 2 * 32) + (i * 32 + 32))
                        for c in range(2):
                            for f in range(4):
                                for s in range(2):
                                    last = nc.tensor.matmul(psum[s * CAP:(s + 1) * CAP, c, :],
                                                            act_t[:, f, s * CAP:(s + 1) * CAP],
                                                            w2_at[b][:, s * 4096 + f * D + c * 512:s * 4096 + f * D + c * 512 + 512],
                                                            start=f == 0, stop=f == 3)
                            last.then_inc((y0_mm, y1_mm)[c], 1)
            n_all = rounds * PAIRS
            pe.wait_ge(y0_c, n_all + 1)
            pe.wait_ge(y1_c, n_all + 1)
            pe.wait_ge(sgt_c, n_all + 1)
            scatter(False, True).then_inc(scattered, 1)

            for j in range(4):
                pe.wait_ge(pg_split, j + 1)
                pe.wait_ge(x_ready, 41 + 2 * j + 2)
                w = lambda part, kt, s: part[:, j, kt * 256 + s * P:kt * 256 + (s + 1) * P]
                for s in range(2):
                    for kt in range(KT):
                        high(8, kt, j == 0 and s == 0)
                        nc.tensor.matmul(y_ps(2 * j + s), w(pg_hi, kt, s), h_hi[:, kt, :], start=kt == 0 and s == 0,
                                         stop=False, skip_group_check=True)
                        nc.tensor.matmul(y_ps(2 * j + s), w(pg_lo, kt, s), h_hi[:, kt, :], start=False, stop=False,
                                         skip_group_check=True)
                for s in range(2):
                    for kt in range(KT):
                        low(8, kt, j == 0 and s == 0)
                        last = nc.tensor.matmul(y_ps(2 * j + s), w(pg_hi, kt, s), g_lo[:, kt, :], start=False,
                                                stop=kt == KT - 1, skip_group_check=True)
                last.then_inc(unit_done, 1)
                if j == 0:
                    sum_squares("gate", half(3, 0), KT)
            sum_squares("final", half(3, 0), KT)

        @block.scalar
        def _(act):
            Id, Cp = ACT.Identity, ACT.Copy

            def A(out_ap, in_ap, func, **kw):
                return nc.scalar.activation(out_ap, in_ap, func, **kw)

            def square(norm, kt, src):
                g = SQ_AT[norm] + kt
                if g >= SQS:
                    act.wait_ge(sq_used, g - SQS + 1)
                A(sq[:, g % SQS, :], src, ACT.Square).then_inc(sq_ready, 1)

            def deviation(norm, n, features, eps):
                act.wait_ge(sq_used, SQ_AT[norm] + n)
                A(rstd[:], half(3, 0), ACT.Sqrt, scale=1.0 / features, bias=eps).then_inc(std_ready, 1)

            eps_ln, eps_rms = small[:, 60:61], small[:, 61:62]
            act.wait_ge(dve_seq, 1)

            act.dma_start(cb[:], a["c_rows"]).then_inc(silu_c, 16)
            act.wait_ge(silu_c, 16)
            A(cb[:], cb[:], ACT.Silu).then_inc(silu_c, 1)
            act.wait_ge(bias_row, 1)
            act.dma_start(scratch, bias_rows).then_inc(bias_out, 16)
            act.wait_ge(drv_ready, 1)
            act.wait_ge(x_in, 16)
            for kt in range(KT):
                A(h_hi[:, kt, :], x[:, kt, :], Id, scale=small[:, kt:kt + 1], bias=ada[:, 0, kt:kt + 1]).then_inc(hi_ready, 1)
            for k in range(2):
                act.wait_ge(w_loaded[k], 16)
                A(w_hi[:, k, :], wring[:, k, :], Cp).then_inc(w_hi_ready, 1)
            act.wait_ge(bias_out, 16)
            toeplitz = bass.AP(scratch.tensor, 0, [[1, P], [384, 16], [1, 256]])
            act.dma_start(reversed_rows.rearrange("p (n t) -> p n t", t=256), toeplitz).then_inc(bias_in, 16)
            act.wait_ge(lam_sum, 2)
            A(small[:, 12:14], small[:, 10:12], ACT.Exp).then_inc(lam_exp, 1)

            def split(k, i=None):
                if k == PLE or k >= PG:
                    return
                n = split_waits(act, k, i)
                act.wait_ge(w_loaded[k % RING], ((k // RING + 1) if i is None else i + (k // RING + 1)) * 16)
                A(w_hi[:, n % 2, :], wring[:, k % RING, :], Cp).then_inc(w_hi_ready, 1)

            def table_of_sqrt():
                A(small[:, 62:63], eps_ln, ACT.Sqrt)

            def high_parts(src, wait, order=range(KT)):
                for kt in order:
                    wait(kt)
                    A(h_hi[:, kt, :], src[:, kt, :], Cp).then_inc(hi_ready, 1)

            def attention(layer):
                items = [(0, [2 * i, 2 * i + 1]) for i in range(4)] if layer == 0 else [(1, [i]) for i in range(8)]
                items += [(1, [8 + i]) for i in range(8)]

                def exps(maps):
                    for m in maps:
                        act.wait_ge(score_rd, MAPS * layer + m + 1)
                        s = score[:, m % 4, :]
                        A(s[:, 0:256], s[:, 0:256], ACT.Exp, scale=-1.0, bias=mins[:, m, 0:1], accum_out=den[:, m, 0:1])
                        A(s[:, 256:384], s[:, 256:384], ACT.Exp, scale=-1.0, bias=mins[:, m, 1:2],
                          accum_out=den[:, m, 1:2]).then_inc(exp_done, 1)

                exps(items[0][1])
                for i in range(len(items)):
                    n = 12 * layer + i
                    if i + 1 < len(items):
                        exps(items[i + 1][1])
                    act.wait_ge(pt_mm, n + 1)
                    if i >= 2:
                        act.wait_ge(o_mm, n - 1)
                    A(prob_t[:, i % 2, :], psum[:, 4 + i % 2, 0:384], Cp).then_inc(pt_copied, 1)

            def layer_norm(q):
                table_of_sqrt()
                for kt in range(KT):
                    act.wait_ge(centred, 8 * q + kt + 1)
                    square(f"ln{q}", kt, d[:, kt, :])
                deviation(f"ln{q}", KT, D, eps_ln)
                if q < 3:
                    for kt in range(KT):
                        act.wait_ge(normed, 8 * q + kt + 1)
                        A(h_hi[:, kt, :], d[:, kt, :], Id, scale=drv[:, q, 1, kt:kt + 1],
                          bias=drv[:, q, 2, kt:kt + 1]).then_inc(hi_ready, 1)

            for layer in range(DEPTH):
                for j in range(4):
                    act.wait_ge(unit_done, UNIT_AT[f"v{layer}"] + j + 1)
                    A(val[:, :, j * 256:(j + 1) * 256], psum[:, j % 2, :].rearrange("p (a n) -> p a n", a=TT),
                      Cp).then_inc(bank_free, 1)
                    split(UNIT_AT[f"v{layer}"] + j + 2)

                if layer == 1:
                    act.wait_ge(fd_mm, 1)
                    act.wait_ge(later_in, LATER)
                    act.wait_ge(x_ready, 17)
                    A(f_x[0:8, :], psum[0:8, 3, 0:T], Id, bias=fsmall[0:8, 0:1]).then_inc(fd_in, 1)
                    act.wait_ge(fd_in, 1)
                    A(f_e[0:8, :], f_x[0:8, :], ACT.Abs).then_inc(fd_abs, 1)
                    act.wait_ge(fd_abs, 1)
                    A(f_e[0:8, :], f_e[0:8, :], ACT.Exp, scale=-1.0).then_inc(fd_exp, 1)

                def take_qk(j, i, idx, layer=layer):
                    act.wait_ge(unit_done, UNIT_AT[f"qk{layer}"] + idx + 1)
                    dst = (arena[:, bass.ds(idx * 512, 512)] if i is not None else arena[:, j * 512:(j + 1) * 512])
                    A(dst, psum[:, j % 2, :], Cp, scale=-DH ** -0.5 if j % 4 < 2 else 1.0).then_inc(bank_free, 1)
                    split(UNIT_AT[f"qk{layer}"] + j + 2, i)
                each_unit(act, 8, 0, take_qk)
                if layer == 0:
                    for n in range(2):
                        act.wait_ge(flip_mm, n + 1)
                        A(arena2[:, n * 2048:(n + 1) * 2048], psum[:, 4:8, :].rearrange("p b n -> p (b n)"), Cp).then_inc(flipped, 1)
                attention(layer)
                if layer == 0:
                    for i in range(4):
                        if i == 2:
                            table_of_sqrt()
                        act.wait_ge(o_copied, i + 1)
                        square("heads", i, o[:, i, :])
                    for n in range(2):
                        act.wait_ge(sq_used, 2 * n + 2)
                        A(d_flat[:, n * 512:(n + 1) * 512], psum[:, 2 + n, :], ACT.Sqrt, scale=1.0 / P,
                          bias=eps_ln).then_inc((head_std, std_ready)[n], 1)

                def wait_o(kt, layer=layer):
                    if kt in (0, 4):
                        act.wait_ge(o_copied, 28 if layer else 12)
                    if layer == 0 and kt < 4:
                        act.wait_ge(o_ready, kt + 1)
                high_parts(o, wait_o, HEADS_LAST if layer == 0 else range(KT))
                for j in range(4):
                    split(UNIT_AT[f"wo{layer}"] + j + 2)
                layer_norm(2 * layer)

                def gate(j, i, idx, layer=layer):
                    n = BANK_AT[f"fi{layer}"] + j
                    act.wait_ge(unit_done, UNIT_AT[f"fi{layer}"] + idx + 1)
                    if i is not None or j >= 2:
                        act.wait_ge(act_split, FT * layer + idx - 1)
                    A(gate_s[:, j % 2, :], half(j % 2, 0), ACT.Silu).then_inc(gate_done, 1)
                    split(UNIT_AT[f"fi{layer}"] + j + 2, i)
                each_unit(act, 22, 0, gate, peel=2)
                each_unit(act, FT // 2, 0, lambda j, i, idx, layer=layer: split(UNIT_AT[f"fo{layer}"] + j + 2, i), peel=1)
                layer_norm(2 * layer + 1)

            table_of_sqrt()
            for kt in range(KT):
                act.wait_ge(x_ready, 25 + kt + 1)
                square("mix", kt, x[:, kt, :])
            deviation("mix", KT, D, eps_rms)
            high_parts(h_lo32, lambda kt: act.wait_ge(h_whole, kt + 1))
            A(small[:, 28:32], V("lam", 0, 4), ACT.Abs).then_inc(lru_abs, 1)
            act.wait_ge(lru_abs, 1)
            A(small[:, 28:32], small[:, 28:32], ACT.Exp, scale=-1.0).then_inc(lru_abs, 1)
            act.wait_ge(pad_zero, 2)
            for j in range(8):
                act.wait_ge(unit_done, UNIT_AT["z"] + j + 1)
                if j < 4:
                    if j >= 2:
                        act.wait_ge(bank_free, BANK_AT["z"] + j - 1)
                    A(gate_s[:, j % 2, :], half(j % 2, 1), ACT.Sigmoid).then_inc(gate_done, 1)
                else:
                    act.wait_ge(bank_free, BANK_AT["z"] + 4)
                    A(l_pad[:, j - 4, PL:PL + T], half(j % 2, 0), Cp)
                    A(lru_g[:, j - 4, :], half(j % 2, 1), ACT.Gelu_apprx_tanh).then_inc(bank_free, 1)
                split(UNIT_AT["z"] + j + 2)
            split(UNIT_AT["wout"] + 1)

            def diagonals(lo, hi):
                for t in range(lo, hi):
                    if t >= DIAGS[1]:
                        act.wait_ge(diag_used[1], t - DIAGS[1] + 1)
                    A(diag[1][:, t % DIAGS[1], :], ident, Cp, scale=V("conv_w", 3 * CONV_W + t)).then_inc(diag_ready[1], 1)

            diagonals(0, DIAGS[1])
            act.wait_ge(unit_done, UNIT_AT["ple"] + 1)
            act.wait_ge(ada_done, ADA_PIECES)
            A(aring[:, 0, :], psum[:, 4:8, :].rearrange("p b n -> p (b n)"), Cp).then_inc(e_copied, 1)
            act.wait_ge(e_copied, 1)
            for kt in range(KT):
                square("ple_proj", kt, ple_e[:, kt, :])
            deviation("ple_proj", KT, D, eps_rms)
            for g in range(2):
                act.wait_ge(gates_mm, g + 1)
                for j in range(CT):
                    ins = A((g_r, g_i)[g][:, j, :], half(4 + 2 * g + j // 2, j % 2), ACT.Sigmoid,
                            bias=V("b_i" if g else "b_r", j))
                ins.then_inc(gates_act, 1)
            act.wait_ge(lru_l, 1)
            A(t_b, t_a, ACT.Tanh).then_inc(lru_t, 1)
            A(g_r, t_a, ACT.Exp, scale=-1.0).then_inc(lru_t, 1)
            for k in range(2):
                if k:
                    diagonals(DIAGS[1], 20)
                    act.wait_ge(lru_u, 1)
                    A(t_a, t_b, ACT.Sqrt).then_inc(lru_t, 1)
                    diagonals(20, CONV_W)
                act.wait_ge(diag_used[k], CONV_W)
                A(conv[:, 2 + k, :], half(k, 0), Id, bias=V("conv_b", 2 + k)).then_inc(conv_done, 1)
            act.wait_ge(lru_u, 8)
            high_parts(cat, lambda kt: None, LRU_FIRST[0:4])
            for j in range(CT):
                act.wait_ge(conv_norm, j + 1)
                square("conv", j, conv[:, j, :])
            deviation("conv", CT, 512, eps_rms)
            for j in range(CT):
                act.wait_ge(conv_norm, 4 + j + 1)
                A(cat[:, j, :], conv[:, j, :], ACT.Silu, scale=V("conv_ln_g", j), bias=V("conv_ln_b", j)).then_inc(cat_ready, 1)

            high_parts(cat, lambda kt: act.wait_ge(cat_ready, kt + 1), LRU_FIRST[4:8])
            split(UNIT_AT["wout"] + 2)
            split(UNIT_AT["wout"] + 3)
            table_of_sqrt()
            for kt in range(KT):
                act.wait_ge(x_ready, 33 + kt + 1)
                square("ffn", kt, x[:, kt, :])
            deviation("ffn", KT, D, eps_rms)
            A(small[:, 62:63], eps_ln, ACT.Exp)
            act.wait_ge(y0_c, 1)
            A(y_e[:, 512:1024], y_e[:, 0:512], Cp).then_inc(y1_c, 1)
            A(hot_gt, y_e[:, 0:256], Cp).then_inc(sgt_c, 1)
            for b in range(2):
                act.wait_ge(tok_mm, 2 * b + 2)
                A(d_flat[:, b * 1024:(b + 1) * 1024], psum[:, 4 + 2 * b:6 + 2 * b, :].rearrange("p b n -> p (b n)"),
                  Cp).then_inc(tok_copied, 2)
            act.wait_ge(route_d, 1)
            A(r_gwork, r_gwork, ACT.Exp).then_inc(route_exp, 1)
            act.wait_ge(route_d, 2)
            A(r_s[:, 6, :], r_s[:, 5, :], ACT.Exp).then_inc(route_exp, 1)

            act.wait_ge(routed, 2)
            rounds = act.value_load(rounds_i[0:1, 0:1], min_val=1, max_val=4)
            act.wait_ge(gat0, 1)
            A(arena2[:, 0:512], psum[:, 2, :], Cp).then_inc(gat0_c, 1)
            with act.Fori(0, rounds) as r:
                with act.Fori(0, PAIRS) as p:
                    n = r * PAIRS + p
                    act.wait_ge(up1, n + 1)
                    A(silu1, psum[:, 0, :], ACT.Silu).then_inc(silu_e, 1)
                    act.wait_ge(actt_mm, n + 1)
                    A(arena2[:, 2816:3328], psum[:, 3, :], Cp).then_inc(actt_c, 1)
                    act.wait_ge(gat0, n + 2)
                    A(arena2[:, 0:512], psum[:, 2, :], Cp).then_inc(gat0_c, 1)
                    act.wait_ge(sgt_mm, n + 1)
                    A(hot_gt, psum[:, 2, 0:256], Cp).then_inc(sgt_c, 1)
                    act.wait_ge(y1_mm, n + 1)
                    A(y_e[:, 512:1024], psum[:, 1, :], Cp).then_inc(y1_c, 1)
            n_all = rounds * PAIRS

            def split_pg(j):
                act.wait_ge(w_loaded[(PG + j) % RING], ((PG + j) // RING + 1) * 16)
                A(pg_hi[:, j, :], pg_in(j), Cp).then_inc(pg_hi_ready, 1)

            act.wait_ge(up1, n_all)
            split_pg(0)
            split_pg(1)
            for kt in range(KT):
                act.wait_ge(x_ready, 41 + kt + 1)
                A(h_hi[:, kt, :], x[:, kt, :], Cp, scale=V("g_ple", kt)).then_inc(hi_ready, 1)
            split_pg(2)
            split_pg(3)
            table_of_sqrt()
            for kt in range(KT):
                square("gate", kt, x[:, kt, :])
            deviation("gate", KT, D, eps_rms)

            def final_squares(n):
                for kt in (2 * n, 2 * n + 1):
                    act.wait_ge(x_ready, 49 + kt + 1)
                    square("final", kt, x[:, kt, :])

            for n in range(4):
                act.wait_ge(gate_scaled, n + 1)
                A(d_flat[:, n * 512:(n + 1) * 512], d_flat[:, n * 512:(n + 1) * 512], ACT.Sigmoid).then_inc(gate_done, 1)
                if n == 3:
                    table_of_sqrt()
                if n:
                    final_squares(n - 1)
            final_squares(3)
            deviation("final", KT, D, eps_rms)

        @block.vector
        def _(dve):
            seq = [0]
            v = nc.vector

            def link(ins):
                seq[0] += 1
                ins.then_inc(dve_seq, 1)
                dve.wait_ge(dve_seq, seq[0])

            def stt(out_ap, in0, scalar, in1, op0, op1):
                return v.scalar_tensor_tensor(out_ap, in0, scalar, in1, op0, op1)

            def ada_piece(k, slot, turn_, cols, bias_cols):
                if turn_ is None:
                    dve.wait_ge(staged_in[k], 16)
                else:
                    dve.wait_ge(a_loaded[slot], (turn_ + (1 - STAGED // ARING)) * 16)
                for t in range(2):
                    w = (staged(k) if turn_ is None else aring[:, slot, :])[:, t * D:(t + 1) * D]
                    v.tensor_tensor_reduce(out=w, in0=w, in1=cb[:], scale=1.0, scalar=0.0, op0=ALU.mult, op1=ALU.add,
                                           accum_out=ada_raw[:, 2 * slot + t:2 * slot + t + 1]).then_inc(ada_sum, 1)
                dve.wait_ge(ada_sum, k * 2 + 2)
                v.tensor_tensor(cols, ada_raw[:, 2 * slot:2 * slot + 2], bias_cols, ALU.add).then_inc(ada_done, 1)

            ada_cols = ada[:].rearrange("p l n -> p (l n)")

            def pieces(lo, hi):
                for k in range(lo, hi):
                    ada_piece(k, k % 2, None if k < STAGED else k // 2, ada_cols[:, 2 * k:2 * k + 2], V("b_ada", 2 * k, 2))

            def split(k, i=None):
                if k == PLE or k >= PG:
                    return
                n = split_waits(dve, k, i)
                dve.wait_ge(w_hi_ready, n + 1 if i is None else i * RING + (n + 1))
                v.tensor_tensor(w_lo[:, n % 2, :], wring[:, k % RING, :], w_hi[:, n % 2, :].bitcast(F32),
                                ALU.subtract).then_inc(w_split, 1)

            def low_parts(version, src, tiles=range(KT), before=0):
                for n, kt in enumerate(tiles):
                    dve.wait_ge(hi_ready, 8 * version + before + n + 1)
                    v.tensor_tensor(h_lo[:, kt, :], src[:, kt, :], h_hi[:, kt, :].bitcast(F32), ALU.subtract).then_inc(lo_ready, 1)

            def scaled_low_parts(version, src, scale, shift):
                for kt in range(KT):
                    seq[0] += 1
                    v.tensor_scalar(h_lo32[:, kt, :], src[:, kt, :], scale[:, kt:kt + 1], shift[:, kt:kt + 1], ALU.mult,
                                    ALU.add).then_inc(dve_seq, 1)
                for kt in range(KT):
                    dve.wait_ge(dve_seq, seq[0] - KT + kt + 1)
                    dve.wait_ge(hi_ready, 8 * version + kt + 1)
                    v.tensor_tensor(h_lo[:, kt, :], h_lo32[:, kt, :], h_hi[:, kt, :].bitcast(F32), ALU.subtract).then_inc(lo_ready, 1)

            def piece_at(k, i, step=RING // 2):
                if i is None:
                    return pieces(k, k + 1)
                ada_piece(i * step + k, k % 2, i * (step // 2) + k // 2, ada_cols[:, bass.ds(i * (2 * step) + 2 * k, 2)],
                          vec[:, bass.ds(i * (2 * step) + (VEC_AT["b_ada"] + 2 * k), 2)])

            def derive(q):
                layer = q // 2
                part = lambda l, n: ada[:, l, 8 * n:8 * n + 8]
                g, b = V("ln_g", 8 * q, 8), V("ln_b", 8 * q, 8)
                dve.wait_ge(ada_done, (20, 32, 44, 48)[q])
                link(v.tensor_scalar(drv[:, q, 0, :], part(layer, 5 if q % 2 else 2), 1.0, None, ALU.add))
                if q < 3:
                    l, sc, sh = ((0, 4, 3), (1, 1, 0), (1, 4, 3))[q]
                    link(stt(drv[:, q, 1, :], part(l, sc), 1.0, g, ALU.add, ALU.mult))
                    link(stt(drv[:, q, 2, :], part(l, sc), 1.0, b, ALU.add, ALU.mult))
                    link(v.tensor_tensor(drv[:, q, 2, :], drv[:, q, 2, :], part(l, sh), ALU.add))
                alpha = ALPHA if q < 3 else 1.0
                link(v.tensor_scalar(drv[:, q, 3, :], g, alpha, None, ALU.mult))
                v.tensor_scalar(drv[:, q, 4, :], b, alpha, None, ALU.mult).then_inc(drv_ready, 1)
                dve.wait_ge(drv_ready, q + 2)

            def log1p_start(y, z, w, s):
                link(v.tensor_scalar(z, y, 2.0, None, ALU.add))
                link(v.reciprocal(z, z))
                link(v.tensor_tensor(z, z, y, ALU.mult))
                link(v.tensor_tensor(w, z, z, ALU.mult))
                link(v.tensor_scalar(s, w, 1.0 / 17, None, ALU.mult))

            def log1p_terms(w, s, ns):
                for n in ns:
                    link(stt(s, s, 1.0 / n, w, ALU.add, ALU.mult))

            def log1p(y, z, w, s):
                log1p_start(y, z, w, s)
                log1p_terms(w, s, (15, 13, 11, 9, 7, 5, 3))
                link(stt(s, s, 1.0, z, ALU.add, ALU.mult))

            link(v.memset(small[:, 60:61], LN_EPS))
            link(v.memset(small[:, 61:62], RMS_EPS))
            dve.wait_ge(bias_mm, 1)
            dve.wait_ge(consts_in, CONSTS)
            stt(bias_rows, psum[0:16, 2, 0:384], -1.0, added_in, ALU.mult, ALU.add).then_inc(bias_row, 1)
            dve.wait_ge(silu_c, 17)
            pieces(0, 8)
            dve.wait_ge(ada_done, 8)
            v.tensor_scalar(small[:, 0:8], ada[:, 0, 8:16], 1.0, None, ALU.add).then_inc(drv_ready, 1)
            dve.wait_ge(drv_ready, 1)
            dve.wait_ge(x_in, 16)
            scaled_low_parts(0, x, small[:, 0:8], ada[:, 0, 0:8])
            split(0)
            split(1)
            dve.wait_ge(later_in, LATER)
            for n in range(2):
                l0, l1 = lam_in[:, 128 * n:128 * n + 64], lam_in[:, 128 * n + 64:128 * n + 128]
                v.tensor_tensor_reduce(out=l0, in0=l0, in1=l1, scale=1.0, scalar=0.0, op0=ALU.mult, op1=ALU.add,
                                       accum_out=small[:, 10 + n:11 + n]).then_inc(lam_sum, 1)
            for j in range(12):
                split(UNIT_AT["v0"] + j + 2)
                if j in QKV_PIECES:
                    k = 8 + QKV_PIECES.index(j)
                    pieces(k, k + 1)
            pieces(16, 18)
            dve.wait_ge(lam_exp, 1)
            link(v.tensor_tensor(small[:, 14:15], small[:, 13:14], small[:, 12:13], ALU.subtract))
            link(v.tensor_scalar(small[:, 14:15], small[:, 14:15], -LAMBDA_INIT, None, ALU.add))
            link(v.tensor_scalar(small[:, 15:16], V("subln_g"), 1.0 - LAMBDA_INIT, None, ALU.mult))

            def attention(layer):
                items = [(0, [2 * i, 2 * i + 1]) for i in range(4)] if layer == 0 else [(1, [i]) for i in range(8)]
                items += [(1, [8 + i]) for i in range(8)]
                item_of = {m: i for i, (_, maps) in enumerate(items) for m in maps}

                def head_operand(hd):
                    if hd >= 2:
                        dve.wait_ge(score_mm, MAPS * layer + 8 + hd - 1)
                    v.tensor_scalar(f_vh[hd % 2], f_v, fsmall[:, 1 + hd:2 + hd], None,
                                    ALU.mult).then_inc(fd_head, 1)

                def shift(maps):
                    for m in maps:
                        n = MAPS * layer + m
                        dve.wait_ge(score_mm, n + 1)
                        if m >= 4:
                            dve.wait_ge(pt_mm, 12 * layer + item_of[m - 4] + 1)
                        if m < 8:
                            bt = bias[:, m // 2 if layer == 0 else m, :]
                        else:
                            bt = bias[:, m if layer == 0 else 16, :]
                        s, b = score[:, m % 4, :], m % 4
                        v.tensor_tensor_reduce(out=s[:, 0:256], in0=psum[:, b, 0:256], in1=bt, scale=1.0,
                                               scalar=3e38, op0=ALU.add, op1=ALU.min, accum_out=mins[:, m, 0:1])
                        v.tensor_tensor_reduce(out=s[:, 256:384], in0=psum[:, b, 256:384], in1=bt[:, P:2 * P],
                                               scale=1.0, scalar=3e38, op0=ALU.add, op1=ALU.min,
                                               accum_out=mins[:, m, 1:2]).then_inc(score_rd, 1)

                def normalise(i, single, maps):
                    m = maps[-1]
                    n = 12 * layer + i
                    dve.wait_ge(exp_done, MAPS * layer + m + 1)
                    s = score[:, maps[0] % 4, :]
                    if single:
                        link(v.reciprocal(den[:, m, :], den[:, m, :]))
                        v.tensor_scalar(s[:, 0:256], s[:, 0:256], den[:, m, 0:1], None, ALU.mult)
                        v.tensor_scalar(s[:, 256:384], s[:, 256:384], den[:, m, 1:2], None, ALU.mult).then_inc(prob_ready, 1)
                    else:
                        s1, m0 = score[:, m % 4, :], maps[0]
                        link(v.reciprocal(den[:, m0:m + 1, :], den[:, m0:m + 1, :]))
                        link(v.tensor_scalar(den[:, m, :], den[:, m, :], small[:, 14:15], None, ALU.mult))
                        v.tensor_scalar(s1[:, 0:256], s1[:, 0:256], den[:, m, 0:1], None, ALU.mult)
                        link(v.tensor_scalar(s1[:, 256:384], s1[:, 256:384], den[:, m, 1:2], None, ALU.mult))
                        stt(s[:, 0:256], s[:, 0:256], den[:, m0, 0:1], s1[:, 0:256], ALU.mult, ALU.add)
                        stt(s[:, 256:384], s[:, 256:384], den[:, m0, 1:2], s1[:, 256:384], ALU.mult,
                            ALU.add).then_inc(prob_ready, 1)

                def take_o(i, single, maps):
                    dve.wait_ge(o_mm, 12 * layer + i + 1)
                    tile, at, width = (maps[0] // 2, (maps[0] % 2) * DH, DH) if single else (i, 0, P)
                    v.tensor_copy(o[at:at + width, tile, :], psum[at:at + width, 6 + i % 2, 0:T]).then_inc(o_copied, 1)

                shift(items[0][1])
                for i, (single, maps) in enumerate(items):
                    if i + 1 < len(items):
                        shift(items[i + 1][1])
                        ahead = items[i + 1][1][0] + 2
                        if layer == 1 and 8 <= ahead < MAPS:
                            head_operand(ahead - 8)
                    normalise(i, single, maps)
                    if i >= 2:
                        take_o(i - 2, *items[i - 2])
                for i in (len(items) - 2, len(items) - 1):
                    take_o(i, *items[i])

            def invert(norm):
                dve.wait_ge(std_ready, NORM_NO[norm] + 1)
                link(v.reciprocal(rstd[:], rstd[:]))

            H_BEFORE = (2, 3, 5, 6)

            def residual(q, tiles):
                for kt in tiles:
                    if q % 2 == 0:
                        dve.wait_ge(unit_done, UNIT_AT[f"wo{q // 2}"] + kt // 2 + 1)
                    stt(d[:, kt, :], y_ps(kt), drv[:, q, 0, kt:kt + 1], x[:, kt, :], ALU.mult, ALU.add).then_inc(resid, 1)

            def layer_norm(q):
                dve.wait_ge(x_ready, 1 + 8 * q)
                dve.wait_ge(hi_ready, 8 * H_BEFORE[q])
                if q % 2:
                    dve.wait_ge(unit_done, UNIT_AT[f"fo{q // 2}"] + 11)
                    residual(q, range(KT))
                    next_unit = UNIT_AT[f"fo{q // 2}"] + FT // 2
                else:
                    next_unit = UNIT_AT[f"wo{q // 2}"] + 4
                    residual(q, (0, 1))
                    split(next_unit)
                    residual(q, range(2, KT))
                dve.wait_ge(mean_mm, q + 1)
                for kt in range(KT):
                    stt(d[:, kt, :], half(2, 0), -1.0 / D, d[:, kt, :], ALU.mult, ALU.add).then_inc(centred, 1)
                split(next_unit + 1)
                invert(f"ln{q}")
                for kt in range(KT):
                    v.tensor_tensor(d[:, kt, :], d[:, kt, :], rstd[:], ALU.mult).then_inc(normed, 1)
                if q < 3:
                    dve.wait_ge(normed, 8 * q + 8)
                    scaled_low_parts(H_BEFORE[q], d, drv[:, q, 1, :], drv[:, q, 2, :])

            def rms(norm, src, gain, dst, signal):
                invert(norm)
                times_gain(src, gain, dst, signal)

            def times_gain(src, gain, dst, signal):
                for kt in range(KT):
                    stt(dst[:, kt, :], src[:, kt, :], V(gain, kt), rstd[:], ALU.mult, ALU.mult).then_inc(signal, 1)

            f8 = lambda ap: ap[0:8, :]

            def forget_step(j):
                y, z, w, s = f8(f_e), f8(f_z), f8(f_w), f8(f_vh[0])
                if j == 2:
                    dve.wait_ge(fd_exp, 1)
                    log1p_start(y, z, w, s)
                elif 3 <= j <= 6:
                    log1p_terms(w, s, ((15, 13), (11, 9), (7, 5), (3,))[j - 3])
                elif j == 7:
                    link(stt(s, s, 1.0, z, ALU.add, ALU.mult))
                    link(v.tensor_scalar(f8(f_x), f8(f_x), 0.0, None, ALU.min))
                    link(stt(f8(f_x), s, -2.0, f8(f_x), ALU.mult, ALU.add))
                elif j == 8:
                    link(v.memset(f_u, 0.0))
                    link(v.memset(f_v, 0.0))
                    link(v.memset(z, 1.0))
                    link(v.tensor_tensor_scan(f8(f_u), z, f8(f_x), 0.0, ALU.mult, ALU.add))
                elif j in (9, 10):
                    at = 32 if j == 9 else 96
                    link(v.tensor_copy(f_v[at:at + 8, :], f8(f_u)))
                    link(v.memset(f_u[at:at + 8, :], 1.0))
                    link(v.memset(f_v[at - 32:at - 24, :], -1.0))
                elif j == 11:
                    link(v.tensor_copy(f_u[64:72, :], f8(f_u)))

            for layer in range(DEPTH):
                if layer == 1:
                    for j in range(12):
                        if j < 11:
                            split(UNIT_AT["v1"] + j + 2)
                        if j < 8:
                            pieces(36 + j, 37 + j)
                        forget_step(j)
                else:
                    dve.wait_ge(flipped, 2)
                attention(layer)
                if layer == 0:
                    for i in range(4):
                        dve.wait_ge((head_std, std_ready)[i // 2], 1)
                        link(v.reciprocal(d[:, i, :], d[:, i, :]))
                        stt(o[:, i, :], o[:, i, :], small[:, 15:16], d[:, i, :], ALU.mult, ALU.mult).then_inc(o_ready, 1)
                        if i == 0:
                            low_parts(1, o, HEADS_LAST[0:4])
                        else:
                            low_parts(1, o, (i - 1,), 4 + i - 1)
                    low_parts(1, o, (3,), 7)
                else:
                    low_parts(4, o)
                    split(UNIT_AT["wo1"] + 1)
                for j in range(2):
                    split(UNIT_AT[f"wo{layer}"] + j + 2)
                    if layer == 0:
                        pieces(18 + j, 19 + j)
                derive(2 * layer)
                layer_norm(2 * layer)

                def gated(j, i, idx, layer=layer):
                    dve.wait_ge(gate_done, 22 * layer + idx + 1)
                    tile = lambda part: part[:, bass.ds(idx, 1), :] if i is not None else part[:, j, :]
                    n = FT * layer + idx
                    v.tensor_tensor(gate_s[:, j % 2, :], gate_s[:, j % 2, :], half(j % 2, 1), ALU.mult).then_inc(bank_free, 1)
                    dve.wait_ge(bank_free, BANK_AT[f"fi{layer}"] + idx + 1)
                    v.tensor_copy(tile(act_hi), gate_s[:, j % 2, :]).then_inc(act_high, 1)
                    dve.wait_ge(act_high, n + 1)
                    v.tensor_tensor(tile(act_lo), gate_s[:, j % 2, :], tile(act_hi).bitcast(F32), ALU.subtract).then_inc(act_split, 1)
                    split(UNIT_AT[f"fi{layer}"] + j + 2, i)
                    if layer == 0 and j % 2 == 0:
                        piece_at(20 + j // 2, i)
                    if layer == 1 and j < 2:
                        pieces(44 + j, 45 + j)
                each_unit(dve, FT, 0, gated, peel=2)

                def behind_ffn_out(j, i, idx, layer=layer):
                    if j < FT // 2 - 1:
                        split(UNIT_AT[f"fo{layer}"] + j + 2, i)
                    if layer == 0 and j in (0, 2, 4):
                        piece_at({0: 31, 2: 32, 4: 33}[j], i)
                    if layer == 1 and j in (0, 9):
                        pieces(46 + j // 9, 47 + j // 9)
                    if j == 9:
                        derive(2 * layer + 1)
                each_unit(dve, FT // 2, 0, behind_ffn_out, peel=1)
                layer_norm(2 * layer + 1)

            rms("mix", x, "g_mix", h_lo32, h_whole)
            dve.wait_ge(h_whole, 8)
            low_parts(6, h_lo32)
            dve.wait_ge(lru_abs, 2)
            log1p(small[:, 28:32], small[:, 32:36], small[:, 36:40], small[:, 40:44])
            link(v.tensor_scalar(small[:, 20:24], V("lam", 0, 4), -1.0, 0.0, ALU.mult, ALU.max))
            link(stt(small[:, 20:24], small[:, 40:44], 2.0, small[:, 20:24], ALU.mult, ALU.add))
            link(v.tensor_scalar(small[:, 20:24], small[:, 20:24], 8.0, None, ALU.mult))
            dve.wait_ge(pad_zero, 2)
            for j in range(CT):
                dve.wait_ge(gate_done, 44 + j + 1)
                v.tensor_tensor(u_pad[:, j, PU:PU + T], gate_s[:, j % 2, :], half(j % 2, 0), ALU.mult).then_inc(bank_free, 1)
                split(UNIT_AT["z"] + j + 2)
            dve.wait_ge(bank_free, BANK_AT["z"] + 4)
            convolve(dve, v, (0, 1), dve_taps, between=lambda t: split(UNIT_AT["z"] + 6 + t // 8) if t in (4, 12) else None)
            split(UNIT_AT["wout"])
            split(UNIT_AT["wout"] + 1)
            dve.wait_ge(bank_free, BANK_AT["z"] + 8)
            for j in range(CT):
                for t in range(LRU_W):
                    w = V("lru_w", j * LRU_W + t)
                    if t:
                        ins = stt(lru_x[:, j, :], l_pad[:, j, t:t + T], w, lru_x[:, j, :], ALU.mult, ALU.add)
                    else:
                        ins = v.tensor_scalar(lru_x[:, j, :], l_pad[:, j, 0:T], w, V("lru_b", j), ALU.mult, ALU.add)
                    if t < LRU_W - 1:
                        link(ins)
                    else:
                        ins.then_inc(xr_ready, 1)
            invert("ple_proj")
            dve.wait_ge(gates_act, 1)
            for j in range(CT):
                ins = v.tensor_scalar(t_a[:, j, :], g_r[:, j, :], small[:, 20 + j:21 + j], None, ALU.mult)
            ins.then_inc(lru_l, 1)
            times_gain(ple_e, "g_ple_proj", ple_e, ple_scaled)
            dve.wait_ge(lru_t, 2)
            link(v.tensor_tensor(t_c, g_r, g_r, ALU.mult))
            stt(t_b, t_c, 1.0, t_b, ALU.add, ALU.mult).then_inc(lru_u, 1)
            dve.wait_ge(gates_act, 2)
            v.tensor_tensor(g_i, g_i, lru_x, ALU.mult).then_inc(lru_u, 1)
            dve.wait_ge(lru_t, 3)
            dve.wait_ge(lru_u, 2)
            v.tensor_tensor(t_b, t_a, g_i, ALU.mult).then_inc(lru_u, 1)
            dve.wait_ge(lru_u, 3)
            for j in range(CT):
                link(v.tensor_tensor_scan(t_c[:, j, :], g_r[:, j, :], t_b[:, j, :], 0.0, ALU.mult, ALU.add))
            v.tensor_tensor(cat[:, CT:2 * CT, :], t_c, lru_g, ALU.mult).then_inc(lru_u, 5)
            low_parts(7, cat, LRU_FIRST[0:4])
            dve.wait_ge(mean_mm, 5)
            for j in range(CT):
                stt(conv[:, j, :], half(2, 0), -1.0 / 512, conv[:, j, :], ALU.mult, ALU.add).then_inc(conv_norm, 1)
            invert("conv")
            for j in range(CT):
                v.tensor_tensor(conv[:, j, :], conv[:, j, :], rstd[:], ALU.mult).then_inc(conv_norm, 1)
            low_parts(7, cat, LRU_FIRST[4:8], 4)
            split(UNIT_AT["wout"] + 2)
            split(UNIT_AT["wout"] + 3)
            for kt in range(KT):
                dve.wait_ge(unit_done, UNIT_AT["wout"] + kt // 2 + 1)
                v.tensor_tensor(x[:, kt, :], x[:, kt, :], y_ps(kt), ALU.add).then_inc(x_ready, 1)
            rms("ffn", x, "g_ffn", h, h_ready)

            v.memset(y_e[:, 0:512], 0.0).then_inc(y0_c, 1)
            dve.wait_ge(rc_in, 32)
            dve.wait_ge(route_mm, 1)
            tiles = lambda ap, n: ap.unsqueeze(1).to_broadcast([P, TT, n])
            along = lambda ap, n: ap.unsqueeze(2).to_broadcast([P, TT, n])
            S = lambda i: r_s[:, i, :]
            w4, w32 = rc[:, RC_W4:RC_W4 + NG], rc[:, RC_W32:RC_W32 + NE]

            def first_max(values, best, n, weights, work, hot):
                link(v.tensor_reduce(best, values, AX_X, ALU.max))
                link(v.tensor_tensor(work, values, along(best, n), ALU.is_equal))
                link(v.tensor_tensor(work, work, tiles(weights, n), ALU.mult))
                link(v.tensor_reduce(S(10), work, AX_X, ALU.max))
                link(v.tensor_tensor(hot, work, along(S(10), n), ALU.is_equal))

            link(v.tensor_tensor(r_logit, psum[:, 0, 0:128].rearrange("p (a n) -> p a n", a=TT)[:, :, 0:36],
                                 tiles(b_route, 36), ALU.add))
            gl, el = r_logit[:, :, 0:NG], r_logit[:, :, NG:NG + NE]
            first_max(gl, S(0), NG, w4, r_gwork, r_ghot)
            v.tensor_tensor(r_gwork, gl, along(S(0), NG), ALU.subtract).then_inc(route_d, 1)
            link(v.tensor_scalar(r_pen, r_ghot, -1.0, 1e30, ALU.add, ALU.mult))
            for t in range(TT):
                link(v.tensor_tensor(r_el[:, t, :].rearrange("p (g e) -> p g e", g=NG),
                                     el[:, t, :].rearrange("p (g e) -> p g e", g=NG),
                                     r_pen[:, t, :].unsqueeze(2).to_broadcast([P, NG, EPG]), ALU.add))
            first_max(r_el, S(3), NE, w32, r_work, r_first)
            link(stt(r_el, r_first, -1e30, r_el, ALU.mult, ALU.add))
            first_max(r_el, S(4), NE, w32, r_work, r_hot_m)
            v.tensor_tensor(S(5), S(4), S(3), ALU.subtract).then_inc(route_d, 1)
            v.tensor_tensor(r_both, r_hot_m, r_first, ALU.add).then_inc(route_m, 1)
            dve.wait_ge(route_m, 1)
            dve.wait_ge(route_exp, 1)
            link(v.tensor_reduce(S(1), r_gwork, AX_X, ALU.add))
            link(v.reciprocal(S(1), S(1)))
            dve.wait_ge(route_exp, 2)
            link(v.tensor_scalar(S(7), S(6), 1.0, None, ALU.add))
            link(v.reciprocal(S(7), S(7)))
            link(v.tensor_tensor(S(7), S(7), S(1), ALU.mult))
            link(v.tensor_tensor(S(8), S(7), S(6), ALU.mult))
            link(v.tensor_tensor(r_gate, r_first, along(S(7), NE), ALU.mult))
            link(v.tensor_tensor(r_work, r_hot_m, along(S(8), NE), ALU.mult))
            link(v.tensor_tensor(r_gate, r_gate, r_work, ALU.add))
            link(v.tensor_scalar(r_work, r_both, -1.0, 1e6, ALU.add, ALU.mult))
            dve.wait_ge(rank_mm, 1)
            for t in range(TT):
                link(v.tensor_tensor(r_rank[:, t, 0:NE], psum[:, 1, t * 64:t * 64 + NE], r_both[:, t, :], ALU.mult))
            link(v.tensor_tensor(r_rank[:, :, 0:NE], r_rank[:, :, 0:NE], r_work, ALU.add))
            link(v.tensor_scalar(r_rank[:, :, NE:NE + 2], r_rank[:, :, 0:2], -float(CAP), None, ALU.add))
            link(v.tensor_reduce(r_s[:, 11, 0:1], psum[:, 1, 128:128 + NE], AX_X, ALU.max))
            link(v.tensor_scalar(r_s[:, 12, 0:1], r_s[:, 11, 0:1], float(CAP), 1.0, ALU.is_gt, ALU.add))
            for n in (2, 3):
                link(v.tensor_scalar(r_s[:, 13, 0:1], r_s[:, 11, 0:1], float(n * CAP), None, ALU.is_gt))
                link(v.tensor_tensor(r_s[:, 12, 0:1], r_s[:, 12, 0:1], r_s[:, 13, 0:1], ALU.add))
            link(v.tensor_copy(rounds_i[:], r_s[:, 12, 0:1]))
            dve.sem_inc(routed, 2)
            rounds = dve.value_load(rounds_i[0:1, 0:1], min_val=1, max_val=4)

            slots4 = rc[:, RC_SLOT:RC_SLOT + CAP].unsqueeze(1).to_broadcast([P, 2, CAP])

            def choose(first):
                for t in range(TT):
                    rank = r_rank[:, t, first].unsqueeze(2).to_broadcast([P, 2, CAP])
                    ins = v.tensor_tensor(hot_s[:, t, :, :], slots4, rank, ALU.is_equal)
                return ins

            choose(slice(0, 2)).then_inc(s_ready, 1)
            dve.wait_ge(gat1, 1)
            v.tensor_copy(arena2[:, 512:1024], psum[:, 3, :]).then_inc(gat1_c, 1)
            with dve.Fori(0, rounds) as r:
                with dve.Fori(0, PAIRS) as p:
                    n = r * PAIRS + p
                    dve.wait_ge(up1, n + 1)
                    dve.wait_ge(s_ready, n + 1)
                    for t in range(TT):
                        gates = r_gate[:, t, bass.ds(p * 2, 2)].unsqueeze(2).to_broadcast([P, 2, CAP])
                        ins = v.tensor_tensor(hot_g[:, t, :, :], hot_s[:, t, :, :], gates, ALU.mult)
                    ins.then_inc(sg_ready, 1)
                    dve.wait_ge(sg_ready, n + 1)
                    choose(bass.ds(p * 2 + 2, 2)).then_inc(s_ready, 1)
                    dve.wait_ge(silu_e, n + 1)
                    dve.wait_ge(up3, n + 1)
                    v.tensor_tensor(act_e, silu1, psum[:, 1, :], ALU.mult).then_inc(act_ready, 1)
                    dve.wait_ge(gat1, n + 2)
                    v.tensor_copy(arena2[:, 512:1024], psum[:, 3, :]).then_inc(gat1_c, 1)
                    dve.wait_ge(y0_mm, n + 1)
                    v.tensor_copy(y_e[:, 0:512], psum[:, 0, :]).then_inc(y0_c, 1)
                dve.wait_ge(s_ready, r * PAIRS + (PAIRS + 1))
                v.tensor_scalar(r_rank, r_rank, -float(CAP), None, ALU.add).then_inc(next_round, 1)
                dve.wait_ge(next_round, r + 1)

            def split_pg(j):
                dve.wait_ge(pg_hi_ready, j + 1)
                v.tensor_tensor(pg_lo[:, j, :], pg_in(j), pg_hi[:, j, :].bitcast(F32), ALU.subtract).then_inc(pg_split, 1)

            dve.wait_ge(y0_mm, rounds * PAIRS)
            split_pg(0)
            dve.wait_ge(scattered, rounds * PAIRS + 1)
            for kt in range(KT):
                v.tensor_tensor(x[:, kt, :], x[:, kt, :], y_ps(kt), ALU.add).then_inc(x_ready, 1)
            for kt in range(KT):
                dve.wait_ge(x_ready, 41 + kt + 1)
                v.tensor_scalar(g_lo32[:, kt, :], x[:, kt, :], V("g_ple", kt), None, ALU.mult).then_inc(g_whole, 1)
            for kt in range(KT):
                dve.wait_ge(g_whole, kt + 1)
                dve.wait_ge(hi_ready, 64 + kt + 1)
                v.tensor_tensor(g_lo[:, kt, :], g_lo32[:, kt, :], h_hi[:, kt, :].bitcast(F32), ALU.subtract).then_inc(lo_ready, 1)
            for j in range(1, 4):
                split_pg(j)
            invert("gate")
            dve.wait_ge(ple_scaled, 8)

            def gated_embedding(n):
                dve.wait_ge(gate_done, 48 + n + 1)
                for kt in (2 * n, 2 * n + 1):
                    link(v.tensor_tensor(d[:, kt, :], d[:, kt, :], ple_e[:, kt, :], ALU.mult))
                    v.tensor_tensor(x[:, kt, :], x[:, kt, :], d[:, kt, :], ALU.add).then_inc(x_ready, 1)

            for n in range(4):
                dve.wait_ge(unit_done, PG + n + 1)
                v.tensor_tensor(d[:, 2 * n, :], y_ps(2 * n), rstd[:], ALU.mult)
                v.tensor_tensor(d[:, 2 * n + 1, :], y_ps(2 * n + 1), rstd[:], ALU.mult).then_inc(gate_scaled, 1)
                if n:
                    gated_embedding(n - 1)
            gated_embedding(3)
            rms("final", x, "g_final", d, out_ready)


INPUTS = ["x_t", "c_rows", "table", "vecs", "ada", "units", "lam_in", "w_forget", "forget_b", "p_t", "w_r", "w_i",
          "w_route", "b_route", "w1", "w3", "w2"]


def lay_out(i):
    f = {k: np.asarray(v) for k, v in i.items()}

    def features(m):
        return np.ascontiguousarray(m.reshape(-1, P, m.shape[1]).transpose(1, 0, 2))

    def cols(v):
        return v.reshape(-1, P).T

    def col_units(w):
        k, n = w.shape
        return w.reshape(KT, P, n // 256, 256).transpose(2, 1, 0, 3).reshape(n // 256, P, UNIT)

    def row_units(w):
        k, n = w.shape
        return w.reshape(k // 256, 2, P, n).transpose(0, 2, 1, 3).reshape(k // 256, P, UNIT)

    def pairs(w):
        k, n = w.shape
        return w.reshape(k, 2, n // 256, P).transpose(0, 2, 1, 3).reshape(k, n)

    ab, cd = f["w_in_ab"][0], f["w_in_cd"][0]
    units = []
    for layer, w in enumerate((ab, cd)):
        units += [col_units(np.concatenate([w[:, 1024:1536], w[:, 2560:3072]], axis=1)),
                  col_units(np.concatenate([w[:, 0:1024], w[:, 1536:2560]], axis=1)),
                  col_units(f["w_o"][layer]), col_units(pairs(f["w_ffn_in"][layer])), row_units(f["w_ffn_out"][layer])]
    w = f["w_in_2"][0]
    units += [col_units(np.concatenate([pairs(w[:, 0:1024]), pairs(w[:, 1024:2048])], axis=1)),
              row_units(f["w_ple_2"][0]), col_units(f["w_out_2"][0]), col_units(f["w_ple_gate_2"][0])]
    vecs = {
        "b_ada": cols(f["b_ada"]), "ln_g": cols(f["ln_g"]), "ln_b": cols(f["ln_b"]), "subln_g": cols(f["diff_subln_g"]),
        "conv_w": f["conv_dw_w_2"][0].reshape(CONV_W, CT, P).transpose(2, 1, 0).reshape(P, -1),
        "conv_b": cols(f["conv_dw_b_2"]), "conv_ln_g": cols(f["conv_ln_g_2"]), "conv_ln_b": cols(f["conv_ln_b_2"]),
        "lru_w": f["lru_conv_w_2"][0].reshape(LRU_W, CT, P).transpose(2, 1, 0).reshape(P, -1),
        "lru_b": cols(f["lru_conv_b_2"]), "b_r": cols(f["lru_b_r_2"]), "b_i": cols(f["lru_b_i_2"]),
        "lam": cols(f["lru_lambda_2"]), "g_mix": cols(f["g_mix_2"]), "g_ffn": cols(f["g_ffn_2"]),
        "g_ple": cols(f["g_ple_2"]), "g_ple_proj": cols(f["g_ple_proj_2"]), "g_final": cols(f["g_final_2"]),
    }
    ada = f["w_ada"].reshape(DEPTH, D, 24, 2, P).transpose(0, 2, 4, 3, 1).reshape(ADA_PIECES, P, UNIT)
    up = lambda w: w[0].reshape(PAIRS, 2, KT, P, FE).transpose(0, 1, 3, 2, 4).reshape(PAIRS, 2, P, 4096)
    blocks = lambda w: w[0].reshape(CT, 2, 64, 64).transpose(1, 2, 0, 3).reshape(P, CT, 64)
    laid = {
        "x_t": features(f["x"][0].T), "c_rows": np.broadcast_to(f["c"], (P, D)),
        "table": np.concatenate([f["rel_bias"][:, 0:8], f["rel_bias"][:, 4:12]], axis=1),
        "vecs": np.concatenate([vecs[n] for n, _ in VECS], axis=1), "ada": ada, "units": np.concatenate(units),
        "lam_in": np.broadcast_to(f["diff_lambda"][0].reshape(1, 256), (P, 256)),
        "w_forget": cd[:, 3072:3080].reshape(KT, P, 8).transpose(1, 0, 2), "forget_b": f["forget_b"].T,
        "p_t": features(f["p_2"][0, 0].T), "w_r": blocks(f["lru_w_r_2"]), "w_i": blocks(f["lru_w_i_2"]),
        "w_route": np.concatenate([f["w_group_2"][0], f["w_expert_2"][0]], axis=1).reshape(KT, P, 36).transpose(1, 0, 2),
        "b_route": np.broadcast_to(np.concatenate([f["b_group_2"][0], f["b_expert_2"][0]])[None], (P, 36)),
        "w1": up(f["w1_2"]), "w3": up(f["w3_2"]),
        "w2": f["w2_2"][0].reshape(PAIRS, 2, 4, P, D).transpose(0, 1, 3, 2, 4).reshape(PAIRS, 2, P, 4096),
    }
    laid.update(shape_constants())
    return {k: np.ascontiguousarray(v) for k, v in laid.items()}


def kernel(**inputs):
    import concourse.bacc as bacc
    from concourse.bass_utils import run_bass_kernel_spmd

    arrays = lay_out(inputs)
    nc = bacc.Bacc("TRN2", target_bir_lowering=False, num_devices=1)
    a = {n: nc.dram_tensor(f"in_{n}", v.shape, mybir.dt.from_np(v.dtype), kind="ExternalInput").ap() for n, v in arrays.items()}
    out = nc.dram_tensor("out", (P, KT, T), F32, kind="ExternalOutput").ap()
    build(nc, a, out)
    r = run_bass_kernel_spmd(nc, [{f"in_{n}": v for n, v in arrays.items()}], core_ids=[0])
    return np.ascontiguousarray(r.results[0]["out"].transpose(2, 1, 0).reshape(1, T, D))
```
